# Optimizing a Trainium2 kernel written in Bass

```python
import math
import jax, jax.numpy as jnp
from jax import lax
import numpy as np

D_MODEL = 1024
BATCH = 1
SEQ = 512
DEPTH = 2

HEAD_DIM = 64
NSA_Q_HEADS = 6
NSA_KV_HEADS = 2
NSA_HPG = NSA_Q_HEADS // NSA_KV_HEADS
NSA_WIDTH = NSA_Q_HEADS * HEAD_DIM
N_BRANCH = 3
NSA_KV_COLS = N_BRANCH * 2 * NSA_KV_HEADS * HEAD_DIM
CMP_BLOCK = 32
CMP_STRIDE = 16
CMP_HIDDEN = 64
SEL_BLOCK = 64
SEL_TOP_N = 16
WINDOW = 512
FORCE_SCORE = 1.0e4
GLA_HEADS = 6
GLA_DK = 32
GLA_DV = 64
GLA_WIDTH = GLA_HEADS * GLA_DV
GLA_GATE_RANK = 16
GLA_GATE_NORM = 16.0
GLA_CHUNK = 64
POOL_WINDOWS = (2, 4, 8, 16)
POOL_GROUPS = 4
POOL_GROUP = 64
POOL_WIDTH = POOL_GROUPS * POOL_GROUP
MIX_WIDTH = NSA_WIDTH + GLA_WIDTH + POOL_WIDTH
SPLIT_SIZES = (NSA_WIDTH, NSA_KV_COLS, NSA_Q_HEADS * N_BRANCH,
               GLA_HEADS * GLA_DK, GLA_HEADS * GLA_DK, GLA_WIDTH, GLA_GATE_RANK, GLA_WIDTH,
               POOL_WIDTH)
P_IN = sum(SPLIT_SIZES)
D_FF = 4 * D_MODEL
ROPE_THETA = 500000.0
ROPE_DIM = HEAD_DIM // 4
Q_BLOCK = 128
SEL_Q_BLOCK = 32
LN_EPS = 1e-5
RMS_EPS = 1e-6
DEEPNORM_ALPHA = (2 * DEPTH) ** 0.25
DEEPNORM_BETA = (8 * DEPTH) ** -0.25


def partial_rope(x, pos):
    half = ROPE_DIM // 2
    inv = ROPE_THETA ** (-jnp.arange(half, dtype=jnp.float32) * 2.0 / ROPE_DIM)
    ang = pos.astype(jnp.float32)[:, None] * inv[None, :]
    cos = jnp.cos(ang).astype(x.dtype)
    sin = jnp.sin(ang).astype(x.dtype)
    x1, x2, xp = x[..., :half], x[..., half:ROPE_DIM], x[..., ROPE_DIM:]
    return jnp.concatenate([x1 * cos - x2 * sin, x1 * sin + x2 * cos, xp], axis=-1)

def layer_norm(x, g, b):
    xf = x.astype(jnp.float32)
    mu = jnp.mean(xf, -1, keepdims=True)
    var = jnp.mean(jnp.square(xf - mu), -1, keepdims=True)
    return ((xf - mu) * lax.rsqrt(var + LN_EPS)).astype(x.dtype) * g + b

def masked_softmax(s, mask):
    s = jnp.where(mask, s.astype(jnp.float32), -jnp.inf)
    m = jnp.max(s, -1, keepdims=True)
    m = jnp.where(jnp.isfinite(m), m, 0.0)
    e = jnp.exp(s - m)
    return e / jnp.maximum(jnp.sum(e, -1, keepdims=True), 1e-30)

def nsa_mixer(q, kv, gates, cmp_pos, cmp_w1, cmp_w2):
    B, S, _ = q.shape
    G, H, Dh = NSA_KV_HEADS, NSA_HPG, HEAD_DIM
    pos = jnp.arange(S)
    q = q.reshape(B, S, G, H, Dh).transpose(0, 2, 3, 1, 4)
    q = partial_rope(q, pos) * (Dh ** -0.5)
    kv = kv.reshape(B, S, N_BRANCH, 2, G, Dh).transpose(2, 3, 0, 4, 1, 5)

    n_cmp = (S - CMP_BLOCK) // CMP_STRIDE + 1
    blk_idx = CMP_STRIDE * jnp.arange(n_cmp)[:, None] + jnp.arange(CMP_BLOCK)[None, :]

    def compress(t, p, w1, w2):
        tb = t[:, :, blk_idx] + p
        hid = jax.nn.gelu(tb.reshape(B, G, n_cmp, CMP_BLOCK * Dh) @ w1)
        return hid @ w2

    kc = compress(partial_rope(kv[0, 0], pos), cmp_pos[0], cmp_w1[0], cmp_w2[0])
    vc = compress(kv[0, 1], cmp_pos[1], cmp_w1[1], cmp_w2[1])
    s_cmp = jnp.einsum('bghsd,bgnd->bghsn', q, kc)
    cmp_mask = blk_idx[:, -1][None, :] <= pos[:, None]
    p_cmp = masked_softmax(s_cmp, cmp_mask)
    o_cmp = jnp.einsum('bghsn,bgnd->bghsd', p_cmp.astype(vc.dtype), vc)

    n_sel = S // SEL_BLOCK
    n_top = min(SEL_TOP_N, n_sel)
    c_lo = blk_idx[:, 0:1]
    s_lo = (SEL_BLOCK * jnp.arange(n_sel))[None, :]
    overlap = jnp.clip(jnp.minimum(c_lo + CMP_BLOCK, s_lo + SEL_BLOCK) - jnp.maximum(c_lo, s_lo), 0, None)
    cmp_to_sel = overlap.astype(jnp.float32) / CMP_BLOCK
    imp = jnp.einsum('bghsn,nj->bgsj', p_cmp, cmp_to_sel)
    cur = (pos // SEL_BLOCK)[:, None]
    jb = jnp.arange(n_sel)[None, :]
    imp = jnp.where((jb == 0) | (jb == cur) | (jb == cur - 1), FORCE_SCORE, imp)
    imp = jnp.where(jb > cur, -FORCE_SCORE, imp)
    _, sel_idx = lax.top_k(imp, n_top)

    k_slc = partial_rope(kv[1, 0], pos).reshape(B, G, n_sel, SEL_BLOCK, Dh)
    v_slc = kv[1, 1].reshape(B, G, n_sel, SEL_BLOCK, Dh)
    nqb = S // SEL_Q_BLOCK
    q_blk = q.reshape(B, G, H, nqb, SEL_Q_BLOCK, Dh).transpose(3, 0, 1, 2, 4, 5)
    idx_blk = sel_idx.reshape(B, G, nqb, SEL_Q_BLOCK, n_top).transpose(2, 0, 1, 3, 4)
    t_blk = pos.reshape(nqb, SEL_Q_BLOCK)
    bi = jnp.arange(B)[:, None, None, None]
    gi = jnp.arange(G)[None, :, None, None]

    def sel_block(args):
        qb, ib, tb = args
        kb = k_slc[bi, gi, ib]
        vb = v_slc[bi, gi, ib]
        s = jnp.einsum('bghqd,bgqnkd->bghqnk', qb, kb)
        kpos = ib[..., None] * SEL_BLOCK + jnp.arange(SEL_BLOCK)
        m = (kpos <= tb[None, None, :, None, None])[:, :, None]
        s = s.reshape(B, G, H, SEL_Q_BLOCK, n_top * SEL_BLOCK)
        m = m.reshape(B, G, 1, SEL_Q_BLOCK, n_top * SEL_BLOCK)
        p = masked_softmax(s, m).reshape(B, G, H, SEL_Q_BLOCK, n_top, SEL_BLOCK)
        return jnp.einsum('bghqnk,bgqnkd->bghqd', p.astype(vb.dtype), vb)

    o_slc = lax.map(sel_block, (q_blk, idx_blk, t_blk))
    o_slc = o_slc.transpose(1, 2, 3, 0, 4, 5).reshape(B, G, H, S, Dh)

    pad = ((0, 0), (0, 0), (WINDOW, 0), (0, 0))
    k_win = jnp.pad(partial_rope(kv[2, 0], pos), pad)
    v_win = jnp.pad(kv[2, 1], pad)
    nwb = S // Q_BLOCK
    span = WINDOW + Q_BLOCK
    q_wb = q.reshape(B, G, H, nwb, Q_BLOCK, Dh).transpose(3, 0, 1, 2, 4, 5)
    starts = jnp.arange(nwb) * Q_BLOCK

    def win_block(args):
        qb, s0 = args
        kb = lax.dynamic_slice_in_dim(k_win, s0, span, axis=2)
        vb = lax.dynamic_slice_in_dim(v_win, s0, span, axis=2)
        s = jnp.einsum('bghqd,bgkd->bghqk', qb, kb)
        tq = s0 + jnp.arange(Q_BLOCK)
        tk = s0 - WINDOW + jnp.arange(span)
        diff = tq[:, None] - tk[None, :]
        m = (diff >= 0) & (diff < WINDOW) & (tk[None, :] >= 0)
        p = masked_softmax(s, m)
        return jnp.einsum('bghqk,bgkd->bghqd', p.astype(vb.dtype), vb)

    o_win = lax.map(win_block, (q_wb, starts))
    o_win = o_win.transpose(1, 2, 3, 0, 4, 5).reshape(B, G, H, S, Dh)

    gt = jax.nn.sigmoid(gates.reshape(B, S, G, H, N_BRANCH).transpose(0, 2, 3, 1, 4))
    o = gt[..., 0:1] * o_cmp + gt[..., 1:2] * o_slc + gt[..., 2:3] * o_win
    return o.transpose(0, 3, 1, 2, 4).reshape(B, S, NSA_WIDTH)

def gla_mixer(q, k, v, g_lr, og, w_gate2, b_gate, norm_g):
    B, S, _ = q.shape
    Hh, dk, dv, C = GLA_HEADS, GLA_DK, GLA_DV, GLA_CHUNK
    N = S // C
    f32 = jnp.float32
    gk = jax.nn.log_sigmoid((g_lr @ w_gate2 + b_gate).astype(f32)) / GLA_GATE_NORM

    def chunks(t, d):
        return t.astype(f32).reshape(B, N, C, Hh, d).transpose(0, 3, 1, 2, 4)

    qc = chunks(q, dk) * (dk ** -0.5)
    kc = chunks(k, dk)
    vc = chunks(v, dv)
    bcum = jnp.cumsum(chunks(gk, dk), axis=3)
    blast = bcum[:, :, :, -1:]
    q_dec = qc * jnp.exp(bcum)
    k_inv = kc * jnp.exp(-bcum)
    k_end = kc * jnp.exp(blast - bcum)
    causal = jnp.tril(jnp.ones((C, C), bool))
    a = jnp.where(causal, jnp.einsum('bhnid,bhnjd->bhnij', q_dec, k_inv), 0.0)
    o_intra = jnp.einsum('bhnij,bhnjv->bhniv', a, vc)
    d_state = jnp.einsum('bhncd,bhncv->bhndv', k_end, vc)
    decay = jnp.exp(blast[:, :, :, 0])

    def step(s_prev, inp):
        dcy, ds = inp
        return s_prev * dcy[..., None] + ds, s_prev

    _, s_in = lax.scan(step, jnp.zeros((B, Hh, dk, dv), f32),
                       (decay.transpose(2, 0, 1, 3), d_state.transpose(2, 0, 1, 3, 4)))
    s_in = s_in.transpose(1, 2, 0, 3, 4)
    o = o_intra + jnp.einsum('bhncd,bhndv->bhncv', q_dec, s_in)
    o = o * lax.rsqrt(jnp.mean(o * o, -1, keepdims=True) + RMS_EPS)
    o = o.transpose(0, 2, 3, 1, 4).reshape(B, S, GLA_WIDTH).astype(og.dtype)
    return o * norm_g * jax.nn.silu(og)

def pool_mixer(u, w_pool, scale):
    B, S, Cw = u.shape
    uf = u.astype(jnp.float32)
    cs = jnp.pad(jnp.cumsum(uf, axis=1), ((0, 0), (1, 0), (0, 0)))
    win = jnp.repeat(jnp.array(POOL_WINDOWS, jnp.int32), POOL_GROUP)
    t = jnp.arange(S)[:, None]
    lo = jnp.maximum(t + 1 - win[None, :], 0)
    cnt = jnp.minimum(t + 1, win[None, :]).astype(jnp.float32)
    lo_sum = jnp.take_along_axis(cs, jnp.broadcast_to(lo[None], (B, S, Cw)), axis=1)
    pooled = (cs[:, 1:] - lo_sum) / cnt - uf
    y = jnp.einsum('bsgc,gcd->bsgd', pooled.reshape(B, S, POOL_GROUPS, POOL_GROUP).astype(u.dtype), w_pool)
    return y.reshape(B, S, POOL_WIDTH) * scale

def first_inputs(seed: int = 0) -> dict:
    key = jax.random.key(seed)
    ks = jax.random.split(key, 20)
    L, D = DEPTH, D_MODEL
    nrm = lambda k, shape, s: jax.random.normal(k, shape, jnp.float32) * s
    return {
        "x": nrm(ks[0], (BATCH, SEQ, D), 1.0),
        "w_in": nrm(ks[1], (L, D, P_IN), D ** -0.5),
        "cmp_pos": nrm(ks[2], (L, 2, CMP_BLOCK, HEAD_DIM), 0.1),
        "cmp_w1": nrm(ks[3], (L, 2, CMP_BLOCK * HEAD_DIM, CMP_HIDDEN), (CMP_BLOCK * HEAD_DIM) ** -0.5),
        "cmp_w2": nrm(ks[4], (L, 2, CMP_HIDDEN, HEAD_DIM), CMP_HIDDEN ** -0.5),
        "gla_w_gate2": nrm(ks[5], (L, GLA_GATE_RANK, GLA_HEADS * GLA_DK), GLA_GATE_RANK ** -0.5),
        "gla_b_gate": nrm(ks[6], (L, GLA_HEADS * GLA_DK), 0.01),
        "gla_norm_g": 1.0 + nrm(ks[7], (L, GLA_WIDTH), 0.02),
        "pool_w": nrm(ks[8], (L, POOL_GROUPS, POOL_GROUP, POOL_GROUP), POOL_GROUP ** -0.5),
        "pool_scale": 1.0 + nrm(ks[9], (L, POOL_WIDTH), 0.02),
        "w_out": nrm(ks[10], (L, MIX_WIDTH, D), MIX_WIDTH ** -0.5 * DEEPNORM_BETA),
        "ln1_g": 1.0 + nrm(ks[11], (L, D), 0.02),
        "ln1_b": nrm(ks[12], (L, D), 0.02),
        "w_up": nrm(ks[13], (L, D, D_FF), D ** -0.5),
        "w_down": nrm(ks[14], (L, D_FF, D), D_FF ** -0.5 * DEEPNORM_BETA),
        "ln2_g": 1.0 + nrm(ks[15], (L, D), 0.02),
        "ln2_b": nrm(ks[16], (L, D), 0.02),
    }

def first_block(x, w_in, cmp_pos, cmp_w1, cmp_w2, gla_w_gate2, gla_b_gate, gla_norm_g, pool_w, pool_scale,
              w_out, ln1_g, ln1_b, w_up, w_down, ln2_g, ln2_b):
    split_points = []
    acc = 0
    for sz in SPLIT_SIZES[:-1]:
        acc += sz
        split_points.append(acc)
    h = x
    for l in range(DEPTH):
        proj = h @ w_in[l]
        nq, nkv, ngate, gq, gk, gv, glr, gog, pu = jnp.split(proj, split_points, axis=-1)
        mixed = jnp.concatenate([
            nsa_mixer(nq, nkv, ngate, cmp_pos[l], cmp_w1[l], cmp_w2[l]),
            gla_mixer(gq, gk, gv, glr, gog, gla_w_gate2[l], gla_b_gate[l], gla_norm_g[l]),
            pool_mixer(pu, pool_w[l], pool_scale[l]),
        ], axis=-1)
        h = layer_norm(DEEPNORM_ALPHA * h + mixed @ w_out[l], ln1_g[l], ln1_b[l])
        ff = jnp.square(jax.nn.relu(h @ w_up[l])) @ w_down[l]
        h = layer_norm(DEEPNORM_ALPHA * h + ff, ln2_g[l], ln2_b[l])
    return h


N_MIXERS = 3
D_HEAD = 64
ROT_DIM = D_HEAD // 4
D_FF_2 = 2816
PLE_DIM = 256
NEG_INF = -1e30
N_NORMS = 8
A_PAIRS = ((128, 1), (512, 4), (2048, 16))
A_HEADS = 8
A_BLOCK = 64
B_HEADS = 16
B_KV_HEADS = 4
B_RADIUS = 128
B_BLOCK = 128
C_HEADS = 16
GRID_W = 64
NA_ROWS = 8
NA_COLS = 16
NA_QC = 16
NA_KC = 2 * NA_QC


def rms_norm(x, g):
    x32 = x.astype(jnp.float32)
    y = x32 * lax.rsqrt(jnp.mean(x32 * x32, axis=-1, keepdims=True) + RMS_EPS)
    return (y * g.astype(jnp.float32)).astype(x.dtype)

def swiglu(x, wi, wo):
    gate, up = jnp.split(x @ wi, 2, axis=-1)
    return (jax.nn.silu(gate) * up) @ wo

def rope_tables(seq):
    pos = jnp.arange(seq, dtype=jnp.float32)
    inv = ROPE_THETA ** (-jnp.arange(0, ROT_DIM, 2, dtype=jnp.float32) / ROT_DIM)
    ang = pos[:, None] * inv[None, :]
    return jnp.cos(ang), jnp.sin(ang)

def apply_rope(x, cos, sin):
    shape = (cos.shape[0],) + (1,) * (x.ndim - 3) + (cos.shape[1],)
    c = cos.reshape(shape).astype(x.dtype)
    s = sin.reshape(shape).astype(x.dtype)
    half = ROT_DIM // 2
    x1, x2, rest = x[..., :half], x[..., half:ROT_DIM], x[..., ROT_DIM:]
    return jnp.concatenate([x1 * c - x2 * s, x2 * c + x1 * s, rest], axis=-1)

def band_attention(q, k, v, radius, block, sink=None):
    n, length, hk, grp, dh = q.shape
    nb = -(-length // block)
    pad = nb * block - length
    qb = jnp.pad(q, ((0, 0), (0, pad), (0, 0), (0, 0), (0, 0))).reshape(n, nb, block, hk, grp, dh)

    def three_blocks(a):
        a = jnp.pad(a, ((0, 0), (block, pad + block), (0, 0), (0, 0))).reshape(n, nb + 2, block, hk, dh)
        return jnp.concatenate([a[:, :-2], a[:, 1:-1], a[:, 2:]], axis=2)

    kb, vb = three_blocks(k), three_blocks(v)
    qpos = jnp.arange(nb * block).reshape(nb, block)
    kpos = jnp.arange(nb)[:, None] * block - block + jnp.arange(3 * block)[None, :]
    rel = kpos[:, None, :] - qpos[:, :, None]
    valid = (jnp.abs(rel) <= radius) & (kpos[:, None, :] >= 0) & (kpos[:, None, :] < length)
    s = jnp.einsum('nbqhgd,nbkhd->nbhgqk', qb, kb).astype(jnp.float32) * (dh ** -0.5)
    s = jnp.where(valid[None, :, None, None], s, NEG_INF)
    m = jnp.max(s, axis=-1)
    if sink is not None:
        sk = sink.astype(jnp.float32)[None, None, :, :, None]
        m = jnp.maximum(m, sk)
    pr = jnp.exp(s - m[..., None])
    den = jnp.sum(pr, axis=-1)
    if sink is not None:
        den = den + jnp.exp(sk - m)
    o = jnp.einsum('nbhgqk,nbkhd->nbqhgd', pr.astype(v.dtype), vb)
    o = o / jnp.transpose(den, (0, 1, 4, 2, 3))[..., None]
    lse = jnp.transpose(m + jnp.log(den), (0, 1, 4, 2, 3))
    o = o.reshape(n, nb * block, hk, grp, dh)[:, :length].astype(q.dtype)
    lse = lse.reshape(n, nb * block, hk, grp)[:, :length]
    return o, lse

def dilated_mixer(h, wqkv, wo, cos, sin):
    b, s, _ = h.shape
    ng = len(A_PAIRS)
    qkv = (h @ wqkv).reshape(b, s, 3, ng, A_HEADS, D_HEAD)
    q = apply_rope(qkv[:, :, 0], cos, sin)
    k = apply_rope(qkv[:, :, 1], cos, sin)
    v = qkv[:, :, 2]
    outs, lses = [], []
    for g, (window, dil) in enumerate(A_PAIRS):
        sub = s // dil

        def to_sub(a):
            return a.reshape(b, sub, dil, A_HEADS, D_HEAD).transpose(0, 2, 1, 3, 4).reshape(b * dil, sub, A_HEADS, D_HEAD)

        o, lse = band_attention(to_sub(q[:, :, g])[:, :, :, None], to_sub(k[:, :, g]), to_sub(v[:, :, g]),
                                window // (2 * dil), A_BLOCK)
        o = o[:, :, :, 0].reshape(b, dil, sub, A_HEADS, D_HEAD).transpose(0, 2, 1, 3, 4).reshape(b, s, A_HEADS, D_HEAD)
        lse = lse[..., 0].reshape(b, dil, sub, A_HEADS).transpose(0, 2, 1, 3).reshape(b, s, A_HEADS)
        outs.append(o)
        lses.append(lse)
    wts = jax.nn.softmax(jnp.stack(lses, axis=0), axis=0)
    o = jnp.sum(wts[..., None] * jnp.stack(outs, axis=0).astype(jnp.float32), axis=0).astype(h.dtype)
    return o.reshape(b, s, A_HEADS * D_HEAD) @ wo

def window_gqa_mixer(h, wqkv, wo, sink, cos, sin):
    b, s, _ = h.shape
    grp = B_HEADS // B_KV_HEADS
    qkv = h @ wqkv
    q = qkv[..., :B_HEADS * D_HEAD].reshape(b, s, B_HEADS, D_HEAD)
    k = qkv[..., B_HEADS * D_HEAD:(B_HEADS + B_KV_HEADS) * D_HEAD].reshape(b, s, B_KV_HEADS, D_HEAD)
    v = qkv[..., (B_HEADS + B_KV_HEADS) * D_HEAD:].reshape(b, s, B_KV_HEADS, D_HEAD)
    q = apply_rope(q, cos, sin).reshape(b, s, B_KV_HEADS, grp, D_HEAD)
    k = apply_rope(k, cos, sin)
    o, _ = band_attention(q, k, v, B_RADIUS, B_BLOCK, sink.reshape(B_KV_HEADS, grp))
    return o.reshape(b, s, B_HEADS * D_HEAD) @ wo

def neighbourhood_mixer(h, wqkv, wo, rpb):
    b, s, _ = h.shape
    rows = s // GRID_W
    kh = min(NA_ROWS, rows)
    ncb = GRID_W // NA_QC
    qkv = (h @ wqkv).reshape(b, rows, GRID_W, 3, C_HEADS, D_HEAD)
    q = qkv[:, :, :, 0] * (D_HEAD ** -0.5)
    k, v = qkv[:, :, :, 1], qkv[:, :, :, 2]
    qcol = np.arange(GRID_W).reshape(ncb, NA_QC)
    kstart = np.clip(np.arange(ncb) * NA_QC - NA_COLS // 2, 0, GRID_W - NA_KC)
    kcol = kstart[:, None] + np.arange(NA_KC)[None, :]
    cstart = np.clip(qcol - NA_COLS // 2, 0, GRID_W - NA_COLS)
    col_valid = (kcol[:, None, :] >= cstart[..., None]) & (kcol[:, None, :] < cstart[..., None] + NA_COLS)
    dc_idx = np.clip(kcol[:, None, :] - qcol[:, :, None] + NA_COLS - 1, 0, 2 * NA_COLS - 2)
    kc = k[:, :, kcol]
    vc = v[:, :, kcol]

    def row_fn(r):
        rs = jnp.clip(r - kh // 2, 0, rows - kh)
        kw = lax.dynamic_slice_in_dim(kc, rs, kh, axis=1)
        vw = lax.dynamic_slice_in_dim(vc, rs, kh, axis=1)
        qr = lax.dynamic_index_in_dim(q, r, axis=1, keepdims=False).reshape(b, ncb, NA_QC, C_HEADS, D_HEAD)
        sc = jnp.einsum('bnqhd,bjnchd->bhnqjc', qr, kw).astype(jnp.float32)
        dr_idx = rs + jnp.arange(kh) - r + NA_ROWS - 1
        bias = rpb[:, dr_idx][:, :, dc_idx].transpose(0, 2, 3, 1, 4)
        sc = sc + bias.astype(jnp.float32)[None]
        sc = jnp.where(col_valid[None, None, :, :, None, :], sc, NEG_INF)
        pr = jax.nn.softmax(sc.reshape(b, C_HEADS, ncb, NA_QC, kh * NA_KC), axis=-1)
        pr = pr.reshape(b, C_HEADS, ncb, NA_QC, kh, NA_KC).astype(vw.dtype)
        o = jnp.einsum('bhnqjc,bjnchd->bnqhd', pr, vw)
        return o.reshape(b, GRID_W, C_HEADS * D_HEAD)

    out = lax.map(row_fn, jnp.arange(rows))
    return out.transpose(1, 0, 2, 3).reshape(b, s, C_HEADS * D_HEAD) @ wo

def second_inputs(seed: int = 0) -> dict:
    key = jax.random.key(seed)
    ks = jax.random.split(key, 16)
    f32 = jnp.float32

    def dense(k, shape, fan_in):
        return jax.random.normal(k, shape, f32) * (fan_in ** -0.5)

    n_a = len(range(0, DEPTH, N_MIXERS))
    n_b = len(range(1, DEPTH, N_MIXERS))
    n_c = len(range(2, DEPTH, N_MIXERS))
    ng = len(A_PAIRS)
    return {
        "x": jax.random.normal(ks[0], (BATCH, SEQ, D_MODEL), f32),
        "p": jax.random.normal(ks[1], (DEPTH, BATCH, SEQ, PLE_DIM), f32),
        "norm_g": 1.0 + 0.02 * jax.random.normal(ks[2], (DEPTH, N_NORMS, D_MODEL), f32),
        "ffn_wi": dense(ks[3], (DEPTH, 2, D_MODEL, 2 * D_FF_2), D_MODEL),
        "ffn_wo": dense(ks[4], (DEPTH, 2, D_FF_2, D_MODEL), D_FF_2),
        "ple_proj": dense(ks[5], (DEPTH, PLE_DIM, D_MODEL), PLE_DIM),
        "ple_gate": dense(ks[6], (DEPTH, D_MODEL, D_MODEL), D_MODEL),
        "a_wqkv": dense(ks[7], (n_a, D_MODEL, 3 * ng * A_HEADS * D_HEAD), D_MODEL),
        "a_wo": dense(ks[8], (n_a, A_HEADS * D_HEAD, D_MODEL), A_HEADS * D_HEAD),
        "b_wqkv": dense(ks[9], (n_b, D_MODEL, (B_HEADS + 2 * B_KV_HEADS) * D_HEAD), D_MODEL),
        "b_wo": dense(ks[10], (n_b, B_HEADS * D_HEAD, D_MODEL), B_HEADS * D_HEAD),
        "b_sink": 0.5 * jax.random.normal(ks[11], (n_b, B_HEADS), f32),
        "c_wqkv": dense(ks[12], (n_c, D_MODEL, 3 * C_HEADS * D_HEAD), D_MODEL),
        "c_wo": dense(ks[13], (n_c, C_HEADS * D_HEAD, D_MODEL), C_HEADS * D_HEAD),
        "c_rpb": 0.1 * jax.random.normal(ks[14], (n_c, C_HEADS, 2 * NA_ROWS - 1, 2 * NA_COLS - 1), f32),
    }

def second_block(x, p, norm_g, ffn_wi, ffn_wo, ple_proj, ple_gate, a_wqkv, a_wo,
              b_wqkv, b_wo, b_sink, c_wqkv, c_wo, c_rpb):
    cos, sin = rope_tables(x.shape[1])
    h = x
    for i in range(DEPTH):
        g = norm_g[i]
        h = h + 0.5 * rms_norm(swiglu(rms_norm(h, g[0]), ffn_wi[i, 0], ffn_wo[i, 0]), g[1])
        hn = rms_norm(h, g[2])
        mixer, j = i % N_MIXERS, i // N_MIXERS
        if mixer == 0:
            y = dilated_mixer(hn, a_wqkv[j], a_wo[j], cos, sin)
        elif mixer == 1:
            y = window_gqa_mixer(hn, b_wqkv[j], b_wo[j], b_sink[j], cos, sin)
        else:
            y = neighbourhood_mixer(hn, c_wqkv[j], c_wo[j], c_rpb[j])
        h = h + rms_norm(y, g[3])
        h = h + 0.5 * rms_norm(swiglu(rms_norm(h, g[4]), ffn_wi[i, 1], ffn_wo[i, 1]), g[5])
        e = p[i].astype(h.dtype) @ ple_proj[i]
        gate = jax.nn.sigmoid(rms_norm(h, g[6]) @ ple_gate[i])
        h = h + rms_norm(e * gate, g[7])
    return h


def setup_inputs(seed=0):
    out = dict(first_inputs(seed))
    for name, value in second_inputs(seed + 1).items():
        if name != "x":
            out[name + "_2"] = value
    return out


def reference(
    x, w_in, cmp_pos, cmp_w1, cmp_w2, gla_w_gate2, gla_b_gate, gla_norm_g, pool_w, pool_scale,
    w_out, ln1_g, ln1_b, w_up, w_down, ln2_g, ln2_b, p_2, norm_g_2, ffn_wi_2, ffn_wo_2,
    ple_proj_2, ple_gate_2, a_wqkv_2, a_wo_2, b_wqkv_2, b_wo_2, b_sink_2, c_wqkv_2, c_wo_2,
    c_rpb_2,
):
    x = first_block(
        x, w_in, cmp_pos, cmp_w1, cmp_w2, gla_w_gate2, gla_b_gate, gla_norm_g, pool_w,
        pool_scale, w_out, ln1_g, ln1_b, w_up, w_down, ln2_g, ln2_b,
    )
    return second_block(
        x, p_2, norm_g_2, ffn_wi_2, ffn_wo_2, ple_proj_2, ple_gate_2, a_wqkv_2, a_wo_2,
        b_wqkv_2, b_wo_2, b_sink_2, c_wqkv_2, c_wo_2, c_rpb_2,
    )


_drawn_inputs = setup_inputs


def setup_inputs(seed=0):
    import zlib

    import numpy as np

    out = dict(_drawn_inputs(seed))
    spreads = {}
    factors = {'cmp_pos': 8.815,
     'gla_w_gate2': 2.931,
     'gla_b_gate': 8.0,
     'gla_norm_g': 22.282,
     'pool_scale': 25.904,
     'b_sink_2': 8.0}
    for name, (base, spread) in spreads.items():
        noise = np.random.default_rng([zlib.crc32(name.encode()), seed]).standard_normal(out[name].shape)
        drawn = base * np.exp(spread * noise) if base else spread * noise
        out[name] = __import__('jax').numpy.asarray(drawn.astype(out[name].dtype))
    for name, factor in factors.items():
        out[name] = (out[name] * factor).astype(out[name].dtype)
    return out
```

```python
from contextlib import ExitStack, contextmanager

import numpy as np
import concourse.bass as bass
from concourse import mybir

F32 = mybir.dt.float32
F32R = mybir.dt.float32r
ALU = mybir.AluOpType
ACT = mybir.ActivationFunctionType
AX = mybir.AxisListType

P = 128
S = 512
D = 1024
DC = D // P
QT = S // P
UNIT = 1024
DEPTH = 2
ALPHA = (2 * DEPTH) ** 0.25
LN_EPS, RMS_EPS = 1e-5, 1e-6
FF2C = 2816 // P
HD = 64
N_CMP = 31
BIG_NEG = -1.0e30
FLOOR = -1.0e20

Q0, KC, VC, KS, KW, VS, VW, GV, GQ, GQX, GK, GKX, GO, PU = 0, 3, 4, 5, 6, 7, 8, 9, 12, 13, 14, 15, 16, 19
N_PROJ = 21
GLR_ROW, GATE_ROW = 64, 96

SM_W1, SM_POS, SM_W2, SM_G2, SM_PW = 0, 4096, 4160, 4288, 4480
SM_W = 4608
V_LN = 0
V_RMS = 64
V_BG, V_NG, V_PS, V_SINK = 192, 196, 202, 206
V_N = 222
T_COS, T_SIN, T_ICNT, T_RESET, T_CAUS, T_CMP, T_GLA, T_B64, T_ROT = (
    0, 512, 1024, 2048, 2560, 3072, 3200, 3328, 3456)
T_N = 3584
A_COS, A_SIN, A_ROT, A_M0, A_M1, A_M2 = 0, 512, 1024, 1152, 1536, 2432
A_N = 2944
B_COS, B_SIN, B_ROT, B_M = 0, 512, 1024, 1152
B_N = 1536


TILES4 = dict(tile=4, used0=2, used1=2)
TILES2 = dict(tile=2, used0=1, used1=1)


class Count:

    def __init__(self, eng):
        self.eng, self.n, self.loops = eng, {}, []

    def at(self, name, back=0, div=1, mult=1):
        v = (self.n.get(name, 0) // div - back) * mult
        for i, per in self.loops:
            k = per.get(name, 0) // div * mult
            if k:
                v = i * k + v
        return v

    def tick(self, name, k=1):
        self.n[name] = self.n.get(name, 0) + k

    def next_tile(self):
        b = self.n.get("tile", 0) % 2
        self.tick("tile")
        self.tick(f"used{b}")
        return b

    def skip_tiles(self, n):
        for _ in range(n):
            self.next_tile()

    def wait(self, sem, k=1):
        self.tick(sem.name, k)
        self.eng.wait_ge(sem, self.at(sem.name))

    @contextmanager
    def loop(self, rounds, **per):
        start = dict(self.n)
        with self.eng.Fori(0, rounds) as i:
            self.loops.append((i, per))
            yield i
            self.loops.pop()
        did = {k: v - start.get(k, 0) for k, v in self.n.items() if v != start.get(k, 0)}
        assert did == per, f"one round adds {did}"
        for k, v in per.items():
            self.n[k] += v * (rounds - 1)


def build(nc, stream, x_t, p_t, small, vecs, tab1, tab_a, tab_b, consts, out):
    n_units = stream.shape[0]
    with ExitStack() as ctx:
        place = [16512]

        def at(name, shape, dt=F32, offset=None):
            size = int(np.prod(shape[1:])) * 4
            if offset is None:
                offset = place[0]
                place[0] += (size + 31) // 32 * 32
            return nc.alloc_sbuf_tensor_at(name, shape, dt, offset=offset)

        def sem(name):
            s = ctx.enter_context(nc.semaphore(name))
            return s

        h = at("h", [P, DC, S])
        x_at = place[0]
        x = at("x", [P, DC, 2, S], F32R)
        y_at = place[0]
        y = at("y", [P, DC, S])
        raw = [at(f"raw{i}", [P, UNIT]) for i in range(4)]
        wh = [at(f"wh{i}", [P, UNIT], F32R) for i in range(2)]
        wl = [at(f"wl{i}", [P, UNIT], F32R) for i in range(2)]
        sq = [at(f"sq{i}", [P, S]) for i in range(2)]
        tmp = [at(f"tmp{i}", [P, S]) for i in range(2)]
        prod = [at(f"prod{i}", [P, S]) for i in range(2)]
        acc = at("acc", [P, S])
        rs = at("rs", [P, S])
        ident = at("ident", [P, P])
        ones = at("ones", [P, P])
        vec = at("vec", [P, V_N])
        mix_at = place[0]
        mid = at("mid", [P, FF2C, 2, S], F32R)
        assert place[0] <= 229368, place[0]

        o = mix_at
        proj = at("proj", [P, N_PROJ, S], offset=o); o += N_PROJ * S * 4
        sm = at("sm", [P, SM_W], offset=o); o += SM_W * 4
        tb1 = at("tb1", [P, T_N], offset=o); o += T_N * 4
        vtok = at("vtok", [P, QT, 2, P], offset=o); o += QT * 2 * P * 4
        s1_at = o
        assert s1_at + 1056 * 4 <= mix_at + FF2C * 2 * S * 4, (s1_at - mix_at)
        at_gla = at("at_gla", [P, QT, 6, P], offset=y_at)
        st_gla = at("st_gla", [P, 8, 2, HD], offset=y_at + QT * 6 * P * 4)
        pt1 = [at(f"pt1_{i}", [P, 9 * P], offset=y_at + i * 9 * P * 4) for i in range(2)]
        sc1 = [at("sc1_0", [P, 1056], offset=y_at + 18 * P * 4), at("sc1_1", [P, 1056], offset=s1_at)]
        gt = [at(f"gt{i}", [P, 2, S], offset=x_at + i * 4096) for i in range(3)]
        xp = [at(f"xp{i}", [P, 32, 32], offset=x_at + i * 4096) for i in range(2)]
        kc_c = at("kc_c", [P, 32], offset=x_at + 8192)
        vc_c = at("vc_c", [32, P], offset=x_at + 8320)
        hid = at("hid", [P, 2, 32], offset=x_at + 8832)
        gate_c = at("gate_c", [P, QT, 18], offset=s1_at + 1056 * 4)
        cmpb = at("cmpb", [P, 2], offset=s1_at + 1056 * 4 + 288)
        otok1 = at("otok1", [P, QT, P], offset=s1_at + 1056 * 4 + 320)
        assert s1_at + 1056 * 4 + 320 + QT * P * 4 <= mix_at + FF2C * 2 * S * 4
        o = mix_at
        aq = at("aq", [P, 9, S], offset=o); o += 9 * S * 4
        av = at("av", [P, QT, 3, P], offset=o); o += QT * 3 * P * 4
        tba = at("tba", [P, A_N], offset=o); o += A_N * 4
        sca = [at(f"sca{i}", [P, 12 * P], offset=o + i * 12 * P * 4) for i in range(2)]; o += 24 * P * 4
        pta = [at(f"pta{i}", [P, 12 * P], offset=o + i * 12 * P * 4) for i in range(2)]; o += 24 * P * 4
        otok = at("otok", [P, QT, P], offset=o); o += QT * P * 4
        ao = at("ao", [P, 4, 2, S], F32R, offset=o); o += 4 * 2 * S * 4
        assert o <= mix_at + FF2C * 2 * S * 4
        o = mix_at
        bk = at("bk", [P, 6, S], offset=o); o += 6 * S * 4
        bv = at("bv", [P, QT, P], offset=o); o += QT * P * 4
        tbb = at("tbb", [P, B_N], offset=o); o += B_N * 4
        scb = [at(f"scb{i}", [P, 12 * P], offset=o + i * 12 * P * 4) for i in range(2)]; o += 24 * P * 4
        ptb = [at(f"ptb{i}", [P, 12 * P], offset=o + i * 12 * P * 4) for i in range(2)]; o += 24 * P * 4
        otokb = at("otokb", [P, QT, P], offset=o); o += QT * P * 4
        bo = at("bo", [P, DC, 2, S], F32R, offset=o); o += DC * 2 * S * 4
        assert o <= mix_at + FF2C * 2 * S * 4
        pf = at("pf", [P, 2, S], offset=mix_at)
        px = at("px", [P, 2, 2, S], F32R, offset=mix_at + 4096)
        emb = at("emb", [P, DC, S], offset=mix_at + 12288)
        mx = at("mx", [P, 2, 4])
        negm = at("negm", [P, 2, 4])
        den = at("den", [P, 2, 4])
        rden = at("rden", [P, 2, 4])
        esink = at("esink", [P, 2, 2])
        eps = at("eps", [P, 2])
        assert place[0] <= 229368, place[0]

        bank = [ctx.enter_context(nc.psum_tensor(f"bank{i}", [P, S], F32)) for i in range(8)]

        raw_in = [sem(f"raw_in{i}") for i in range(4)]
        hi_done = sem("hi_done")
        split_done = sem("split_done")
        unit_done = sem("unit_done")
        bank_free = [sem("bank_free0"), sem("bank_free1")]
        relu_done = sem("relu_done")
        mid_hi, mid_ready = sem("mid_hi"), sem("mid_ready")
        sq_done, acc_done = sem("sq_done"), sem("acc_done")
        acc_clear = sem("acc_clear")
        stat_done = sem("stat_done")
        centred, sq_made, sq_used = sem("centred"), sem("sq_made"), sem("sq_used")
        rstd_ready, normed, affine = sem("rstd_ready"), sem("normed"), sem("affine")
        xf_done, x_hi, x_ready = sem("xf_done"), sem("x_hi"), sem("x_ready")
        h_ready = sem("h_ready")
        consts_in, h_in = sem("consts_in"), sem("h_in")
        tab_in, sm_in, p_in = sem("tab_in"), sem("sm_in"), sem("p_in")
        area_free = sem("area_free")
        dve_step, act_step, pool_step = sem("dve_step"), sem("act_step"), sem("pool_step")
        rot_done, rope_used, rope_done = sem("rot_done"), sem("rope_used"), sem("rope_done")
        turned, turn_read = sem("turned"), sem("turn_read")
        z_done, gk_act, gk_done = sem("z_done"), sem("gk_act"), sem("gk_done")
        gla_exp, gla_in, gla_kend = sem("gla_exp"), sem("gla_in"), sem("gla_kend")
        ds_done, st_done = sem("ds_done"), sem("st_done")
        am_done, am_read = sem("am_done"), sem("am_read")
        go_done, go_copied, go_sq, go_stat = sem("go_done"), sem("go_copied"), sem("go_sq"), sem("go_stat")
        go_rstd, go_silu, go_out = sem("go_rstd"), sem("go_silu"), sem("go_out")
        mx_hi, mx_ready = sem("mx_hi"), sem("mx_ready")
        pooled, pool_mm = sem("pooled"), sem("pool_mm")
        cmp_in, cmp_mm, cmp_bias, cmp_hid, cmp_out, cmp_ready = (
            sem("cmp_in"), sem("cmp_mm"), sem("cmp_bias"), sem("cmp_hid"), sem("cmp_out"), sem("cmp_ready"))
        gate_exp, gate_in = sem("gate_exp"), sem("gate_in")
        scored, score_read = sem("scored"), sem("score_read")
        max_ready, exp_done = sem("max_ready"), sem("exp_done")
        blk_turned = sem("blk_turned")
        blk_act, blk_dve = sem("blk_act"), sem("blk_dve")
        pv_done, o_done, o_read = sem("pv_done"), sem("o_done"), sem("o_read")
        ot_turned, ot_hi, ot_ready = sem("ot_turned"), sem("ot_hi"), sem("ot_ready")
        sink_exp = sem("sink_exp")
        p_hi, p_ready, emb_read = sem("p_hi"), sem("p_ready"), sem("emb_read")
        sig_done, gated = sem("sig_done"), sem("gated")
        out_done = sem("out_done")

        def gv_t(rows, t, head):
            return proj[rows, VS + head // 2, t * P + head % 2 * HD:t * P + head % 2 * HD + HD]

        def jobs_nsa(c):
            for g in range(2):
                r = slice(g * HD, g * HD + HD)
                for t in range(QT):
                    n = (t + 1) * P
                    ts = slice(t * P, t * P + P)
                    caus = tb1[:, T_CAUS + (QT - 1 - t) * P:T_CAUS + QT * P]
                    yield dict(
                        q=proj[r, Q0 + c, ts], kind="nsa", t=t, g=g, head=g * 3 + c,
                        segs=[(kc_c[r, 0:N_CMP], tb1[:, T_CMP + t * 32:T_CMP + t * 32 + N_CMP],
                               [vc_c[0:N_CMP, r]], 0),
                              (proj[r, KS, 0:n], caus, [vtok[:, k, 0, r] for k in range(t + 1)], 1),
                              (proj[r, KW, 0:n], caus, [vtok[:, k, 1, r] for k in range(t + 1)], 2)])

        def jobs_a():
            for g in range(2):
                r = slice(g * HD, g * HD + HD)
                for t in range(QT):
                    lo, hi = max(t - 1, 0), min(t + 2, QT)
                    ts = slice(t * P, t * P + P)
                    yield dict(
                        q=[aq[r, k, ts] for k in range(3)], kind="a", t=t, g=g, head=g,
                        segs=[(aq[r, 3, lo * P:hi * P], tba[:, A_M0 + (lo - t + 1) * P:A_M0 + (hi - t + 1) * P],
                               [av[:, k, 0, r] for k in range(lo, hi)], 0),
                              (aq[r, 4, :], tba[:, A_M1 + (3 - t) * P:A_M1 + (7 - t) * P],
                               [av[:, k, 1, r] for k in range(QT)], 0),
                              (aq[r, 5, :], tba[:, A_M2:A_M2 + S], [av[:, k, 2, r] for k in range(QT)], 0)])

        def jobs_b(c4, c):
            for g in range(2):
                r = slice(g * HD, g * HD + HD)
                for t in range(QT):
                    lo, hi = max(t - 1, 0), min(t + 2, QT)
                    yield dict(
                        q=bk[r, 2 + c, t * P:t * P + P], kind="b", t=t, g=g, head=8 * c4 + 4 * g + c,
                        segs=[(bk[r, 0, lo * P:hi * P], tbb[:, B_M + (lo - t + 1) * P:B_M + (hi - t + 1) * P],
                               [bv[:, k, r] for k in range(lo, hi)], 0)])

        def spans(job):
            off, out_ = 0, []
            for k, m, v, s in job["segs"]:
                w = k.shape[-1]
                out_.append((off, w, [(off + j * P, min(P, w - j * P)) for j in range(len(v))]))
                off += w if w >= P else 32
            return out_, off

        def blocks(job):
            b = [(si, j, o_, w) for si, (_, _, tiles) in enumerate(spans(job)[0]) for j, (o_, w) in enumerate(tiles)]
            return [b[i:i + 4] for i in range(0, len(b), 4)]

        block = ctx.enter_context(nc.Block())

        @block.sync
        def _(sp):
            c = Count(sp)

            def load(k, wait=True):
                if wait:
                    sp.wait_ge(split_done, c.at("unit", back=3))
                sp.dma_start(raw[k % 4][:, :], stream[c.at("unit"), :, :]).then_inc(raw_in[k % 4], 16)
                c.tick("unit")

            for k in range(4):
                load(k, False)
            rounds = (n_units - 4) // 4
            with c.loop(rounds, unit=4):
                for k in range(4):
                    load(k)
            for k in range((n_units - 4) % 4):
                load(k)
            for k in range(DC):
                sp.wait_ge(h_ready, 7 * DC + k + 1)
                sp.dma_start(out[k], h[:, k, :]).then_inc(out_done, 16)
            sp.wait_ge(out_done, 16 * DC)

        @block.gpsimd
        def _(pool):
            c = Count(pool)
            pool.dma_start(ident[:, :], consts[0]).then_inc(consts_in, 16)
            pool.dma_start(ones[:, :], consts[1]).then_inc(consts_in, 16)
            pool.dma_start(vec[:, :], vecs).then_inc(consts_in, 16)
            pool.dma_start(h[:, :, :], x_t.rearrange("(c p) t -> p c t", p=P)).then_inc(h_in, 16)
            pool.memset(eps[:, 0:1], LN_EPS).then_inc(pool_step, 1)
            pool.memset(eps[:, 1:2], RMS_EPS).then_inc(pool_step, 1)

            n_ln = 2 * DEPTH

            def square_sums():
                k = c.n.get("posts", 0)
                if k:
                    pool.wait_ge(stat_done, n_ln + k)
                pool.memset(acc[:, :], 0.0).then_inc(acc_done, 1)
                c.wait(acc_done)
                for m in range(DC):
                    c.wait(sq_done)
                    pool.tensor_tensor(acc[:, :], acc[:, :], sq[m % 2][:, :], ALU.add).then_inc(acc_done, 1)
                    c.wait(acc_done)
                c.tick("posts")

            def after(units_):
                pool.wait_ge(unit_done, units_)

            ffn, ple = 2 * FF2C + 3 * DC, 2 + DC
            u = 0
            for layer in range(DEPTH):
                if layer:
                    after(u)
                pool.dma_start(sm[:, :], small[layer]).then_inc(sm_in, 16)
                pool.dma_start(tb1[:, :], tab1).then_inc(tab_in, 16)
                u += N_PROJ + DC + 8 * DC
            for layer in range(DEPTH):
                square_sums()
                u += ffn
                after(u)
                if layer == 0:
                    pool.dma_start(tba[:, :], tab_a).then_inc(tab_in, 16)
                else:
                    pool.dma_start(tbb[:, :], tab_b).then_inc(tab_in, 16)
                square_sums()
                square_sums()
                u += (40, 20)[layer] + ffn
                after(u)
                pool.dma_start(pf[:, :, :], p_t[layer].rearrange("(c p) t -> p c t", p=P)).then_inc(p_in, 16)
                square_sums()
                u += ple
            assert u == n_units, (u, n_units)

        @block.tensor
        def _(pe):
            c = Count(pe)

            def unit(bk_, cols, src, chunks, start, stop, last=True):
                u = c.n.get("unit", 0) % 2
                for j, (col, kc) in enumerate(zip(cols, chunks)):
                    hi = wh[u][:, col:col + P]
                    lo = wl[u][:, col:col + P]
                    pe.matmul(bk_[:, :], hi, src[:, kc, 0, :], start=start and j == 0, stop=False)
                    pe.matmul(bk_[:, :], hi, src[:, kc, 1, :], start=False, stop=False)
                    mm = pe.matmul(bk_[:, :], lo, src[:, kc, 0, :], start=False, stop=stop and j == len(cols) - 1)
                if last:
                    mm.then_inc(unit_done, 1)
                    c.tick("unit")

            def tile(src, spread=(range(8),)):
                t = c.next_tile()
                if c.n[f"used{t}"] > 1:
                    pe.wait_ge(bank_free[t], c.at(f"used{t}", back=1))
                for n, chunks in enumerate(spread):
                    pe.wait_ge(split_done, c.at("unit") + 1)
                    unit(bank[t], [j * P for j in range(len(chunks))], src, chunks, n == 0, n == len(spread) - 1)

            def read_all():
                for t in range(2):
                    pe.wait_ge(bank_free[t], c.at(f"used{t}"))
                if c.n.get("ot", 0):
                    pe.wait_ge(ot_ready, c.n["ot"])

            def stat_h():
                read_all()
                for k in range(DC):
                    mm = pe.matmul(bank[2][:, :], ones[:, :], h[:, k, :], start=k == 0, stop=k == DC - 1)
                mm.then_inc(stat_done, 1)

            def stat():
                c.wait(acc_done, DC + 1)
                pe.matmul(bank[2][:, :], ones[:, :], acc[:, :], start=True, stop=True).then_inc(stat_done, 1)

            def stat_chunks():
                for k in range(DC):
                    c.wait(sq_made)
                    pe.matmul(bank[3][:, :], ones[:, :], sq[k % 2][:, :], start=k == 0,
                              stop=k == DC - 1).then_inc(sq_used, 1)

            def rope(chunks):
                for ap, rot in chunks:
                    if c.n.get("rope", 0) >= 2:
                        pe.wait_ge(rope_used, c.at("rope", back=1))
                    pe.matmul(bank[2 + c.n.get("rope", 0) % 2][:, :], rot, ap, start=True, stop=True).then_inc(rot_done, 1)
                    c.tick("rope")

            def turn(groups, free=turn_read):
                for n, g in enumerate(groups):
                    k = c.n.get("turn", 0)
                    if k >= 2:
                        pe.wait_ge(free, c.at("turn", back=1))
                    for i, (dst, src) in enumerate(g):
                        mm = pe.transpose(dst(bank[4 + k % 2]), src, ident[:src.shape[0], :src.shape[0]])
                    mm.then_inc(turned, 1)
                    c.tick("turn")

            def attend(jobs, sc, pt):
                jobs = list(jobs)
                if c.n.get("ot", 0):
                    pe.wait_ge(ot_ready, c.n["ot"])

                def scores(j):
                    job = jobs[j]
                    for si, (k, m, v, s) in enumerate(job["segs"]):
                        n = c.n.get("scored", 0)
                        key = f"bank_seg{si}"
                        if c.n.get(key, 0):
                            pe.wait_ge(score_read, c.n[key])
                        q = job["q"][si] if isinstance(job["q"], list) else job["q"]
                        pe.matmul(bank[2 + si][:, 0:k.shape[-1]], q, k, start=True, stop=True).then_inc(scored, 1)
                        c.tick("scored")
                        c.n[key] = n + 1

                def turns(j):
                    job = jobs[j]
                    n_softmax = len({s for *_, s in job["segs"]})
                    c.wait(exp_done, n_softmax)
                    for grp in blocks(job):
                        k = c.n.get("blk", 0)
                        b = k % 2
                        if c.n.get(f"blk{b}", 0):
                            pe.wait_ge((blk_act, blk_dve)[b], c.n[f"blk{b}"])
                        for i, (si, t_, off, w) in enumerate(grp):
                            mm = pe.transpose(bank[5 + b][0:w, i * P:i * P + P], sc[j % 2][:, off:off + w], ident[:, :])
                        mm.then_inc(blk_turned, 1)
                        c.tick("blk")
                        c.tick(f"blk{b}")

                def values(j):
                    job = jobs[j]
                    for b in range(2):
                        if c.n.get(f"blk{b}", 0):
                            pe.wait_ge((blk_act, blk_dve)[b], c.n[f"blk{b}"])
                    n = c.n.get("o", 0)
                    if n >= 2:
                        pe.wait_ge(o_read, n - 1)
                    flat = [x_ for g in blocks(job) for x_ in g]
                    for s in sorted({s for *_, s in job["segs"]}):
                        mine = [(p_, f) for p_, f in enumerate(flat) if job["segs"][f[0]][3] == s]
                        for q_, (p_, (si, t_, off, w)) in enumerate(mine):
                            mm = pe.matmul(bank[(7, 0)[n % 2]][:, s * HD:s * HD + HD],
                                           pt[j % 2][0:w, p_ * P:p_ * P + P], job["segs"][si][2][t_],
                                           start=q_ == 0, stop=q_ == len(mine) - 1, skip_group_check=True)
                    mm.then_inc(o_done, 1)
                    c.tick("o")

                scores(0)
                for j in range(len(jobs)):
                    if j + 1 < len(jobs):
                        scores(j + 1)
                    turns(j)
                    values(j)

            def turn_out(src):
                pe.wait_ge(o_read, c.n["o"])
                if c.n.get("ot", 0):
                    pe.wait_ge(ot_ready, c.n["ot"])
                for t in range(QT):
                    mm = pe.transpose(bank[4][:, t * P:t * P + P], src[:, t, :], ident[:, :])
                mm.then_inc(ot_turned, 1)
                c.tick("ot")

            def gla():
                c.wait(sm_in, 16)
                for i, (a, b) in enumerate(((0, 128), (128, 192))):
                    pe.matmul(bank[6 + i][0:b - a, :], sm[GLR_ROW:GLR_ROW + 16, SM_G2 + a:SM_G2 + b],
                              proj[GLR_ROW:GLR_ROW + 16, GQX, :], start=True, stop=True).then_inc(z_done, 1)
                turn([[(lambda b, i=i: b[:, i * P:i * P + P], proj[:, ch, i * P:i * P + P]) for i in range(QT)]
                      for ch in (VS, VW, GV, GV + 1, GV + 2, GQX)])
                c.wait(gla_kend)
                turn([[(lambda b, i=i, w=w: b[:, i * w:i * w + w], proj[0:w, ch, i * P:i * P + P]) for i in range(QT)]
                      for ch, w in ((GK, 128), (GKX, 64))])
                pe.wait_ge(turn_read, c.n["turn"])
                for n in range(8):
                    t, half = n // 2, n % 2
                    r = slice(half * 64, half * 64 + 64)
                    for hh in range(6):
                        gi, q = hh // 4, hh % 4
                        mm = pe.matmul(bank[(2, 3, 6, 7)[half * 2 + gi]][q * 32:q * 32 + 32, n // 2 * HD:n // 2 * HD + HD],
                                       gt[2][r, :, :].rearrange("p a s -> p (a s)")[:, t * 192 + hh * 32:t * 192 + hh * 32 + 32],
                                       gv_t(r, t, hh), start=True, stop=True, skip_group_check=True)
                mm.then_inc(ds_done, 1)
                c.wait(st_done)
                for t in range(QT):
                    if t:
                        c.wait(am_read)
                    ts = slice(t * P, t * P + P)
                    for hh in range(6):
                        r = slice(hh % 4 * 32, hh % 4 * 32 + 32)
                        mm = pe.matmul(bank[(2, 3, 6, 7)[hh % 4]][:, hh // 4 * P:hh // 4 * P + P],
                                       gt[1][r, hh // 4, ts], proj[r, (GQ, GQX)[hh // 4], ts],
                                       start=True, stop=True, skip_group_check=True)
                    mm.then_inc(am_done, 1)
                c.wait(am_read)
                for cc in range(3):
                    for e in range(2):
                        hh = 2 * cc + e
                        r = slice(hh % 4 * 32, hh % 4 * 32 + 32)
                        if e == 0 and cc:
                            c.wait(go_copied)
                        for t in range(QT):
                            dst = bank[2 + e][e * HD:e * HD + HD, :]
                            pe.matmul(dst[:, t * P:t * P + P], gv_t(slice(0, P), t, hh), at_gla[:, t, hh, :],
                                      start=True, stop=False, skip_group_check=True)
                            for n in (2 * t, 2 * t + 1):
                                mm = pe.matmul(dst[:, n * 64:n * 64 + 64], st_gla[r, n, hh // 4, :],
                                               proj[r, (GQ, GQX)[hh // 4], n * 64:n * 64 + 64],
                                               start=False, stop=n % 2 == 1, skip_group_check=True)
                    mm.then_inc(go_done, 1)
                    c.wait(go_sq)
                    pe.matmul(bank[6][:, :], tb1[:, T_B64:T_B64 + P], sq[0][:, :], start=True, stop=True).then_inc(go_stat, 1)
                c.wait(go_copied)

            def pool_mix():
                for k in range(2):
                    c.wait(pooled)
                    for e in range(2):
                        r = slice(e * HD, e * HD + HD)
                        mm = pe.matmul(bank[2 + e][r, :], sm[r, SM_PW + k * HD:SM_PW + k * HD + HD], gt[0][r, 0, :],
                                       start=True, stop=True)
                    mm.then_inc(pool_mm, 1)

            def compress():
                for kind in range(2):
                    c.wait(cmp_in)
                    for g in range(2):
                        r = slice(g * HD, g * HD + HD)
                        for j in range(32):
                            mm = pe.matmul(bank[(2, 0)[kind] + g][r, 0:32], sm[r, SM_W1 + kind * 2048 + j * HD:SM_W1 + kind * 2048 + j * HD + HD],
                                           xp[kind][r, j, :], start=j == 0, stop=j == 31, skip_group_check=True)
                    mm.then_inc(cmp_mm, 1)
                c.wait(cmp_hid, 4)
                for g in range(2):
                    r = slice(g * HD, g * HD + HD)
                    pe.matmul(bank[6 + g][r, 0:N_CMP], sm[r, SM_W2:SM_W2 + HD], hid[r, 0, 0:N_CMP], start=True, stop=True, skip_group_check=True)
                    mm = pe.matmul(bank[4 + g][0:N_CMP, r], hid[r, 1, 0:N_CMP], sm[r, SM_W2 + HD:SM_W2 + 2 * HD], start=True, stop=True, skip_group_check=True)
                mm.then_inc(cmp_out, 1)
                c.wait(cmp_ready)

            c.wait(consts_in, 48)
            for layer in range(DEPTH):
                c.wait(x_ready, DC)
                if layer == 0:
                    for k in range(5):
                        tile(x)
                    with c.loop(4, unit=4, **TILES4):
                        for k in range(4):
                            tile(x)
                else:
                    tile(x)
                    with c.loop(5, unit=4, **TILES4):
                        for k in range(4):
                            tile(x)
                read_all()
                c.wait(tab_in, 16)
                rope([(proj[:, k, :], tb1[:, T_ROT:T_ROT + P]) for k in (0, 1, 2, KC, KS, KW)])
                gla()
                pool_mix()
                compress()
                for k in range(3):
                    attend(jobs_nsa(k), sc1, pt1)
                    turn_out(otok1)
                c.wait(x_ready, 5)
                read_all()
                with c.loop(2, unit=4, **TILES4):
                    for k in range(4):
                        tile(x)
                stat_h()
                stat_chunks()
                c.wait(x_ready, DC)
                for half in range(2):
                    with c.loop(4, unit=4, **TILES4):
                        for k in range(4):
                            tile(x)
                    c.wait(mid_ready, 16)
                    with c.loop(4, unit=4, **TILES2):
                        for k in range(2):
                            tile(mid, (range(0, 8), range(8, 16)))
                stat_h()
                stat_chunks()

            def ffn2():
                with c.loop(FF2C // 2, unit=4, **TILES4):
                    for k in range(4):
                        tile(x)
                c.wait(mid_ready, FF2C)
                with c.loop(2, unit=12, **TILES4):
                    for k in range(4):
                        tile(mid, (range(0, 8), range(8, 16), range(16, FF2C)))
                stat()

            for layer in range(DEPTH):
                stat_chunks()
                c.wait(x_ready, DC)
                ffn2()
                stat_chunks()
                c.wait(x_ready, DC)
                if layer == 0:
                    c.wait(tab_in, 16)
                    for pair in range(4):
                        for k in range(9):
                            tile(x)
                        read_all()
                        rope([(aq[:, k, :], tba[:, A_ROT:A_ROT + P]) for k in range(6)])
                        turn([[(lambda b, i=i: b[:, i * P:i * P + P], aq[:, 6 + g, i * P:i * P + P]) for i in range(QT)]
                              for g in range(3)])
                        pe.wait_ge(turn_read, c.n["turn"])
                        c.wait(rope_done, 6)
                        attend(jobs_a(), sca, pta)
                        turn_out(otok)
                    read_all()
                    for n in range(4):
                        pe.wait_ge(split_done, c.at("unit") + 1)
                        if n >= 2:
                            c.wait(emb_read, 2)
                        for j in range(2):
                            unit(bank[n % 2 * 2 + j], [j * 512 + q * P for q in range(4)], ao, range(4), True, True, last=j == 1)
                    c.wait(emb_read, 4)
                else:
                    c.wait(tab_in, 16)
                    for c4 in range(2):
                        for k in range(6):
                            tile(x)
                        read_all()
                        rope([(bk[:, k, :], tbb[:, B_ROT:B_ROT + P]) for k in (0, 2, 3, 4, 5)])
                        turn([[(lambda b, i=i: b[:, i * P:i * P + P], bk[:, 1, i * P:i * P + P]) for i in range(QT)]])
                        pe.wait_ge(turn_read, c.n["turn"])
                        c.wait(rope_done, 5)
                        for k in range(4):
                            attend(jobs_b(c4, k), scb, ptb)
                            turn_out(otokb)
                    read_all()
                    with c.loop(2, unit=4, **TILES4):
                        for k in range(4):
                            tile(bo)
                stat()
                stat_chunks()
                c.wait(x_ready, DC)
                ffn2()
                stat_chunks()
                c.wait(p_ready, 2)
                read_all()
                for n in range(2):
                    pe.wait_ge(split_done, c.at("unit") + 1)
                    if n == 1:
                        c.wait(emb_read, 4)
                    for j in range(4):
                        unit(bank[4 + j], [j * 256, j * 256 + P], px, range(2), True, True, last=j == 3)
                c.wait(emb_read, 4)
                c.wait(x_ready, DC)
                with c.loop(2, unit=4, **TILES4):
                    for k in range(4):
                        tile(x)
                stat()

        @block.scalar
        def _(act):
            c = Count(act)

            def split(last=False):
                if last:
                    return
                n = c.n.get("split", 0)
                act.wait_ge(raw_in[n % 4], c.at("split", back=-1, div=4, mult=16))
                if n >= 2:
                    act.wait_ge(unit_done, c.at("split", back=1))
                act.activation(wh[n % 2][:, :], raw[n % 4][:, :], ACT.Copy).then_inc(hi_done, 1)
                c.tick("split")

            def units(n, last=False):
                for k in range(n):
                    split(last and k == n - 1)
                c.wait(unit_done, n)

            def link(ins):
                ins.then_inc(act_step, 1)
                c.wait(act_step)

            def rstd(src, e, banks=1):
                link(act.activation(rs[:, :], src, ACT.Ln, bias=eps[:, e:e + 1]))
                act.activation(rs[:, :], rs[:, :], ACT.Exp, scale=-0.5).then_inc(rstd_ready, 1)

            def squares(ready=None):
                for k in range(DC):
                    if ready is not None:
                        c.wait(ready)
                    n = c.n.get("sqm", 0)
                    if n >= 2:
                        act.wait_ge(sq_used, n - 1)
                    act.activation(sq[k % 2][:, :], h[:, k, :], ACT.Square).then_inc(sq_made, 1)
                    c.tick("sqm")

            def layer_norm(g, b, to_x):
                c.tick("stat_done")
                squares(centred)
                c.wait(sq_used, DC)
                rstd(bank[3][:, :], 0)
                for k in range(DC):
                    c.wait(normed)
                    link(act.activation(h[:, k, :], h[:, k, :], ACT.Identity, bias=vec[:, b + k:b + k + 1],
                                        scale=vec[:, g + k:g + k + 1]))
                    if to_x:
                        act.activation(x[:, k, 0, :], h[:, k, :], ACT.Copy).then_inc(x_hi, 1)

            def rms_pre(ready):
                squares(ready)
                c.wait(sq_used, DC)
                rstd(bank[3][:, :], 1)
                for k in range(DC):
                    c.wait(xf_done)
                    act.activation(x[:, k, 0, :], prod[k % 2][:, :], ACT.Copy).then_inc(x_hi, 1)

            def rms_post():
                c.tick("acc")
                c.wait(stat_done)
                rstd(bank[2][:, :], 1)

            def tile_square(n, last=False):
                units(n, last)
                square_of(bank[c.next_tile()][:, :])

            def square_of(src):
                k = c.n.get("sqs", 0)
                act.wait_ge(acc_done, c.at("acc") + 1)
                act.activation(sq[k % 2][:, :], src, ACT.Square).then_inc(sq_done, 1)
                c.tick("sqs")
                c.tick("acc")

            def attend(jobs, sc, pt):
                jobs = list(jobs)

                def exps(j):
                    job = jobs[j]
                    sp_, total = spans(job)
                    n = c.n.get("job", 0) % 2
                    groups = {}
                    for si, (off, w, _) in enumerate(sp_):
                        groups.setdefault(job["segs"][si][3], []).append((off, w))
                    c.wait(max_ready)
                    for s, parts in sorted(groups.items()):
                        a, b = parts[0][0], parts[-1][0] + parts[-1][1]
                        act.activation(sc[j % 2][:, a:b], sc[j % 2][:, a:b], ACT.Exp, bias=negm[:, n, s:s + 1],
                                       scale=0.125, accum_out=den[:, n, s:s + 1]).then_inc(exp_done, 1)
                    if job["kind"] == "b":
                        hd_ = V_SINK + job["head"]
                        act.activation(esink[:, n, 0:1], vec[:, hd_:hd_ + 1], ACT.Exp, bias=negm[:, n, 0:1]).then_inc(sink_exp, 1)
                    c.tick("job")

                exps(0)
                for j in range(len(jobs)):
                    for gi, grp in enumerate(blocks(jobs[j])):
                        c.tick("blk_turned")
                        k = c.n.get("blk", 0)
                        c.tick("blk")
                        if k % 2:
                            continue
                        act.wait_ge(blk_turned, c.n["blk_turned"])
                        if c.n.get("o", 0) >= 2:
                            act.wait_ge(o_done, c.n["o"] - 1)
                        copy_group(act.activation, pt[j % 2], gi, grp, bank[5], blk_act)
                    c.tick("o")
                    if j + 1 < len(jobs):
                        exps(j + 1)

            def copy_group(op, pt_, gi, grp, src, done):
                if all(w == P for *_, w in grp):
                    op(pt_[:, gi * 512:gi * 512 + len(grp) * P], src[:, 0:len(grp) * P], ACT.Copy).then_inc(done, 1)
                    return
                w0 = grp[0][3]
                assert gi == 0 and all(w == P for *_, w in grp[1:])
                if len(grp) > 1:
                    op(pt_[:, P:len(grp) * P], src[:, P:len(grp) * P], ACT.Copy)
                op(pt_[0:w0, 0:P], src[0:w0, 0:P], ACT.Copy).then_inc(done, 1)

            def turn_out(dst):
                c.wait(ot_turned)
                act.activation(dst, bank[4][:, :], ACT.Copy).then_inc(ot_hi, 1)

            act.preload_act_table_set("natural_log_exp_and_others")
            split()
            c.wait(h_in, 16)
            act.wait_ge(pool_step, 2)
            for k in range(DC):
                act.activation(x[:, k, 0, :], h[:, k, :], ACT.Copy).then_inc(x_hi, 1)
            act.wait_ge(consts_in, 48)

            for layer in range(DEPTH):
                done = (5, 1)[layer]
                for k in range(done):
                    units(1)
                    c.next_tile()
                with c.loop((N_PROJ - done) // 4, split=4, unit_done=4, **TILES4):
                    for k in range(4):
                        units(1)
                        c.next_tile()
                for i, w in enumerate((128, 64)):
                    c.wait(z_done)
                    bg = V_BG + 2 * layer + i
                    link(act.activation(gt[0][0:w, i, :], bank[6 + i][0:w, :], ACT.Abs, bias=vec[0:w, bg:bg + 1]))
                    link(act.activation(gt[0][0:w, i, :], gt[0][0:w, i, :], ACT.Exp, scale=-1.0))
                    act.activation(gt[0][0:w, i, :], gt[0][0:w, i, :], ACT.Ln, bias=1.0).then_inc(gk_act, 1)
                for i, w in enumerate((128, 64)):
                    c.wait(gk_done)
                    act.activation(gt[2][0:w, i, :], gt[0][0:w, i, :], ACT.Exp, scale=1.0 / 16).then_inc(gla_exp, 1)
                    act.activation(gt[1][0:w, i, :], gt[0][0:w, i, :], ACT.Exp, scale=-1.0 / 16).then_inc(gla_exp, 1)
                for i, w in enumerate((128, 64)):
                    c.wait(gk_done)
                    act.activation(gt[0][0:w, i, :], gt[0][0:w, i, :], ACT.Exp, scale=1.0 / 16).then_inc(gla_exp, 1)
                for cc in range(3):
                    c.wait(go_copied)
                    act.activation(sq[0][:, :], tmp[0][:, :], ACT.Square).then_inc(go_sq, 1)
                    link(act.activation(prod[0][:, :], proj[:, GO + cc, :], ACT.Exp, scale=-1.0))
                    act.activation(prod[0][:, :], prod[0][:, :], ACT.Identity, bias=1.0).then_inc(go_silu, 1)
                    c.wait(go_stat)
                    rstd(bank[6][:, :], 1)
                    c.wait(go_out)
                    act.activation(x[:, 3 + cc, 0, :], tmp[1][:, :], ACT.Copy).then_inc(mx_hi, 1)
                for k in range(2):
                    c.wait(pool_mm)
                    ps = V_PS + 2 * layer + k
                    for e in range(2):
                        r = slice(e * HD, e * HD + HD)
                        ins = act.activation(tmp[0][r, :], bank[2 + e][r, :], ACT.Copy, scale=vec[r, ps:ps + 1])
                    link(ins)
                    act.activation(x[:, 6 + k, 0, :], tmp[0][:, :], ACT.Copy).then_inc(mx_hi, 1)
                for kind in range(2):
                    for g in range(2):
                        r = slice(g * HD, g * HD + HD)
                        c.wait(cmp_bias)
                        act.activation(hid[r, kind, 0:N_CMP], tmp[0][r, 64:64 + N_CMP], ACT.Exp,
                                       scale=-2.0 * 0.7978845608028654).then_inc(gate_exp, 1)
                c.wait(cmp_ready)
                act.activation(gate_c[:, :, :], gate_c[:, :, :], ACT.Exp, scale=-1.0).then_inc(gate_exp, 1)
                for k in range(3):
                    attend(jobs_nsa(k), sc1, pt1)
                    turn_out(x[:, k, 0, :])
                with c.loop(2, split=4, unit_done=4, **TILES4):
                    for k in range(4):
                        units(1)
                        c.next_tile()
                layer_norm(V_LN + 32 * layer, V_LN + 32 * layer + 8, True)
                for half in range(2):
                    with c.loop(4, split=4, unit_done=4, **TILES4) as i:
                        for k in range(4):
                            units(1)
                            b = c.next_tile()
                            act.activation(tmp[k % 2][:, :], bank[b][:, :], ACT.Relu).then_inc(relu_done, 1)
                            act.wait_ge(bank_free[b], c.at(f"used{b}"))
                            act.activation(mid[:, i * 4 + k, 0, :], prod[k % 2][:, :], ACT.Copy).then_inc(mid_hi, 1)
                    with c.loop(4, split=4, unit_done=4, **TILES2):
                        for k in range(2):
                            units(2)
                            c.next_tile()
                layer_norm(V_LN + 32 * layer + 16, V_LN + 32 * layer + 24, layer == 0)

            def ffn2():
                with c.loop(FF2C // 2, split=4, unit_done=4, **TILES4) as i:
                    for k in range(2):
                        units(1)
                        b = c.next_tile()
                        act.activation(tmp[k][:, :], bank[b][:, :], ACT.Silu).then_inc(bank_free[b], 1)
                        units(1)
                        b = c.next_tile()
                        act.wait_ge(bank_free[b], c.at(f"used{b}"))
                        act.activation(mid[:, i * 2 + k, 0, :], prod[k][:, :], ACT.Copy).then_inc(mid_hi, 1)
                with c.loop(2, split=12, unit_done=12, sqs=4, acc=4, **TILES4):
                    for k in range(4):
                        tile_square(3)
                rms_post()

            for layer in range(DEPTH):
                rms_pre(h_ready if layer else None)
                ffn2()
                rms_pre(h_ready)
                if layer == 0:
                    for pair in range(4):
                        for k in range(9):
                            units(1)
                            c.next_tile()
                        attend(jobs_a(), sca, pta)
                        turn_out(ao[:, pair, 0, :])
                    for n in range(4):
                        units(1)
                        for j in range(2):
                            square_of(bank[n % 2 * 2 + j][:, :])
                else:
                    for c4 in range(2):
                        for k in range(6):
                            units(1)
                            c.next_tile()
                        for k in range(4):
                            attend(jobs_b(c4, k), scb, ptb)
                            turn_out(bo[:, c4 * 4 + k, 0, :])
                    with c.loop(2, split=4, unit_done=4, sqs=4, acc=4, **TILES4):
                        for k in range(4):
                            tile_square(1)
                rms_post()
                rms_pre(h_ready)
                ffn2()
                c.wait(p_in, 16)
                for k in range(2):
                    act.activation(px[:, k, 0, :], pf[:, k, :], ACT.Copy).then_inc(p_hi, 1)
                rms_pre(h_ready)
                units(2)
                for k in range(DC):
                    units(1, last=layer == DEPTH - 1 and k == DC - 1)
                    b = c.next_tile()
                    act.activation(tmp[k % 2][:, :], bank[b][:, :], ACT.Sigmoid).then_inc(bank_free[b], 1)
                    c.wait(sig_done)
                    square_of(y[:, k, :])
                rms_post()

        @block.vector
        def _(dve):
            c = Count(dve)

            def split(last=False):
                if last:
                    return
                n = c.n.get("hi_done", 0)
                c.wait(hi_done)
                dve.tensor_tensor(wl[n % 2][:, :], raw[n % 4][:, :], wh[n % 2][:, :].bitcast(F32),
                                  ALU.subtract).then_inc(split_done, 1)

            def units(n, last=False):
                for k in range(n):
                    split(last and k == n - 1)
                c.wait(unit_done, n)

            def link(ins):
                ins.then_inc(dve_step, 1)
                c.wait(dve_step)

            def free(ins):
                ins.then_inc(bank_free[c.next_tile()], 1)

            def lo_of(dst, src, hi, done):
                dve.tensor_tensor(dst, src, hi.bitcast(F32), ALU.subtract).then_inc(done, 1)
                c.tick(f"made {done.name}")

            def layer_norm(to_x):
                c.wait(stat_done)
                for k in range(DC):
                    dve.tensor_tensor(h[:, k, :], h[:, k, :], bank[2][:, :], ALU.subtract).then_inc(centred, 1)
                c.wait(centred, DC)
                c.wait(rstd_ready)
                for k in range(DC):
                    dve.tensor_tensor(h[:, k, :], h[:, k, :], rs[:, :], ALU.mult).then_inc(normed, 1)
                if to_x:
                    for k in range(DC):
                        c.wait(x_hi)
                        lo_of(x[:, k, 1, :], h[:, k, :], x[:, k, 0, :], x_ready)

            def rms_pre(g):
                c.wait(rstd_ready)

                def xf(k):
                    if k >= 2:
                        dve.wait_ge(x_ready, c.at(f"made {x_ready.name}"))
                    dve.scalar_tensor_tensor(prod[k % 2][:, :], h[:, k, :], vec[:, g + k:g + k + 1], rs[:, :],
                                             ALU.mult, ALU.mult).then_inc(xf_done, 1)
                xf(0)
                for k in range(DC):
                    if k + 1 < DC:
                        xf(k + 1)
                    c.wait(x_hi)
                    lo_of(x[:, k, 1, :], prod[k % 2][:, :], x[:, k, 0, :], x_ready)

            def rms_post(g):
                c.wait(rstd_ready)
                for k in range(DC):
                    link(dve.scalar_tensor_tensor(prod[k % 2][:, :], y[:, k, :], vec[:, g + k:g + k + 1], rs[:, :],
                                                  ALU.mult, ALU.mult))
                    dve.tensor_tensor(h[:, k, :], h[:, k, :], prod[k % 2][:, :], ALU.add).then_inc(h_ready, 1)

            def copy_tile(dst, n=1, last=False):
                units(n, last)
                free(dve.tensor_copy(dst, bank[c.n.get("tile", 0) % 2][:, :]))

            def copy_tile_sq(dst, n):
                units(n)
                c.wait(sq_done)
                free(dve.tensor_copy(dst, bank[c.n.get("tile", 0) % 2][:, :]))

            def rope(chunks, cos, sin):
                for ap in chunks:
                    c.wait(rot_done)
                    k = c.n.get("rope", 0)
                    dve.tensor_tensor(tmp[k % 2][:, :], bank[2 + k % 2][:, :], sin, ALU.mult).then_inc(rope_used, 1)
                    link(dve.tensor_tensor(ap, ap, cos, ALU.mult))
                    dve.wait_ge(rope_used, k + 1)
                    dve.tensor_tensor(ap, ap, tmp[k % 2][:, :], ALU.add).then_inc(rope_done, 1)
                    c.tick("rope")

            def turned_into(dst, src):
                c.wait(turned)
                k = c.n.get("turn", 0)
                dve.tensor_copy(dst, src(bank[4 + k % 2])).then_inc(turn_read, 1)
                c.tick("turn")

            def attend(jobs, sc, pt, ot):
                jobs = list(jobs)

                def masks(j):
                    job = jobs[j]
                    n = c.n.get("job", 0) % 2
                    sp_, _ = spans(job)
                    for si, (k, m, v, s) in enumerate(job["segs"]):
                        off, w, _ = sp_[si]
                        c.wait(scored)
                        dve.tensor_tensor_reduce(out=sc[j % 2][:, off:off + w], in0=bank[2 + si][:, 0:w], in1=m,
                                                 scale=1.0, scalar=-3.0e38, op0=ALU.add, op1=ALU.max,
                                                 accum_out=mx[:, n, si:si + 1]).then_inc(score_read, 1)
                        c.tick("score_read")
                    dve.wait_ge(score_read, c.n["score_read"])
                    if job["kind"] == "nsa":
                        dve.tensor_scalar(negm[:, n, 0:3], mx[:, n, 0:3], FLOOR, -0.125, ALU.max, ALU.mult).then_inc(max_ready, 1)
                    elif job["kind"] == "a":
                        link(dve.tensor_reduce(mx[:, n, 3:4], mx[:, n, 0:3], AX.X, ALU.max))
                        dve.tensor_scalar(negm[:, n, 0:1], mx[:, n, 3:4], -0.125, None, ALU.mult).then_inc(max_ready, 1)
                    else:
                        hd_ = V_SINK + job["head"]
                        link(dve.tensor_scalar(mx[:, n, 3:4], mx[:, n, 0:1], 0.125, None, ALU.mult))
                        link(dve.tensor_tensor(mx[:, n, 2:3], mx[:, n, 3:4], vec[:, hd_:hd_ + 1], ALU.max))
                        dve.tensor_scalar(negm[:, n, 0:1], mx[:, n, 2:3], -1.0, None, ALU.mult).then_inc(max_ready, 1)
                    c.tick("job")

                masks(0)
                for j in range(len(jobs)):
                    job = jobs[j]
                    if j + 1 < len(jobs):
                        masks(j + 1)
                    for gi, grp in enumerate(blocks(job)):
                        c.tick("blk_turned")
                        k = c.n.get("blk", 0)
                        c.tick("blk")
                        if k % 2 == 0:
                            continue
                        dve.wait_ge(blk_turned, c.n["blk_turned"])
                        copy_group(pt[j % 2], gi, grp, bank[6], blk_dve)
                    n = c.n.get("o_done", 0) % 2
                    c.wait(exp_done, len({s for *_, s in job["segs"]}))
                    if job["kind"] == "nsa":
                        link(dve.tensor_scalar(den[:, n, 0:3], den[:, n, 0:3], 1e-30, None, ALU.max))
                        link(dve.reciprocal(rden[:, n, 0:3], den[:, n, 0:3]))
                        gg = gate_c[:, job["t"], 3 * job["head"]:3 * job["head"] + 3]
                        link(dve.tensor_tensor(rden[:, n, 0:3], rden[:, n, 0:3], gg, ALU.mult))
                        nb = 3
                    elif job["kind"] == "b":
                        c.wait(sink_exp)
                        link(dve.tensor_tensor(den[:, n, 0:1], den[:, n, 0:1], esink[:, n, 0:1], ALU.add))
                        link(dve.reciprocal(rden[:, n, 0:1], den[:, n, 0:1]))
                        nb = 1
                    else:
                        link(dve.reciprocal(rden[:, n, 0:1], den[:, n, 0:1]))
                        nb = 1
                    c.wait(o_done)
                    dst = ot[:, job["t"], job["g"] * HD:job["g"] * HD + HD]
                    for s in range(nb):
                        src = bank[(7, 0)[n]][:, s * HD:s * HD + HD]
                        if s == 0:
                            ins = dve.tensor_scalar(dst, src, rden[:, n, 0:1], None, ALU.mult)
                        else:
                            ins = dve.scalar_tensor_tensor(dst, src, rden[:, n, s:s + 1], dst, ALU.mult, ALU.add)
                        if s < nb - 1:
                            link(ins)
                    ins.then_inc(o_read, 1)

            def copy_group(pt_, gi, grp, src, done):
                if all(w == P for *_, w in grp):
                    dve.tensor_copy(pt_[:, gi * 512:gi * 512 + len(grp) * P], src[:, 0:len(grp) * P]).then_inc(done, 1)
                    return
                w0 = grp[0][3]
                if len(grp) > 1:
                    dve.tensor_copy(pt_[:, P:len(grp) * P], src[:, P:len(grp) * P])
                dve.tensor_copy(pt_[0:w0, 0:P], src[0:w0, 0:P]).then_inc(done, 1)

            def turn_out(dst, hi):
                c.wait(ot_hi)
                dve.tensor_tensor(dst, bank[4][:, :], hi.bitcast(F32), ALU.subtract).then_inc(ot_ready, 1)

            def gla(layer):
                c.wait(z_done, 2)
                for i, w in enumerate((128, 64)):
                    bg = V_BG + 2 * layer + i
                    c.wait(gk_act)
                    link(dve.tensor_scalar(tmp[i][0:w, :], bank[6 + i][0:w, :], vec[0:w, bg:bg + 1], 0.0, ALU.add, ALU.min))
                    link(dve.tensor_tensor(tmp[i][0:w, :], tmp[i][0:w, :], gt[0][0:w, i, :], ALU.subtract))
                    dve.tensor_tensor_scan(gt[0][0:w, i, :], tb1[0:w, T_RESET:T_RESET + S], tmp[i][0:w, :], 0.0,
                                           ALU.mult, ALU.add).then_inc(gk_done, 1)
                for dst, src in ((vtok[:, :, 0, :], VS), (vtok[:, :, 1, :], VW)):
                    turned_into(dst, lambda b: b[:, :].rearrange("p (t d) -> p t d", t=QT))
                for k in range(3):
                    turned_into(proj[:, VS + k, :], lambda b: b[:, :])
                turned_into(gate_c[:, :, :], lambda b: b[:, :].rearrange("p (t d) -> p t d", t=QT)[:, :, GATE_ROW:GATE_ROW + 18])
                for i, (w, qc, kc) in enumerate(((128, GQ, GK), (64, GQX, GKX))):
                    c.wait(gla_exp, 2)
                    link(dve.scalar_tensor_tensor(proj[0:w, qc, :], proj[0:w, qc, :], 32.0 ** -0.5, gt[2][0:w, i, :], ALU.mult, ALU.mult))
                    link(dve.tensor_copy(prod[1][0:w, i * 8:i * 8 + 8], gt[2][0:w, i, 63::64]))
                    link(dve.tensor_tensor(gt[1][0:w, i, :], gt[1][0:w, i, :], proj[0:w, kc, :], ALU.mult))
                    b3 = gt[0][0:w, i, :].rearrange("p (n c) -> p n c", c=64)
                    link(dve.tensor_copy(prod[0][0:w, 0:8], gt[0][0:w, i, 63::64]))
                    last = prod[0][0:w, 0:8].rearrange("p (n o) -> p n o", o=1).broadcast_to([w, 8, 64])
                    dve.tensor_tensor(b3, last, b3, ALU.subtract).then_inc(gk_done, 1)
                for i, (w, kc) in enumerate(((128, GK), (64, GKX))):
                    c.wait(gla_exp)
                    ins = dve.tensor_tensor(proj[0:w, kc, :], proj[0:w, kc, :], gt[0][0:w, i, :], ALU.mult)
                    if i == 0:
                        link(ins)
                ins.then_inc(gla_kend, 1)
                kt_ = gt[2][:, :, :].rearrange("p a s -> p (a s)")[:, 0:QT * 192].rearrange("p (t d) -> p t d", t=QT)
                turned_into(kt_[:, :, 0:128], lambda b: b[:, :].rearrange("p (t d) -> p t d", t=QT))
                turned_into(kt_[:, :, 128:192], lambda b: b[:, 0:256].rearrange("p (t d) -> p t d", t=QT))
                link(dve.memset(st_gla[:, 0, :, :], 0.0))
                c.wait(ds_done)
                for n in range(7):
                    for gi, w in enumerate((128, 64)):
                        ins = dve.scalar_tensor_tensor(
                            st_gla[0:w, n + 1, gi, :], st_gla[0:w, n, gi, :], prod[1][0:w, gi * 8 + n:gi * 8 + n + 1],
                            bank[(2, 3, 6, 7)[n % 2 * 2 + gi]][0:w, n // 2 * HD:n // 2 * HD + HD], ALU.mult, ALU.add)
                        if n < 6 or gi == 0:
                            link(ins)
                ins.then_inc(st_done, 1)
                for t in range(QT):
                    c.wait(am_done)
                    for hh in range(6):
                        ins = dve.scalar_tensor_tensor(
                            at_gla[:, t, hh, :], bank[(2, 3, 6, 7)[hh % 4]][:, hh // 4 * P:hh // 4 * P + P], 3.0e38,
                            tb1[:, T_GLA:T_GLA + P], ALU.min, ALU.mult)
                    ins.then_inc(am_read, 1)
                for cc in range(3):
                    c.wait(go_done)
                    dve.tensor_copy(tmp[0][0:64, :], bank[2][0:64, :])
                    dve.tensor_copy(tmp[0][64:128, :], bank[3][64:128, :]).then_inc(go_copied, 1)
                    c.wait(go_copied)
                    c.wait(go_silu)
                    link(dve.reciprocal(prod[0][:, :], prod[0][:, :]))
                    link(dve.tensor_tensor(prod[0][:, :], prod[0][:, :], proj[:, GO + cc, :], ALU.mult))
                    c.wait(rstd_ready)
                    ng = V_NG + 3 * layer + cc
                    link(dve.scalar_tensor_tensor(tmp[1][:, :], tmp[0][:, :], vec[:, ng:ng + 1], rs[:, :], ALU.mult, ALU.mult))
                    dve.tensor_tensor(tmp[1][:, :], tmp[1][:, :], prod[0][:, :], ALU.mult).then_inc(go_out, 1)
                    c.wait(mx_hi)
                    lo_of(x[:, 3 + cc, 1, :], tmp[1][:, :], x[:, 3 + cc, 0, :], x_ready)

            def pool_mix(layer):
                for k in range(2):
                    src = proj[:, PU + k, :]
                    a, b = gt[0][:, 1, :], gt[1][:, 0, :]
                    cur, nxt, w = src, a, 1
                    steps = 2 if k == 0 else 4
                    res = {}
                    for s in range(steps):
                        dve.tensor_copy(nxt[:, 0:w], cur[:, 0:w])
                        link(dve.tensor_tensor(nxt[:, w:S], cur[:, w:S], cur[:, 0:S - w], ALU.add))
                        w *= 2
                        res[w] = nxt
                        cur = nxt
                        nxt = b if cur is a else a
                    for e in range(2):
                        r = slice(e * HD, e * HD + HD)
                        win = (2, 4, 8, 16)[2 * k + e]
                        ic = tb1[r, T_ICNT + k * S:T_ICNT + k * S + S]
                        link(dve.tensor_tensor(gt[1][r, 1, :], res[win][r, :], ic, ALU.mult))
                        ins = dve.tensor_tensor(gt[0][r, 0, :], gt[1][r, 1, :], src[r, :], ALU.subtract)
                        if e == 0:
                            link(ins)
                    ins.then_inc(pooled, 1)
                    c.wait(mx_hi)
                    lo_of(x[:, 6 + k, 1, :], tmp[0][:, :], x[:, 6 + k, 0, :], x_ready)

            def compress():
                for kind in range(2):
                    src = proj[:, (KC, VC)[kind], :]
                    win = bass.AP(tensor=src.tensor, offset=src.offset, ap=[list(src.ap[0]), [1, 32], [16, N_CMP]])
                    dve.tensor_copy(xp[kind][:, :, 0:N_CMP], win)
                    pos = sm[:, SM_POS + 32 * kind:SM_POS + 32 * kind + 32]
                    dve.tensor_copy(xp[kind][:, :, N_CMP:32].rearrange("p j o -> p (j o)"), pos).then_inc(cmp_in, 1)
                z, t1 = tmp[0], tmp[1]
                for kind in range(2):
                    c.wait(cmp_mm)
                    for g in range(2):
                        r = slice(g * HD, g * HD + HD)
                        ps = bank[(2, 0)[kind] + g][r, 0:32]
                        link(dve.tensor_copy(cmpb[r, 0:1], ps[:, N_CMP:32]))
                        zz = z[r, 0:N_CMP]
                        link(dve.tensor_scalar(zz, ps[:, 0:N_CMP], cmpb[r, 0:1], None, ALU.add))
                        link(dve.tensor_tensor(t1[r, 0:N_CMP], zz, zz, ALU.mult))
                        link(dve.tensor_scalar(t1[r, 0:N_CMP], t1[r, 0:N_CMP], 0.044715, 1.0, ALU.mult, ALU.add))
                        dve.tensor_tensor(z[r, 64:64 + N_CMP], t1[r, 0:N_CMP], zz, ALU.mult).then_inc(cmp_bias, 1)
                        c.wait(gate_exp)
                        link(dve.tensor_scalar(t1[r, 0:N_CMP], hid[r, kind, 0:N_CMP], 1.0, None, ALU.add))
                        link(dve.reciprocal(t1[r, 64:64 + N_CMP], t1[r, 0:N_CMP]))
                        dve.tensor_tensor(hid[r, kind, 0:N_CMP], t1[r, 64:64 + N_CMP], zz, ALU.mult).then_inc(cmp_hid, 1)
                c.wait(cmp_out)
                for g in range(2):
                    r = slice(g * HD, g * HD + HD)
                    dve.tensor_copy(kc_c[r, 0:N_CMP], bank[6 + g][r, 0:N_CMP])
                    ins = dve.tensor_copy(vc_c[0:N_CMP, r], bank[4 + g][0:N_CMP, r])
                ins.then_inc(cmp_ready, 1)
                c.wait(gate_exp)
                link(dve.tensor_scalar(gate_c[:, :, :], gate_c[:, :, :], 1.0, None, ALU.add))
                link(dve.reciprocal(gate_c[:, :, :], gate_c[:, :, :]))

            c.wait(consts_in, 48)
            for layer in range(DEPTH):
                for j in (1, 5):
                    g = V_RMS + 64 * layer + 8 * j
                    link(dve.tensor_scalar(vec[:, g:g + 8], vec[:, g:g + 8], 0.5, None, ALU.mult))
            split()
            for k in range(DC):
                c.wait(x_hi)
                lo_of(x[:, k, 1, :], h[:, k, :], x[:, k, 0, :], x_ready)

            for layer in range(DEPTH):
                done = 5 if layer == 0 else 1
                for k in range(done):
                    copy_tile(proj[:, k, :])
                with c.loop((N_PROJ - done) // 4, hi_done=4, unit_done=4, **TILES4) as i:
                    for k in range(4):
                        copy_tile(proj[:, i * 4 + (done + k), :])
                c.wait(tab_in, 16)
                rope([proj[:, k, :] for k in (0, 1, 2, KC, KS, KW)], tb1[:, T_COS:T_COS + S], tb1[:, T_SIN:T_SIN + S])
                gla(layer)
                pool_mix(layer)
                compress()
                for k in range(3):
                    attend(jobs_nsa(k), sc1, pt1, otok1)
                    turn_out(x[:, k, 1, :], x[:, k, 0, :])
                with c.loop(2, hi_done=4, unit_done=4, **TILES4) as i:
                    for k in range(4):
                        units(1)
                        b = bank[c.n.get("tile", 0) % 2]
                        hm = h[:, i * 4 + k, :]
                        free(dve.scalar_tensor_tensor(hm, hm, ALPHA, b[:, :], ALU.mult, ALU.add))
                layer_norm(True)
                for half in range(2):
                    with c.loop(4, hi_done=4, unit_done=4, relu_done=4, mid_hi=4, **{"made mid_ready": 4}, **TILES4) as i:
                        for k in range(4):
                            units(1)
                            c.wait(relu_done)
                            b = bank[c.n.get("tile", 0) % 2]
                            free(dve.tensor_tensor(prod[k % 2][:, :], tmp[k % 2][:, :], b[:, :], ALU.mult))
                            c.wait(mid_hi)
                            lo_of(mid[:, i * 4 + k, 1, :], prod[k % 2][:, :], mid[:, i * 4 + k, 0, :], mid_ready)
                    with c.loop(4, hi_done=4, unit_done=4, **TILES2) as i:
                        for k in range(2):
                            units(2)
                            b = bank[c.n.get("tile", 0) % 2]
                            hm = h[:, i * 2 + k, :]
                            free(dve.scalar_tensor_tensor(hm, hm, ALPHA if half == 0 else 1.0, b[:, :], ALU.mult, ALU.add))
                layer_norm(layer == 0)

            def ffn2():
                with c.loop(FF2C // 2, hi_done=4, unit_done=4, mid_hi=2, **{"made mid_ready": 2}, **TILES4) as i:
                    for k in range(2):
                        units(1)
                        g = c.next_tile()
                        units(1)
                        dve.wait_ge(bank_free[g], c.at(f"used{g}"))
                        b = bank[c.n["tile"] % 2]
                        free(dve.tensor_tensor(prod[k][:, :], tmp[k][:, :], b[:, :], ALU.mult))
                        c.wait(mid_hi)
                        lo_of(mid[:, i * 2 + k, 1, :], prod[k][:, :], mid[:, i * 2 + k, 0, :], mid_ready)
                with c.loop(2, hi_done=12, unit_done=12, sq_done=4, **TILES4) as i:
                    for k in range(4):
                        copy_tile_sq(y[:, i * 4 + k, :], 3)

            for layer in range(DEPTH):
                g = V_RMS + 64 * layer
                rms_pre(g)
                ffn2()
                rms_post(g + 8)
                rms_pre(g + 16)
                if layer == 0:
                    c.wait(tab_in, 16)
                    for pair in range(4):
                        for k in range(9):
                            copy_tile(aq[:, k, :])
                        rope([aq[:, k, :] for k in range(6)], tba[:, A_COS:A_COS + S], tba[:, A_SIN:A_SIN + S])
                        for k in range(3):
                            turned_into(av[:, :, k, :], lambda b: b[:, :].rearrange("p (t d) -> p t d", t=QT))
                        attend(jobs_a(), sca, pta, otok)
                        turn_out(ao[:, pair, 1, :], ao[:, pair, 0, :])
                    for n in range(4):
                        units(1)
                        for j in range(2):
                            c.wait(sq_done)
                            dve.tensor_copy(y[:, 2 * n + j, :], bank[n % 2 * 2 + j][:, :]).then_inc(emb_read, 1)
                else:
                    c.wait(tab_in, 16)
                    for c4 in range(2):
                        for k in range(6):
                            copy_tile(bk[:, k, :])
                        rope([bk[:, k, :] for k in (0, 2, 3, 4, 5)], tbb[:, B_COS:B_COS + S], tbb[:, B_SIN:B_SIN + S])
                        turned_into(bv[:, :, :], lambda b: b[:, :].rearrange("p (t d) -> p t d", t=QT))
                        for k in range(4):
                            attend(jobs_b(c4, k), scb, ptb, otokb)
                            turn_out(bo[:, c4 * 4 + k, 1, :], bo[:, c4 * 4 + k, 0, :])
                    with c.loop(2, hi_done=4, unit_done=4, sq_done=4, **TILES4) as i:
                        for k in range(4):
                            copy_tile_sq(y[:, i * 4 + k, :], 1)
                rms_post(g + 24)
                rms_pre(g + 32)
                ffn2()
                rms_post(g + 40)
                for k in range(2):
                    c.wait(p_hi)
                    lo_of(px[:, k, 1, :], pf[:, k, :], px[:, k, 0, :], p_ready)
                rms_pre(g + 48)
                for n in range(2):
                    units(1)
                    for j in range(4):
                        dve.tensor_copy(emb[:, 4 * n + j, :], bank[4 + j][:, :]).then_inc(emb_read, 1)
                for k in range(DC):
                    units(1, last=layer == DEPTH - 1 and k == DC - 1)
                    b = c.next_tile()
                    dve.wait_ge(bank_free[b], c.at(f"used{b}"))
                    dve.tensor_tensor(y[:, k, :], tmp[k % 2][:, :], emb[:, k, :], ALU.mult).then_inc(sig_done, 1)
                c.tick("sq_done", DC)
                rms_post(g + 56)


def tables():
    f = np.float32
    pos = np.arange(S, dtype=f)
    inv = (f(500000.0) ** (-np.arange(8, dtype=f) * f(2.0) / f(16))).astype(f)
    ang = (pos[None, :] * inv[:, None]).astype(f)
    cos, sin = np.ones((P, S), f), np.zeros((P, S), f)
    rot = np.zeros((P, P), f)
    for r in (0, HD):
        for d in range(16):
            cos[r + d], sin[r + d] = np.cos(ang[d % 8]), np.sin(ang[d % 8])
        for d in range(8):
            rot[r + 8 + d, r + d], rot[r + d, r + 8 + d] = -1.0, 1.0
    p = np.arange(P)[:, None]

    def mask(width, first, ok):
        d = np.arange(width)[None, :] - first - p
        return np.where(ok(d), 0.0, BIG_NEG).astype(f)

    tok = np.arange(S)
    icnt = np.concatenate([np.repeat(np.stack([1.0 / np.minimum(tok + 1, w) for w in ws]), HD, 0)
                           for ws in ((2, 4), (8, 16))], 1).astype(f)
    reset = np.broadcast_to((tok % 64 != 0).astype(f), (P, S))
    t_, n_ = np.arange(QT)[None, :, None], np.arange(32)[None, None, :]
    cmp_ = np.where(16 * n_ + 31 <= t_ * P + p[:, :, None], 0.0, BIG_NEG).astype(f).reshape(P, QT * 32)
    i = np.arange(P)[None, :]
    gla = ((p <= i) & (p // 64 == i // 64)).astype(f)
    b64 = (p // HD == i // HD).astype(f) / HD
    t1 = np.concatenate([cos, sin, icnt, reset, mask(4 * P, 3 * P, lambda d: d <= 0), cmp_, gla, b64, rot], 1)
    ta = np.concatenate([cos, sin, rot, mask(3 * P, P, lambda d: abs(d) <= 64),
                         mask(7 * P, 3 * P, lambda d: (abs(d) <= 256) & (d % 4 == 0)),
                         mask(4 * P, 0, lambda d: d % 16 == 0)], 1)
    tb = np.concatenate([cos, sin, rot, mask(3 * P, P, lambda d: abs(d) <= 128)], 1)
    assert t1.shape[1] == T_N and ta.shape[1] == A_N and tb.shape[1] == B_N
    cs = np.stack([np.eye(P, dtype=f), np.full((P, P), 1.0 / D, f)])
    return [np.ascontiguousarray(a, dtype=f) for a in (t1, ta, tb, cs)]


def tiles(w):
    k, m = w.shape
    return w.reshape(k // P, P, m // P, P).transpose(2, 1, 0, 3).reshape(m // P, P, k)


def cut(t, n):
    return t.reshape(t.shape[0], P, n, UNIT).transpose(0, 2, 1, 3).reshape(-1, P, UNIT)


def weight_stream(a):
    units = []
    z = np.zeros
    for l in range(DEPTH):
        w = a["w_in"][l]
        cols = []
        for c in range(3):
            cols += [w[:, c * HD:c * HD + HD], w[:, (3 + c) * HD:(4 + c) * HD]]
        kv = [w[:, 384 + i * P:384 + i * P + P] for i in range(6)]
        cols += [kv[0], kv[1], kv[2], kv[4], kv[3], kv[5]]
        gate, gq, gk, gv, glr, go, pu = (w[:, i:j] for i, j in (
            (1152, 1170), (1170, 1362), (1362, 1554), (1554, 1938), (1938, 1954), (1954, 2338), (2338, 2594)))
        cols += [gv, gq, glr, z((D, 16), w.dtype), gate, z((D, 14), w.dtype), gk, z((D, 64), w.dtype), go, pu]
        units.append(tiles(np.concatenate(cols, 1)))
        wo = a["w_out"][l]
        rows = []
        for c in range(3):
            rows += [wo[c * HD:c * HD + HD], wo[(3 + c) * HD:(4 + c) * HD]]
        units.append(tiles(np.concatenate(rows + [wo[384:]], 0)))
        for half in range(2):
            units.append(tiles(a["w_up"][l][:, half * 2048:half * 2048 + 2048]))
            units.append(cut(tiles(a["w_down"][l][half * 2048:half * 2048 + 2048]), 2))
    for l in range(DEPTH):
        def ffn(i):
            wi = tiles(a["ffn_wi_2"][l, i])
            pairs = np.stack([wi[:FF2C], wi[FF2C:]], 1).reshape(-1, P, UNIT)
            wo = np.concatenate([a["ffn_wo_2"][l, i], z((2 * P, D), wi.dtype)], 0)
            return [pairs, cut(tiles(wo), 3)]
        units += ffn(0)
        if l == 0:
            w = a["a_wqkv_2"][0].reshape(D, 3, 3, 4, P)
            for pair in range(4):
                units.append(tiles(w[:, :, :, pair].reshape(D, 9 * P)))
            units.append(tiles(a["a_wo_2"][0]).reshape(4, 2, P, 512).transpose(0, 2, 1, 3).reshape(4, P, UNIT))
        else:
            w, wo = a["b_wqkv_2"][0], a["b_wo_2"][0]
            rows = []
            for c4 in range(2):
                cols = [w[:, 1024 + c4 * P:1024 + c4 * P + P], w[:, 1280 + c4 * P:1280 + c4 * P + P]]
                for c in range(4):
                    for hd in (8 * c4 + c, 8 * c4 + 4 + c):
                        cols.append(w[:, hd * HD:hd * HD + HD])
                        rows.append(wo[hd * HD:hd * HD + HD])
                units.append(tiles(np.concatenate(cols, 1)))
            units.append(tiles(np.concatenate(rows, 0)))
        units += ffn(1)
        units.append(tiles(a["ple_proj_2"][l]).reshape(2, 4, P, 256).transpose(0, 2, 1, 3).reshape(2, P, UNIT))
        units.append(tiles(a["ple_gate_2"][l]))
    return np.concatenate(units, 0)


def small_weights(a):
    out = []
    for l in range(DEPTH):
        blk = np.zeros((P, SM_W), a["cmp_w1"].dtype)
        for r in (0, HD):
            for kind in range(2):
                w1 = a["cmp_w1"][l, kind].reshape(32, HD, HD).transpose(1, 0, 2).reshape(HD, 2048)
                blk[r:r + HD, SM_W1 + kind * 2048:SM_W1 + kind * 2048 + 2048] = w1
                blk[r:r + HD, SM_POS + kind * 32:SM_POS + kind * 32 + 32] = a["cmp_pos"][l, kind].T
                blk[r:r + HD, SM_W2 + kind * HD:SM_W2 + kind * HD + HD] = a["cmp_w2"][l, kind]
        blk[GLR_ROW:GLR_ROW + 16, SM_G2:SM_G2 + 192] = a["gla_w_gate2"][l]
        for g in range(4):
            blk[g % 2 * HD:g % 2 * HD + HD, SM_PW + g // 2 * HD:SM_PW + g // 2 * HD + HD] = a["pool_w"][l, g]
        out.append(blk)
    return np.stack(out)


def vectors(a):
    v = np.zeros((P, V_N), a["ln1_g"].dtype)

    def put(col, x):
        n = -(-x.size // P)
        for i in range(n):
            part = x[i * P:(i + 1) * P]
            v[:part.size, col + i] = part

    for l in range(DEPTH):
        for j, name in enumerate(("ln1_g", "ln1_b", "ln2_g", "ln2_b")):
            put(V_LN + 32 * l + 8 * j, a[name][l])
        for j in range(8):
            put(V_RMS + 64 * l + 8 * j, a["norm_g_2"][l, j])
        put(V_BG + 2 * l, a["gla_b_gate"][l])
        put(V_NG + 3 * l, a["gla_norm_g"][l])
        put(V_PS + 2 * l, a["pool_scale"][l])
    v[:, V_SINK:V_SINK + 16] = a["b_sink_2"][0][None, :]
    return v


def kernel(**inputs):
    import concourse.bacc as _bacc
    from concourse.bass_utils import run_bass_kernel_spmd as _run

    a = {k: np.asarray(v) for k, v in inputs.items()}
    t1, ta, tb, cs = tables()
    arrays = {
        "stream": weight_stream(a),
        "x_t": np.ascontiguousarray(a["x"][0].T),
        "p_t": np.ascontiguousarray(a["p_2"][:, 0].transpose(0, 2, 1)),
        "small": small_weights(a),
        "vecs": vectors(a),
        "tab1": t1, "tab_a": ta, "tab_b": tb, "consts": cs,
    }
    nc = _bacc.Bacc("TRN2", target_bir_lowering=False, num_devices=1)
    args = [nc.dram_tensor(n, v.shape, F32, kind="ExternalInput").ap() for n, v in arrays.items()]
    out = nc.dram_tensor("out_t", (DC, P, S), F32, kind="ExternalOutput").ap()
    build(nc, *args, out)
    r = _run(nc, [arrays], core_ids=[0])
    return np.ascontiguousarray(r.results[0]["out_t"].reshape(D, S).T).reshape(1, S, D)
```

```python
from contextlib import ExitStack, contextmanager

import numpy as np
import concourse.bass as bass
from concourse import mybir

F32 = mybir.dt.float32
F32R = mybir.dt.float32r
ALU = mybir.AluOpType
ACT = mybir.ActivationFunctionType
AX = mybir.AxisListType

P = 128
S = 512
D = 1024
DC = D // P
QT = S // P
UNIT = 1024
DEPTH = 2
ALPHA = (2 * DEPTH) ** 0.25
LN_EPS, RMS_EPS = 1e-5, 1e-6
FF2C = 2816 // P
HD = 64
N_CMP = 31
BIG_NEG = -1.0e30
FLOOR = -1.0e20

Q0, KC, VC, KS, KW, VS, VW, GV, GQ, GQX, GK, GKX, GO, PU = 0, 3, 4, 5, 6, 7, 8, 9, 12, 13, 14, 15, 16, 19
N_PROJ = 21
GLR_ROW, GATE_ROW = 64, 96

SM_W1, SM_POS, SM_W2, SM_G2, SM_PW = 0, 4096, 4160, 4288, 4480
SM_W = 4608
V_LN = 0
V_RMS = 64
V_BG, V_NG, V_PS, V_SINK = 192, 196, 202, 206
V_N = 222
T_COS, T_SIN, T_ICNT, T_RESET, T_CAUS, T_CMP, T_GLA, T_B64, T_ROT = (
    0, 512, 1024, 2048, 2560, 3072, 3200, 3328, 3456)
T_N = 3584
A_COS, A_SIN, A_ROT, A_M0, A_M1 = 0, 512, 1024, 1152, 3200
A_N = 3456
B_COS, B_SIN, B_ROT, B_M = 0, 512, 1024, 1152
B_N = 1536


ORDER = (GQX, GK, GKX, GQ, KC, GV, GV + 1, GV + 2, KS, KW, Q0, Q0 + 1, Q0 + 2, PU, PU + 1,
         GO, GO + 1, GO + 2, VS, VW, VC)
ROPED = {5: KC, 9: KS, 11: Q0, 12: Q0 + 1, 13: Q0 + 2, 14: KW}
TURNED = {7: GV, 8: GV + 1, 9: GV + 2, 10: GK, 11: GKX, 18: GQX, 19: VS, 20: VW}

TILES4 = dict(tile=4, used0=2, used1=2)
TILES2 = dict(tile=2, used0=1, used1=1)


class Count:

    def __init__(self, eng):
        self.eng, self.n, self.loops = eng, {}, []

    def at(self, name, back=0, div=1, mult=1):
        v = (self.n.get(name, 0) // div - back) * mult
        for i, per in self.loops:
            k = per.get(name, 0) // div * mult
            if k:
                v = i * k + v
        return v

    def tick(self, name, k=1):
        self.n[name] = self.n.get(name, 0) + k

    def next_tile(self):
        b = self.n.get("tile", 0) % 2
        self.tick("tile")
        self.tick(f"used{b}")
        return b

    def skip_tiles(self, n):
        for _ in range(n):
            self.next_tile()

    def wait(self, sem, k=1):
        self.tick(sem.name, k)
        self.eng.wait_ge(sem, self.at(sem.name))

    @contextmanager
    def loop(self, rounds, **per):
        start = dict(self.n)
        with self.eng.Fori(0, rounds) as i:
            self.loops.append((i, per))
            yield i
            self.loops.pop()
        did = {k: v - start.get(k, 0) for k, v in self.n.items() if v != start.get(k, 0)}
        assert did == per, f"one round adds {did}"
        for k, v in per.items():
            self.n[k] += v * (rounds - 1)


def build(nc, stream, x_t, p_t, small, vecs, tab1, tab_a, tab_b, consts, out):
    n_units = stream.shape[0]
    with ExitStack() as ctx:
        place = [16512]

        def at(name, shape, dt=F32, offset=None):
            size = int(np.prod(shape[1:])) * 4
            if offset is None:
                offset = place[0]
                place[0] += (size + 31) // 32 * 32
            return nc.alloc_sbuf_tensor_at(name, shape, dt, offset=offset)

        def sem(name):
            s = ctx.enter_context(nc.semaphore(name))
            return s

        h = at("h", [P, DC, S])
        x_at = place[0]
        x = at("x", [P, DC, 2, S], F32R)
        y_at = place[0]
        y = at("y", [P, DC, S])
        px = at("px", [P, 2, 2, S], F32R, offset=x_at + 6 * 2 * S * 4)
        raw = [at(f"raw{i}", [P, UNIT]) for i in range(4)]
        wh = [at(f"wh{i}", [P, UNIT], F32R) for i in range(2)]
        wl = [at(f"wl{i}", [P, UNIT], F32R) for i in range(2)]
        pf = at("pf", [P, 2, S], offset=place[0])
        sq = [at(f"sq{i}", [P, S]) for i in range(2)]
        tmp = [at(f"tmp{i}", [P, S]) for i in range(2)]
        prod = [at(f"prod{i}", [P, S]) for i in range(2)]
        acc = at("acc", [P, S])
        rs = at("rs", [P, S])
        rs_in = at("rs_in", [P, S])
        ident = at("ident", [P, P])
        ones = at("ones", [P, P])
        vec = at("vec", [P, V_N])
        mix_at = place[0]
        mid = at("mid", [P, FF2C, 2, S], F32R)
        assert place[0] <= 229368, place[0]

        o = mix_at
        proj = at("proj", [P, N_PROJ, S], offset=o); o += N_PROJ * S * 4
        sm = at("sm", [P, SM_W], offset=o); o += SM_W * 4
        tb1 = at("tb1", [P, T_N], offset=o); o += T_N * 4
        vtok = at("vtok", [P, QT, 2, P], offset=o); o += QT * 2 * P * 4
        s1_at = o
        assert s1_at + 1056 * 4 <= mix_at + FF2C * 2 * S * 4, (s1_at - mix_at)
        gt = [at(f"gt{i}", [P, 2, S], offset=a_)
              for i, a_ in enumerate((y_at, s1_at, y_at + 4096))]
        at_gla = at("at_gla", [P, QT, 6, P], offset=y_at)
        st_gla = at("st_gla", [P, 8, 2, HD], offset=y_at + QT * 6 * P * 4)
        pt1 = [at(f"pt1_{i}", [P, 9 * P], offset=y_at + i * 9 * P * 4) for i in range(2)]
        sc1 = [at(f"sc1_{i}", [P, 1056], offset=a_)
               for i, a_ in enumerate((y_at + 18 * P * 4, s1_at, mix_at + GQ * S * 4))]
        win = at("win", [P, S], offset=s1_at + 1056 * 4 + 320)
        xp = [at(f"xp{i}", [P, 32, 32], offset=x_at + i * 4096) for i in range(2)]
        kc_c = at("kc_c", [P, 32], offset=x_at + 8192)
        vc_c = at("vc_c", [32, P], offset=x_at + 8320)
        hid = at("hid", [P, 2, 32], offset=x_at + 8832)
        gate_c = at("gate_c", [P, QT, 18], offset=s1_at + 1056 * 4)
        cmpb = at("cmpb", [P, 2], offset=s1_at + 1056 * 4 + 288)
        otok1 = [at(f"otok1_{i}", [P, QT, P], offset=a_)
                 for i, a_ in enumerate((s1_at + 1056 * 4 + 320, y_at + 18 * P * 4 + 1056 * 4))]
        assert s1_at + 1056 * 4 + 320 + QT * P * 4 <= mix_at + FF2C * 2 * S * 4
        o = mix_at
        aq = at("aq", [P, 9, S], offset=o); o += 9 * S * 4
        av = at("av", [P, QT, 3, P], offset=o); o += QT * 3 * P * 4
        tba = at("tba", [P, A_N], offset=o); o += A_N * 4
        sca = [at(f"sca{i}", [P, 6 * P], offset=o + i * 6 * P * 4) for i in range(3)]; o += 18 * P * 4
        pta = [at(f"pta{i}", [P, 6 * P], offset=o + i * 6 * P * 4) for i in range(2)]; o += 12 * P * 4
        otok = [at(f"otok{i}", [P, QT, P], offset=o + i * QT * P * 4) for i in range(2)]; o += 2 * QT * P * 4
        ao = at("ao", [P, 4, 2, S], F32R, offset=o); o += 4 * 2 * S * 4
        assert o <= mix_at + FF2C * 2 * S * 4
        o = mix_at
        bk = at("bk", [P, 6, S], offset=o); o += 6 * S * 4
        bv = at("bv", [P, QT, P], offset=o); o += QT * P * 4
        tbb = at("tbb", [P, B_N], offset=o); o += B_N * 4
        scb = [at(f"scb{i}", [P, 3 * P], offset=o + i * 3 * P * 4) for i in range(3)]; o += 9 * P * 4
        ptb = [at(f"ptb{i}", [P, 3 * P], offset=o + i * 3 * P * 4) for i in range(2)]; o += 6 * P * 4
        otokb = [at(f"otokb{i}", [P, QT, P], offset=o + i * QT * P * 4) for i in range(2)]; o += 2 * QT * P * 4
        bo = at("bo", [P, DC, 2, S], F32R, offset=o); o += DC * 2 * S * 4
        assert o <= mix_at + FF2C * 2 * S * 4
        emb = at("emb", [P, DC, S], offset=mix_at)
        mx = at("mx", [P, 2, QT, 4])
        negm = at("negm", [P, 2, 3, QT])
        den = at("den", [P, 2, 3, QT])
        rden = at("rden", [P, 2, 3, QT])
        esink = at("esink", [P, 2, QT])
        nsink = at("nsink", [P, 16])
        eps = at("eps", [P, 2])
        assert place[0] <= 229368, place[0]

        bank = [ctx.enter_context(nc.psum_tensor(f"bank{i}", [P, S], F32)) for i in range(8)]

        raw_in = [sem(f"raw_in{i}") for i in range(4)]
        hi_done = sem("hi_done")
        split_done = sem("split_done")
        unit_done = sem("unit_done")
        bank_free = [sem("bank_free0"), sem("bank_free1")]
        relu_done = sem("relu_done")
        mid_hi, mid_ready = sem("mid_hi"), sem("mid_ready")
        sq_done, acc_done = sem("sq_done"), sem("acc_done")
        z_added = sem("z_added")
        gate_made, pair_made = sem("gate_made"), sem("pair_made")
        stat_done = sem("stat_done")
        centred, sq_made, sq_used = sem("centred"), sem("sq_made"), sem("sq_used")
        rstd_ready, normed, affine = sem("rstd_ready"), sem("normed"), sem("affine")
        x_hi, x_ready = sem("x_hi"), sem("x_ready")
        part_made, h_ready = sem("part_made"), sem("h_ready")
        consts_in = sem("consts_in")
        h_in = [sem(f"h_in{i}") for i in range(4)]
        tab_in, sm_in, p_in = sem("tab_in"), sem("sm_in"), sem("p_in")
        area_free = sem("area_free")
        dve_step, act_step, pool_step = sem("dve_step"), sem("act_step"), sem("pool_step")
        rot_done, rope_used, rope_done = sem("rot_done"), sem("rope_used"), sem("rope_done")
        turned, turn_read = sem("turned"), sem("turn_read")
        z_done, gk_act, gk_done = sem("z_done"), sem("gk_act"), sem("gk_done")
        gla_exp, gla_in, gla_kend = sem("gla_exp"), sem("gla_in"), sem("gla_kend")
        ds_done, st_done = sem("ds_done"), sem("st_done")
        am_done, am_read = sem("am_done"), sem("am_read")
        go_done, go_copied, go_sq, go_stat = sem("go_done"), sem("go_copied"), sem("go_sq"), sem("go_stat")
        go_rstd, go_silu, go_out = sem("go_rstd"), sem("go_silu"), sem("go_out")
        mx_hi, mx_ready = sem("mx_hi"), sem("mx_ready")
        pooled, pool_mm = sem("pooled"), sem("pool_mm")
        cmp_in, cmp_mm, cmp_bias, cmp_hid, cmp_out, cmp_ready = (
            sem("cmp_in"), sem("cmp_mm"), sem("cmp_bias"), sem("cmp_hid"), sem("cmp_out"), sem("cmp_ready"))
        gate_exp, gate_in = sem("gate_exp"), sem("gate_in")
        scored, score_read = sem("scored"), sem("score_read")
        max_ready, exp_done = sem("max_ready"), sem("exp_done")
        blk_turned = sem("blk_turned")
        blk_act, blk_dve = sem("blk_act"), sem("blk_dve")
        pv_done, o_done, o_read = sem("pv_done"), sem("o_done"), sem("o_read")
        ot_turned, ot_hi, ot_ready = sem("ot_turned"), sem("ot_hi"), sem("ot_ready")
        sink_exp = sem("sink_exp")
        p_hi, p_ready, emb_read = sem("p_hi"), sem("p_ready"), sem("emb_read")
        sig_done = sem("sig_done")
        out_done = sem("out_done")

        def gv_t(rows, t, head):
            return proj[rows, GV + head // 2, t * P + head % 2 * HD:t * P + head % 2 * HD + HD]

        def jobs_nsa():
            for c in range(3):
                for g in range(2):
                    r = slice(g * HD, g * HD + HD)
                    for t in range(QT):
                        n = (t + 1) * P
                        q = proj[r, Q0 + c, t * P:t * P + P]
                        caus = tb1[:, T_CAUS + (QT - 1 - t) * P:T_CAUS + QT * P]
                        yield dict(kind="nsa", t=t, g=g, head=g * 3 + c, segs=[
                            ([(q, kc_c[r, 0:N_CMP])], tb1[:, T_CMP + t * 32:T_CMP + t * 32 + N_CMP],
                             [vc_c[0:N_CMP, r]], 0),
                            ([(q, proj[r, KS, 0:n])], caus, [vtok[:, k, 0, r] for k in range(t + 1)], 1),
                            ([(q, proj[r, KW, 0:n])], caus, [vtok[:, k, 1, r] for k in range(t + 1)], 2)])

        def jobs_a():
            for g in range(2):
                r = slice(g * HD, g * HD + HD)
                for t in range(QT):
                    ts = slice(t * P, t * P + P)
                    yield dict(kind="a", t=t, g=g, head=g, segs=[
                        ([(aq[r, 0, ts], aq[r, 3, :])], tba[:, A_M0 + t * S:A_M0 + t * S + S],
                         [av[:, k, 0, r] for k in range(QT)], 0),
                        ([(aq[r, 1, ts], aq[r, 4, ts]), (aq[r, 2, ts], aq[r, 5, ts])], tba[:, A_M1:A_M1 + 2 * P],
                         [av[:, t, 1, r], av[:, t, 2, r]], 0)])

        def jobs_b(c4):
            for c in range(4):
                for g in range(2):
                    r = slice(g * HD, g * HD + HD)
                    for t in range(QT):
                        lo, hi = max(t - 1, 0), min(t + 2, QT)
                        yield dict(kind="b", t=t, g=g, head=8 * c4 + 4 * g + c, segs=[
                            ([(bk[r, 2 + c, t * P:t * P + P], bk[r, 0, lo * P:hi * P])],
                             tbb[:, B_M + (lo - t + 1) * P:B_M + (hi - t + 1) * P],
                             [bv[:, k, r] for k in range(lo, hi)], 0)])

        def width(seg):
            return sum(k.shape[-1] for _, k in seg[0])

        def spans(job):
            off, out_ = 0, []
            for seg in job["segs"]:
                w = width(seg)
                out_.append((off, w, [(off + j * P, min(P, w - j * P)) for j in range(len(seg[2]))]))
                off += max(w, 32)
            return out_

        def blocks(job):
            b = [(si, j, o_, w) for si, (_, _, tiles_) in enumerate(spans(job)) for j, (o_, w) in enumerate(tiles_)]
            return [b[i:i + 4] for i in range(0, len(b), 4)]

        def pair_done(j):
            return j and j % 8 == 0

        def outs_a(pair):
            view = [ao[:, pair, e, :].rearrange("p (j c r) -> p j c r", c=4, r=4) for e in range(2)]
            return (*view, True)

        def outs_b(c4):
            return [(bo[:, c4 * 4 + k, 0, :], bo[:, c4 * 4 + k, 1, :], False) for k in range(4)]

        def in_order(out_, src):
            return src.rearrange("p (r c j) -> p j c r", r=4, c=4) if out_[2] else src

        def o_bank(job, head, s):
            return (7, 0, 1)[s] if job["kind"] == "nsa" else (7, 0)[head % 2]

        block = ctx.enter_context(nc.Block())

        @block.sync
        def _(sp):
            c = Count(sp)

            def load(k, wait=True):
                if wait:
                    sp.wait_ge(split_done, c.at("unit", back=3))
                sp.dma_start(raw[k % 4][:, :], stream[c.at("unit"), :, :]).then_inc(raw_in[k % 4], 16)
                c.tick("unit")

            for k in range(4):
                load(k, False)
            rounds = (n_units - 4) // 4
            with c.loop(rounds, unit=4):
                for k in range(4):
                    load(k)
            for k in range((n_units - 4) % 4):
                load(k)
            for k in range(DC):
                sp.wait_ge(h_ready, 7 * DC + k + 1)
                sp.dma_start(out[k], h[:, k, :]).then_inc(out_done, 16)
            sp.wait_ge(out_done, 16 * DC)

        @block.gpsimd
        def _(pool):
            c = Count(pool)
            pool.dma_start(ident[:, :], consts[0]).then_inc(consts_in, 16)
            pool.dma_start(ones[:, :], consts[1]).then_inc(consts_in, 16)
            pool.dma_start(vec[:, :], vecs).then_inc(consts_in, 16)
            pool.memset(eps[:, 0:1], LN_EPS).then_inc(pool_step, 1)
            pool.memset(eps[:, 1:2], RMS_EPS).then_inc(pool_step, 1)
            c.tick("pool_step", 2)

            def acc_read():
                k = c.n.get("stats", 0)
                if k:
                    pool.wait_ge(stat_done, k)
                c.tick("stats")

            def square_sums():
                acc_read()
                pool.memset(acc[:, :], 0.0).then_inc(acc_done, 1)
                c.wait(acc_done)
                for m in range(DC - 1):
                    c.wait(sq_done)
                    pool.tensor_tensor(acc[:, :], acc[:, :], sq[m % 2][:, :], ALU.add).then_inc(acc_done, 1)
                    c.wait(acc_done)
                c.tick("sq_done")

            def z_sums():
                acc_read()
                for m in range(DC - 1):
                    b = c.next_tile()
                    if m:
                        pool.wait_ge(bank_free[b], c.at(f"used{b}"))
                        if m == 1:
                            pool.wait_ge(bank_free[1 - b], c.at(f"used{1 - b}"))
                        pool.tensor_tensor(acc[:, :], h[:, 0, :] if m == 1 else acc[:, :], h[:, m, :],
                                           ALU.add).then_inc(z_added, 1)
                        c.wait(z_added)
                c.next_tile()

            def link(ins):
                ins.then_inc(pool_step, 1)
                c.wait(pool_step)

            def window_sums():
                a, b = acc[:, :], rs_in[:, :]
                for k in range(2):
                    t = c.next_tile()
                    pool.wait_ge(bank_free[t], c.at(f"used{t}"))
                    if k == 0:
                        c.wait(tab_in, 16)
                    src = proj[:, PU + k, :]
                    cur, nxt, w, res = src, a, 1, {}
                    for _ in range(2 + 2 * k):
                        pool.tensor_copy(nxt[:, 0:w], cur[:, 0:w])
                        link(pool.tensor_tensor(nxt[:, w:S], cur[:, w:S], cur[:, 0:S - w], ALU.add))
                        w *= 2
                        res[w] = nxt
                        cur, nxt = nxt, b if nxt is a else a
                    for e in range(2):
                        r = slice(e * HD, e * HD + HD)
                        ins = pool.tensor_tensor(win[r, :], res[(2, 4, 8, 16)[2 * k + e]][r, :],
                                                 tb1[r, T_ICNT + k * S:T_ICNT + k * S + S], ALU.mult)
                    link(ins)
                    pool.tensor_tensor(src, win[:, :], src, ALU.subtract).then_inc(pooled, 1)
                    c.wait(pooled)

            def add_parts():
                for m in range(DC):
                    c.wait(part_made)
                    pool.tensor_tensor(h[:, m, :], h[:, m, :], prod[m % 2][:, :], ALU.add).then_inc(h_ready, 1)

            def after(units_):
                pool.wait_ge(unit_done, units_)

            ffn, ple = 2 * FF2C + 3 * DC, 2 + DC
            u = 0
            for layer in range(DEPTH):
                if layer:
                    after(u)
                pool.dma_start(sm[:, :], small[layer]).then_inc(sm_in, 16)
                pool.dma_start(tb1[:, :], tab1).then_inc(tab_in, 16)
                u += N_PROJ + DC + 8 * DC
                c.skip_tiles(ORDER.index(PU))
                window_sums()
                c.skip_tiles(N_PROJ - ORDER.index(PU) - 2)
                z_sums()
                c.skip_tiles(16 + DC + 16)
                z_sums()
            for layer in range(DEPTH):
                square_sums()
                add_parts()
                u += ffn
                after(u)
                if layer == 0:
                    pool.dma_start(tba[:, :], tab_a).then_inc(tab_in, 16)
                else:
                    pool.dma_start(tbb[:, :], tab_b).then_inc(tab_in, 16)
                square_sums()
                add_parts()
                u += (40, 20)[layer]
                pool.wait_ge(sq_used, DC * (2 * DEPTH + 4 * layer + 3))
                pool.dma_start(pf[:, :, :], p_t[layer].rearrange("(c p) t -> p c t", p=P)).then_inc(p_in, 16)
                square_sums()
                add_parts()
                u += ffn + ple
                square_sums()
                add_parts()
            assert u == n_units, (u, n_units)

        @block.tensor
        def _(pe):
            c = Count(pe)

            def unit(bk_, cols, src, chunks, start, stop, last=True, ready=None, also=None):
                u = c.n.get("unit", 0) % 2
                for j, (col, kc) in enumerate(zip(cols, chunks)):
                    if ready is not None:
                        c.wait(ready)
                    if also is not None and j:
                        also(j - 1)
                    hi = wh[u][:, col:col + P]
                    lo = wl[u][:, col:col + P]
                    pe.matmul(bk_[:, :], hi, src[:, kc, 0, :], start=start and j == 0, stop=False)
                    pe.matmul(bk_[:, :], hi, src[:, kc, 1, :], start=False, stop=False)
                    mm = pe.matmul(bk_[:, :], lo, src[:, kc, 0, :], start=False, stop=stop and j == len(cols) - 1)
                if last:
                    mm.then_inc(unit_done, 1)
                    c.tick("unit")
                if also is not None:
                    also(len(cols) - 1)

            def tile(src, spread=(range(8),), ready=None, also=None):
                t = c.next_tile()
                if c.n[f"used{t}"] > 1:
                    pe.wait_ge(bank_free[t], c.at(f"used{t}", back=1))
                for n, chunks in enumerate(spread):
                    pe.wait_ge(split_done, c.at("unit") + 1)
                    unit(bank[t], [j * P for j in range(len(chunks))], src, chunks, n == 0, n == len(spread) - 1,
                         ready=ready, also=also)

            def tiles_of(n, per, src, spread=(range(8),), ready=None, also=None):
                for k in range(per):
                    tile(src, spread, *((ready, also) if k == 0 else ()))
                with c.loop(n // per - 1, unit=per * len(spread), **(TILES4 if per == 4 else TILES2)):
                    for k in range(per):
                        tile(src, spread)

            def read_all():
                for t in range(2):
                    pe.wait_ge(bank_free[t], c.at(f"used{t}"))
                if c.n.get("pairs", 0):
                    pe.wait_ge(ot_ready, c.n["pairs"])

            def stat(added, n, last, made=None):
                c.wait(added, n)
                pe.matmul(bank[2][:, :], ones[:, :], acc[:, :], start=True, stop=False)
                if made is None:
                    read_all()
                else:
                    c.wait(made, DC)
                pe.matmul(bank[2][:, :], ones[:, :], last, start=False, stop=True).then_inc(stat_done, 1)

            def stat_z():
                stat(z_added, DC - 2, h[:, DC - 1, :])

            def stat_sq():
                stat(acc_done, DC, sq[1][:, :], sq_done)

            def square_sum(k):
                c.wait(sq_made)
                pe.matmul(bank[3][:, :], ones[:, :], sq[k % 2][:, :], start=k == 0,
                          stop=k == DC - 1).then_inc(sq_used, 1)

            def stat_chunks():
                for k in range(DC):
                    square_sum(k)

            def rope(ap, rot, waited=False, banks=(2, 3)):
                if not waited:
                    b = c.n["tile"] % 2
                    pe.wait_ge(bank_free[b], c.at(f"used{b}"))
                n = len(banks)
                if c.n.get("rope", 0) >= n:
                    pe.wait_ge(rope_used, c.at("rope", back=n - 1))
                pe.matmul(bank[banks[c.n.get("rope", 0) % n]][:, :], rot, ap, start=True, stop=True).then_inc(rot_done, 1)
                c.tick("rope")

            def turn(groups, banks=(4, 5)):
                for g in groups:
                    k, n = c.n.get("turn", 0), len(banks)
                    if k >= n:
                        pe.wait_ge(turn_read, c.at("turn", back=n - 1))
                    for i, (dst, src) in enumerate(g):
                        mm = pe.transpose(dst(bank[banks[k % n]]), src, ident[:src.shape[0], :src.shape[0]])
                    mm.then_inc(turned, 1)
                    c.tick("turn")

            def attend(jobs, sc, pt, ot):
                jobs = list(jobs)

                def scores(j):
                    for si, seg in enumerate(jobs[j]["segs"]):
                        n = c.n.get("scored", 0)
                        key = f"bank_seg{si}"
                        if c.n.get(key, 0):
                            pe.wait_ge(score_read, c.n[key])
                        at_ = 0
                        for q, k in seg[0]:
                            w = k.shape[-1]
                            mm = pe.matmul(bank[2 + si][:, at_:at_ + w], q, k, start=True, stop=True, skip_group_check=True)
                            at_ += w
                        mm.then_inc(scored, 1)
                        c.tick("scored")
                        c.n[key] = n + 1

                def bank_of_group():
                    b = c.n.get("blk", 0) % 2
                    if c.n.get(f"blk{b}", 0):
                        pe.wait_ge((blk_act, blk_dve)[b], c.n[f"blk{b}"])
                    c.tick("blk")
                    c.tick(f"blk{b}")
                    return bank[5 + b]

                def turns(j):
                    job = jobs[j]
                    c.wait(exp_done, len({seg[3] for seg in job["segs"]}))
                    for grp in blocks(job):
                        dst = bank_of_group()
                        for i, (si, t_, off, w) in enumerate(grp):
                            mm = pe.transpose(dst[0:w, i * P:i * P + P], sc[j % 3][:, off:off + w], ident[:, :])
                        mm.then_inc(blk_turned, 1)
                    return c.n.get("blk0", 0), c.n.get("blk1", 0)

                def values(j, copied):
                    job = jobs[j]
                    pe.wait_ge(blk_act, copied[0])
                    if copied[1]:
                        pe.wait_ge(blk_dve, copied[1])
                    n = c.n.get("o", 0)
                    hd_, depth = n // 4, 1 if job["kind"] == "nsa" else 2
                    if job["t"] == 0 and hd_ >= depth:
                        pe.wait_ge(o_read, hd_ + 1 - depth)
                    flat = [x_ for g in blocks(job) for x_ in g]
                    for s in sorted({seg[3] for seg in job["segs"]}):
                        mine = [(p_, f) for p_, f in enumerate(flat) if job["segs"][f[0]][3] == s]
                        dst = bank[o_bank(job, hd_, s)]
                        for q_, (p_, (si, t_, off, w)) in enumerate(mine):
                            mm = pe.matmul(dst[:, job["t"] * HD:job["t"] * HD + HD],
                                           pt[j % 2][0:w, p_ * P:p_ * P + P], job["segs"][si][2][t_],
                                           start=q_ == 0, stop=q_ == len(mine) - 1, skip_group_check=True)
                    mm.then_inc(o_done, 1)
                    c.tick("o")

                def turn_out(k):
                    pe.wait_ge(o_read, c.n["o"] // 8 * 2)
                    dst = bank_of_group()
                    for t in range(QT):
                        mm = pe.transpose(dst[:, t * P:t * P + P], ot[k % 2][:, t, :], ident[:, :])
                    mm.then_inc(blk_turned, 1)

                scores(0)
                scores(1)
                copied = {0: turns(0)}
                n_jobs = len(jobs)
                for j in range(n_jobs):
                    if j + 2 < n_jobs:
                        scores(j + 2)
                    if j + 1 < n_jobs:
                        copied[j + 1] = turns(j + 1)
                    values(j, copied[j])
                    if pair_done(j):
                        turn_out(j // 8 - 1)
                turn_out(n_jobs // 8 - 1)
                c.tick("pairs", n_jobs // 8)

            def ds():
                for n in range(8):
                    t, half = n // 2, n % 2
                    r = slice(half * 64, half * 64 + 64)
                    for hh in range(6):
                        gi, q = hh // 4, hh % 4
                        mm = pe.matmul(bank[(2, 3, 6, 7)[half * 2 + gi]][q * 32:q * 32 + 32, n // 2 * HD:n // 2 * HD + HD],
                                       gt[2][r, :, :].rearrange("p a s -> p (a s)")[:, t * 192 + hh * 32:t * 192 + hh * 32 + 32],
                                       gv_t(r, t, hh), start=True, stop=True, skip_group_check=True)
                mm.then_inc(ds_done, 1)

            def inside(t):
                ts = slice(t * P, t * P + P)
                for hh in range(6):
                    r = slice(hh % 4 * 32, hh % 4 * 32 + 32)
                    mm = pe.matmul(bank[(2, 3, 6, 7)[hh % 4]][:, hh // 4 * P:hh // 4 * P + P],
                                   gt[1][r, hh // 4, ts], proj[r, (GQ, GQX)[hh // 4], ts],
                                   start=True, stop=True, skip_group_check=True)
                mm.then_inc(am_done, 1)

            def gla_out(cc):
                for e in range(2):
                    hh = 2 * cc + e
                    r = slice(hh % 4 * 32, hh % 4 * 32 + 32)
                    for t in range(QT):
                        dst = bank[2 + e][e * HD:e * HD + HD, :]
                        pe.matmul(dst[:, t * P:t * P + P], gv_t(slice(0, P), t, hh), at_gla[:, t, hh, :],
                                  start=True, stop=False, skip_group_check=True)
                        for n in (2 * t, 2 * t + 1):
                            mm = pe.matmul(dst[:, n * 64:n * 64 + 64], st_gla[r, n, hh // 4, :],
                                           proj[r, (GQ, GQX)[hh // 4], n * 64:n * 64 + 64],
                                           start=False, stop=n % 2 == 1, skip_group_check=True)
                mm.then_inc(go_done, 1)

            def prepare(k):
                b = c.n["tile"] % 2
                pe.wait_ge(bank_free[b], c.at(f"used{b}"))
                if k == 2:
                    c.wait(sm_in, 16)
                    for i, (a, b) in enumerate(((0, 128), (128, 192))):
                        pe.matmul(bank[6 + i][0:b - a, :], sm[GLR_ROW:GLR_ROW + 16, SM_G2 + a:SM_G2 + b],
                                  proj[GLR_ROW:GLR_ROW + 16, GQX, :], start=True, stop=True).then_inc(z_done, 1)
                if k == 12:
                    pe.wait_ge(turn_read, c.n["turn"])
                    ds()
                if k == 13:
                    c.wait(st_done)
                if k == 17:
                    c.wait(am_read)
                if 13 <= k < 17:
                    if k > 13:
                        c.wait(am_read)
                    inside(k - 13)
                if 18 <= k:
                    c.wait(go_sq)
                    pe.matmul(bank[6][:, :], tb1[:, T_B64:T_B64 + P], sq[0][:, :], start=True, stop=True).then_inc(go_stat, 1)
                if 17 <= k < 20:
                    if k > 17:
                        c.wait(go_copied)
                    gla_out(k - 17)
                if k in ROPED:
                    if k == 5:
                        c.wait(tab_in, 16)
                    rope(proj[:, ROPED[k], :], tb1[:, T_ROT:T_ROT + P], True, (5,))
                if k in TURNED:
                    ch = TURNED[k]
                    if ch == GK:
                        c.wait(gla_kend)
                    w = 64 if ch == GKX else P
                    turn([[(lambda b, i=i: b[:, i * w:i * w + w], proj[0:w, ch, i * P:i * P + P]) for i in range(QT)]], (4,))

            def pool_mix():
                for k in range(2):
                    c.wait(pooled)
                    for e in range(2):
                        r = slice(e * HD, e * HD + HD)
                        mm = pe.matmul(bank[4 + 2 * k + e][r, :], sm[r, SM_PW + k * HD:SM_PW + k * HD + HD], proj[r, PU + k, :],
                                       start=True, stop=True)
                    mm.then_inc(pool_mm, 1)

            def compress():
                for kind in range(2):
                    c.wait(cmp_in)
                    for g in range(2):
                        r = slice(g * HD, g * HD + HD)
                        for j in range(32):
                            mm = pe.matmul(bank[(2, 0)[kind] + g][r, 0:32], sm[r, SM_W1 + kind * 2048 + j * HD:SM_W1 + kind * 2048 + j * HD + HD],
                                           xp[kind][r, j, :], start=j == 0, stop=j == 31, skip_group_check=True)
                    mm.then_inc(cmp_mm, 1)
                c.wait(cmp_hid, 4)
                c.wait(mx_hi, 5)
                for g in range(2):
                    r = slice(g * HD, g * HD + HD)
                    pe.matmul(bank[6 + g][r, 0:N_CMP], sm[r, SM_W2:SM_W2 + HD], hid[r, 0, 0:N_CMP], start=True, stop=True, skip_group_check=True)
                    mm = pe.matmul(bank[4 + g][0:N_CMP, r], hid[r, 1, 0:N_CMP], sm[r, SM_W2 + HD:SM_W2 + 2 * HD], start=True, stop=True, skip_group_check=True)
                mm.then_inc(cmp_out, 1)
                c.wait(cmp_ready)

            for layer in range(DEPTH):
                tile(x, ready=x_ready)
                if layer == 0:
                    c.wait(consts_in, 48)
                for k in range(1, N_PROJ):
                    tile(x)
                    prepare(k)
                c.wait(go_copied)
                pe.wait_ge(turn_read, c.n["turn"])
                read_all()
                pool_mix()
                compress()
                attend(jobs_nsa(), sc1, pt1, otok1)
                c.wait(x_ready, 5)
                read_all()
                with c.loop(2, unit=4, **TILES4):
                    for k in range(4):
                        tile(x)
                stat_z()
                stat_chunks()
                for half in range(2):
                    tiles_of(16, 4, x, ready=None if half else x_ready)
                    tiles_of(8, 2, mid, (range(0, 8), range(8, 16)), ready=mid_ready)
                stat_z()
                stat_chunks()

            def ffn2():
                tiles_of(2 * FF2C, 4, x, ready=x_ready, also=square_sum)
                tiles_of(8, 2, mid, (range(0, 8), range(8, 16), range(16, FF2C)), ready=mid_ready)

            for layer in range(DEPTH):
                ffn2()
                stat_sq()
                first = dict(ready=x_ready, also=square_sum)
                if layer == 0:
                    for pair in range(4):
                        for k in range(9):
                            tile(x, **(first if pair == k == 0 else {}))
                            if pair == 0 and k == 1:
                                c.wait(tab_in, 16)
                            if 1 <= k < 7:
                                rope(aq[:, k - 1, :], tba[:, A_ROT:A_ROT + P])
                        read_all()
                        turn([[(lambda b, i=i: b[:, i * P:i * P + P], aq[:, 6 + g, i * P:i * P + P]) for i in range(QT)]
                              for g in range(3)])
                        pe.wait_ge(turn_read, c.n["turn"])
                        c.wait(rope_done, 6)
                        attend(jobs_a(), sca, pta, otok)
                    read_all()
                    for n in range(4):
                        pe.wait_ge(split_done, c.at("unit") + 1)
                        if n >= 2:
                            c.wait(emb_read, 2)
                        for j in range(2):
                            unit(bank[n % 2 * 2 + j], [j * 512 + q * P for q in range(4)], ao, range(4), True, True, last=j == 1)
                    c.wait(emb_read, 4)
                else:
                    for c4 in range(2):
                        for k in range(6):
                            tile(x, **(first if c4 == k == 0 else {}))
                            if c4 == 0 and k == 1:
                                c.wait(tab_in, 16)
                            if k in (1, 3, 4, 5):
                                rope(bk[:, k - 1, :], tbb[:, B_ROT:B_ROT + P])
                        read_all()
                        rope(bk[:, 5, :], tbb[:, B_ROT:B_ROT + P], True)
                        turn([[(lambda b, i=i: b[:, i * P:i * P + P], bk[:, 1, i * P:i * P + P]) for i in range(QT)]])
                        pe.wait_ge(turn_read, c.n["turn"])
                        c.wait(rope_done, 5)
                        attend(jobs_b(c4), scb, ptb, otokb)
                    read_all()
                    with c.loop(2, unit=4, **TILES4):
                        for k in range(4):
                            tile(bo)
                stat_sq()
                ffn2()
                read_all()
                c.wait(p_ready, 2)
                for n in range(2):
                    pe.wait_ge(split_done, c.at("unit") + 1)
                    if n == 1:
                        c.wait(emb_read, 4)
                    for j in range(4):
                        unit(bank[4 + j], [j * 256, j * 256 + P], px, range(2), True, True, last=j == 3)
                    if n == 0:
                        stat_sq()
                tiles_of(8, 2, x, ready=x_ready, also=square_sum)
                c.wait(emb_read, 4)
                stat_sq()

        @block.scalar
        def _(act):
            c = Count(act)

            def split(last=False):
                if last:
                    return
                n = c.n.get("split", 0)
                act.wait_ge(raw_in[n % 4], c.at("split", back=-1, div=4, mult=16))
                if n >= 2:
                    act.wait_ge(unit_done, c.at("split", back=1))
                act.activation(wh[n % 2][:, :], raw[n % 4][:, :], ACT.Copy).then_inc(hi_done, 1)
                c.tick("split")

            def units(n, last=False):
                for k in range(n):
                    if c.n.get("early", 0):
                        c.n["early"] -= 1
                    else:
                        split(last and k == n - 1)
                c.wait(unit_done, n)

            def split_early():
                split()
                c.tick("early")

            def link(ins):
                ins.then_inc(act_step, 1)
                c.wait(act_step)

            def rstd(src, e, dst=rs):
                link(act.activation(dst[:, :], src, ACT.Ln, bias=eps[:, e:e + 1]))
                act.activation(dst[:, :], dst[:, :], ACT.Exp, scale=-0.5).then_inc(rstd_ready, 1)

            def square(k):
                n = c.n.get("sqm", 0)
                if n >= 2:
                    act.wait_ge(sq_used, n - 1)
                act.activation(sq[k % 2][:, :], h[:, k, :], ACT.Square).then_inc(sq_made, 1)
                c.tick("sqm")

            def layer_norm(g, b, to_x):
                c.tick("stat_done")
                for k in range(DC):
                    c.wait(centred)
                    square(k)
                c.wait(sq_used, DC)
                rstd(bank[3][:, :], 0)
                for k in range(DC):
                    c.wait(normed)
                    bias = vec[:, b + k:b + k + 1]
                    if to_x:
                        act.activation(x[:, k, 0, :], prod[k % 2][:, :], ACT.Identity, bias=bias)
                        c.tick("affine")
                    act.activation(h[:, k, :], prod[k % 2][:, :], ACT.Identity, bias=bias).then_inc(affine, 1)
                    if to_x and k == 3:
                        split_early()

            def rms_pre(g, ready, early=(4,)):
                for k in range(DC):
                    c.wait(ready)
                    act.activation(x[:, k, 0, :], h[:, k, :], ACT.Copy, scale=vec[:, g + k:g + k + 1]).then_inc(x_hi, 1)
                    square(k)
                    if k in early:
                        split_early()
                c.wait(sq_used, DC)
                rstd(bank[3][:, :], 1, rs_in)

            def rms_post():
                c.wait(stat_done)
                rstd(bank[2][:, :], 1)

            def tile_square(n, last=False):
                units(n, last)
                square_of(bank[c.next_tile()][:, :])

            def square_of(src):
                k = c.n.get("sqs", 0)
                act.wait_ge(acc_done, c.at("acc") + 1)
                act.activation(sq[k % 2][:, :], src, ACT.Square).then_inc(sq_done, 1)
                c.tick("sqs")
                c.tick("acc")

            def attend(jobs, sc, pt, outs):
                jobs = list(jobs)

                def exps(j):
                    job = jobs[j]
                    n, t = c.n.get("job", 0) // 4 % 2, job["t"]
                    parts = {}
                    for seg, (off, w, _) in zip(job["segs"], spans(job)):
                        parts.setdefault(seg[3], []).append((off, off + w))
                    c.wait(max_ready)
                    for s_, p_ in sorted(parts.items()):
                        sl = sc[j % 3][:, p_[0][0]:p_[-1][1]]
                        act.activation(sl, sl, ACT.Exp, bias=negm[:, n, s_, t:t + 1], scale=0.125,
                                       accum_out=den[:, n, s_, t:t + 1]).then_inc(exp_done, 1)
                    if job["kind"] == "b" and t == QT - 1:
                        act.activation(esink[:, n, :], negm[:, n, 0, :], ACT.Exp,
                                       bias=vec[:, V_SINK + job["head"]:V_SINK + job["head"] + 1]).then_inc(sink_exp, 1)
                    c.tick("job")

                def group():
                    c.tick("blk_turned")
                    c.tick("blk")
                    return c.n["blk"] % 2 == 1

                def copies(j):
                    for gi, grp in enumerate(blocks(jobs[j])):
                        if group():
                            act.wait_ge(blk_turned, c.n["blk_turned"])
                            if c.n.get("o", 0) >= 2:
                                act.wait_ge(o_done, c.n["o"] - 1)
                            copy_group(pt[j % 2], gi, grp, bank[5], blk_act)
                    c.tick("o")

                def pair_out(k):
                    src = tmp[k % 2][:, :]
                    if group():
                        act.wait_ge(blk_turned, c.n["blk_turned"])
                        if c.n.get("pairs", 0):
                            act.wait_ge(ot_ready, c.n["pairs"])
                        act.activation(src, bank[5][:, :], ACT.Copy).then_inc(blk_act, 1)
                        act.wait_ge(blk_act, c.n["blk"] // 2 + c.n["blk"] % 2)
                    else:
                        act.wait_ge(blk_dve, c.n["blk"] // 2)
                    c.tick("pairs")
                    act.activation(outs[k][0], in_order(outs[k], src), ACT.Copy).then_inc(ot_hi, 1)

                exps(0)
                exps(1)
                copies(0)
                n_jobs = len(jobs)
                for j in range(n_jobs):
                    if j + 1 < n_jobs:
                        copies(j + 1)
                    if j + 2 < n_jobs:
                        exps(j + 2)
                    if pair_done(j):
                        pair_out(j // 8 - 1)
                pair_out(n_jobs // 8 - 1)

            def log_exp():
                act.preload_act_table_set("natural_log_exp_and_others")

            def copy_group(pt_, gi, grp, src, done):
                w0 = grp[0][3]
                first = 0 if w0 == P else P
                if len(grp) * P > first:
                    ins = act.activation(pt_[:, gi * 512 + first:gi * 512 + len(grp) * P], src[:, first:len(grp) * P], ACT.Copy)
                if first:
                    ins = act.activation(pt_[0:w0, 0:P], src[0:w0, 0:P], ACT.Copy)
                ins.then_inc(done, 1)

            for k in range(4):
                act.dma_start(h[:, 2 * k:2 * k + 2, :],
                              x_t[2 * k * P:2 * k * P + 2 * P].rearrange("(c p) t -> p c t", p=P)).then_inc(h_in[k], 16)
            log_exp()
            split()
            act.wait_ge(pool_step, 2)
            for k in range(DC):
                if k % 2 == 0:
                    act.wait_ge(h_in[k // 2], 16)
                act.activation(x[:, k, 0, :], h[:, k, :], ACT.Copy).then_inc(x_hi, 1)
            act.wait_ge(consts_in, 48)

            for layer in range(DEPTH):
                def prepare(k):
                    if k in (3, 4):
                        i, w = k - 3, (128, 64)[k - 3]
                        c.wait(z_done)
                        bg = V_BG + 2 * layer + i
                        link(act.activation(gt[0][0:w, i, :], bank[6 + i][0:w, :], ACT.Abs, bias=vec[0:w, bg:bg + 1]))
                        link(act.activation(gt[0][0:w, i, :], gt[0][0:w, i, :], ACT.Exp, scale=-1.0))
                        act.activation(gt[0][0:w, i, :], gt[0][0:w, i, :], ACT.Ln, bias=1.0).then_inc(gk_act, 1)
                    if k in (5, 6):
                        i, w = k - 5, (128, 64)[k - 5]
                        c.wait(gk_done)
                        act.activation(gt[2][0:w, i, :], gt[0][0:w, i, :], ACT.Exp, scale=1.0 / 16).then_inc(gla_exp, 1)
                        act.activation(gt[1][0:w, i, :], gt[0][0:w, i, :], ACT.Exp, scale=-1.0 / 16).then_inc(gla_exp, 1)
                    if k in (7, 8):
                        i, w = k - 7, (128, 64)[k - 7]
                        c.wait(gk_done)
                        act.activation(gt[0][0:w, i, :], gt[0][0:w, i, :], ACT.Exp, scale=1.0 / 16).then_inc(gla_exp, 1)
                    if k >= 18:
                        c.wait(go_stat)
                        rstd(bank[6][:, :], 1)
                    if 17 <= k < 20:
                        if k > 17:
                            c.wait(go_out)
                        link(act.activation(prod[0][:, :], proj[:, GO + k - 17, :], ACT.Exp, scale=-1.0))
                        link(act.activation(prod[0][:, :], prod[0][:, :], ACT.Ln, bias=1.0))
                        act.activation(prod[0][:, :], prod[0][:, :], ACT.Exp, scale=-1.0).then_inc(go_silu, 1)
                        c.wait(go_copied)
                        act.activation(sq[0][:, :], tmp[0][:, :], ACT.Square).then_inc(go_sq, 1)

                for k in range(N_PROJ):
                    units(1)
                    c.next_tile()
                    prepare(k)
                c.wait(go_out)
                for cc in range(3):
                    act.activation(x[:, 3 + cc, 0, :], proj[:, GO + cc, :], ACT.Copy).then_inc(mx_hi, 1)
                for k in range(2):
                    c.wait(pool_mm)
                    ps = V_PS + 2 * layer + k
                    for e in range(2):
                        r = slice(e * HD, e * HD + HD)
                        ins = act.activation(proj[r, PU + k, :], bank[4 + 2 * k + e][r, :], ACT.Copy, scale=vec[r, ps:ps + 1])
                    link(ins)
                    act.activation(x[:, 6 + k, 0, :], proj[:, PU + k, :], ACT.Copy).then_inc(mx_hi, 1)
                for kind in range(2):
                    for g in range(2):
                        r = slice(g * HD, g * HD + HD)
                        c.wait(cmp_bias)
                        act.activation(hid[r, kind, 0:N_CMP], tmp[0][r, 64:64 + N_CMP], ACT.Exp,
                                       scale=-2.0 * 0.7978845608028654).then_inc(gate_exp, 1)
                c.wait(cmp_ready)
                act.activation(gate_c[:, :, :], gate_c[:, :, :], ACT.Exp, scale=-1.0).then_inc(gate_exp, 1)
                attend(jobs_nsa(), sc1, pt1, [(x[:, k, 0, :], x[:, k, 1, :], False) for k in range(3)])
                with c.loop(2, split=4, unit_done=4, **TILES4):
                    for k in range(4):
                        units(1)
                        c.next_tile()
                layer_norm(V_LN + 32 * layer, V_LN + 32 * layer + 8, True)
                def up4(i):
                    for k in range(4):
                        units(1)
                        b = c.next_tile()
                        act.activation(tmp[k % 2][:, :], bank[b][:, :], ACT.Relu).then_inc(relu_done, 1)
                        act.wait_ge(bank_free[b], c.at(f"used{b}"))
                        act.activation(mid[:, i * 4 + k, 0, :], prod[k % 2][:, :], ACT.Copy).then_inc(mid_hi, 1)

                for half in range(2):
                    up4(0)
                    with c.loop(3, split=4, unit_done=4, **TILES4) as i:
                        up4(i + 1)
                    with c.loop(4, split=4, unit_done=4, **TILES2):
                        for k in range(2):
                            units(2)
                            c.next_tile()
                layer_norm(V_LN + 32 * layer + 16, V_LN + 32 * layer + 24, layer == 0)

            def ffn2(embed=False):
                def two(i):
                    for k in range(2):
                        units(1)
                        b = c.next_tile()
                        act.wait_ge(bank_free[b], c.at(f"used{b}"))
                        act.activation(tmp[k][:, :], tmp[k][:, :], ACT.Silu).then_inc(gate_made, 1)
                        units(1)
                        c.next_tile()
                        c.wait(pair_made)
                        act.activation(mid[:, i * 2 + k, 0, :], prod[k][:, :], ACT.Copy).then_inc(mid_hi, 1)

                two(0)
                with c.loop(FF2C // 2 - 1, split=4, unit_done=4, pair_made=2, **TILES4) as i:
                    two(i + 1)
                log_exp()
                if embed:
                    c.wait(p_in, 16)
                    for k in range(2):
                        act.activation(px[:, k, 0, :], pf[:, k, :], ACT.Copy).then_inc(p_hi, 1)
                    c.wait(p_ready, 2)
                with c.loop(2, split=12, unit_done=12, sqs=4, acc=4, **TILES4):
                    for k in range(4):
                        tile_square(3)

            for layer in range(DEPTH):
                g = V_RMS + 64 * layer
                if layer == 0:
                    rms_pre(g, affine)
                ffn2()
                rms_post()
                rms_pre(g + 16, h_ready)
                if layer == 0:
                    for pair in range(4):
                        for k in range(9):
                            units(1)
                            c.next_tile()
                        attend(jobs_a(), sca, pta, [outs_a(pair)])
                    for n in range(4):
                        units(1)
                        for j in range(2):
                            square_of(bank[n % 2 * 2 + j][:, :])
                else:
                    for c4 in range(2):
                        for k in range(6):
                            units(1)
                            c.next_tile()
                        attend(jobs_b(c4), scb, ptb, outs_b(c4))
                    with c.loop(2, split=4, unit_done=4, sqs=4, acc=4, **TILES4):
                        for k in range(4):
                            tile_square(1)
                rms_post()
                rms_pre(g + 32, h_ready)
                ffn2(True)
                units(1)
                rms_post()
                rms_pre(g + 48, h_ready, (0, 5))
                units(1)
                for k in range(DC):
                    units(1, last=layer == DEPTH - 1 and k == DC - 1)
                    b = c.next_tile()
                    act.wait_ge(bank_free[b], c.at(f"used{b}"))
                    act.activation(tmp[k % 2][:, :], tmp[k % 2][:, :], ACT.Sigmoid).then_inc(gate_made, 1)
                    if k == DC - 1:
                        log_exp()
                    c.wait(sig_done)
                    square_of(y[:, k, :])
                rms_post()
                if layer < DEPTH - 1:
                    rms_pre(g + 64, h_ready)

        @block.vector
        def _(dve):
            c = Count(dve)

            def split(last=False):
                if last:
                    return
                n = c.n.get("hi_done", 0)
                c.wait(hi_done)
                dve.tensor_tensor(wl[n % 2][:, :], raw[n % 4][:, :], wh[n % 2][:, :].bitcast(F32),
                                  ALU.subtract).then_inc(split_done, 1)

            def units(n, last=False):
                for k in range(n):
                    if c.n.get("early", 0):
                        c.n["early"] -= 1
                    else:
                        split(last and k == n - 1)
                c.wait(unit_done, n)

            def split_early():
                split()
                c.tick("early")

            def link(ins):
                ins.then_inc(dve_step, 1)
                c.wait(dve_step)

            def free(ins):
                ins.then_inc(bank_free[c.next_tile()], 1)

            def lo_of(dst, src, hi, done):
                dve.tensor_tensor(dst, src, hi.bitcast(F32), ALU.subtract).then_inc(done, 1)
                c.tick(f"made {done.name}")

            def layer_norm(g, to_x):
                c.wait(stat_done)
                for k in range(DC):
                    dve.tensor_tensor(h[:, k, :], h[:, k, :], bank[2][:, :], ALU.subtract).then_inc(centred, 1)
                c.wait(centred, DC)
                c.wait(rstd_ready)

                def scaled(k):
                    if k >= 2:
                        c.wait(affine)
                    dve.scalar_tensor_tensor(prod[k % 2][:, :], h[:, k, :], vec[:, g + k:g + k + 1], rs[:, :],
                                             ALU.mult, ALU.mult).then_inc(normed, 1)
                scaled(0)
                scaled(1)
                for k in range(DC):
                    if k + 2 < DC:
                        scaled(k + 2)
                    else:
                        c.wait(affine)
                    if to_x:
                        lo_of(x[:, k, 1, :], h[:, k, :], x[:, k, 0, :], x_ready)
                        if k == 3:
                            split_early()

            def low_part(g, k, early=(4,)):
                c.wait(x_hi)
                dve.scalar_tensor_tensor(x[:, k, 1, :], h[:, k, :], vec[:, g + k:g + k + 1],
                                         x[:, k, 0, :].bitcast(F32), ALU.mult, ALU.subtract).then_inc(x_ready, 1)
                if k in early:
                    split_early()

            def residual(g, pre=None, meanwhile=None, early=(4,)):
                c.wait(rstd_ready)

                def part(k):
                    if k >= 2:
                        c.wait(h_ready)
                    dve.scalar_tensor_tensor(prod[k % 2][:, :], y[:, k, :], vec[:, g + k:g + k + 1], rs[:, :],
                                             ALU.mult, ALU.mult).then_inc(part_made, 1)
                part(0)
                part(1)
                if meanwhile is not None:
                    meanwhile()
                for k in range(DC):
                    if k + 2 < DC:
                        part(k + 2)
                    else:
                        c.wait(h_ready)
                    if pre is not None:
                        low_part(pre, k, early)
                if pre is not None:
                    c.wait(rstd_ready)

            def copy_tile(dst, n=1, last=False):
                units(n, last)
                free(dve.tensor_copy(dst, bank[c.n.get("tile", 0) % 2][:, :]))

            def scale_tile(dst):
                units(1)
                free(dve.tensor_tensor(dst, bank[c.n.get("tile", 0) % 2][:, :], rs_in[:, :], ALU.mult))

            def copy_tile_sq(dst, n):
                units(n)
                c.wait(sq_done)
                free(dve.tensor_copy(dst, bank[c.n.get("tile", 0) % 2][:, :]))

            def rope(ap, cos, sin, banks=(2, 3)):
                c.wait(rot_done)
                k = c.n.get("rope", 0)
                dve.tensor_tensor(tmp[k % 2][:, :], bank[banks[k % len(banks)]][:, :], sin, ALU.mult).then_inc(rope_used, 1)
                link(dve.tensor_tensor(ap, ap, cos, ALU.mult))
                dve.wait_ge(rope_used, k + 1)
                dve.tensor_tensor(ap, ap, tmp[k % 2][:, :], ALU.add).then_inc(rope_done, 1)
                c.tick("rope")

            def turned_into(dst, src, banks=(4, 5)):
                c.wait(turned)
                k = c.n.get("turn", 0)
                dve.tensor_copy(dst, src(bank[banks[k % len(banks)]])).then_inc(turn_read, 1)
                c.tick("turn")

            def attend(jobs, sc, pt, ot, outs):
                jobs = list(jobs)

                def masks(j):
                    job = jobs[j]
                    n, t = c.n.get("job", 0) // 4 % 2, job["t"]
                    nsa = job["kind"] == "nsa"
                    for si, (seg, (off, w, _)) in enumerate(zip(job["segs"], spans(job))):
                        c.wait(scored)
                        dve.tensor_tensor_reduce(
                            out=sc[j % 3][:, off:off + w], in0=bank[2 + si][:, 0:w], in1=seg[1], scale=1.0,
                            scalar=-3.0e38, op0=ALU.add, op1=ALU.max,
                            accum_out=mx[:, n, t, si:si + 1]).then_inc(score_read, 1)
                        c.wait(score_read)
                    if nsa:
                        dve.tensor_scalar(negm[:, n, :, t], mx[:, n, t, 0:3], FLOOR, -0.125, ALU.max, ALU.mult).then_inc(max_ready, 1)
                    elif job["kind"] == "a":
                        dve.tensor_scalar(negm[:, n, 0, t:t + 1], mx[:, n, t, 0:1], mx[:, n, t, 1:2], -0.125,
                                          ALU.max, ALU.mult).then_inc(max_ready, 1)
                    else:
                        hd_ = job["head"]
                        dve.tensor_scalar(negm[:, n, 0, t:t + 1], mx[:, n, t, 0:1], -0.125, nsink[:, hd_:hd_ + 1],
                                          ALU.mult, ALU.min).then_inc(max_ready, 1)
                    c.tick("job")

                def group():
                    c.tick("blk_turned")
                    c.tick("blk")
                    return c.n["blk"] % 2 == 0

                def copies(j):
                    for gi, grp in enumerate(blocks(jobs[j])):
                        if group():
                            dve.wait_ge(blk_turned, c.n["blk_turned"])
                            if c.n.get("copied", 0) >= 2:
                                dve.wait_ge(o_done, c.n["copied"] - 1)
                            copy_group(pt[j % 2], gi, grp, bank[6], blk_dve)
                    c.tick("copied")

                def norm(j):
                    job = jobs[j]
                    c.wait(o_done, QT)
                    hd_ = c.n.get("heads", 0)
                    n = hd_ % 2
                    if hd_ >= 2 and job["g"] == 0:
                        dve.wait_ge(ot_ready, c.n.get("pairs", 0) - 1) if c.n.get("pairs", 0) >= 2 else None
                    dst = ot[j // 8 % 2][:, :, job["g"] * HD:job["g"] * HD + HD]
                    cols = lambda s: bank[o_bank(job, hd_, s)][:, 0:QT * HD].rearrange("p (t d) -> p t d", t=QT)
                    bc = lambda s: rden[:, n, s, :].rearrange("p (t o) -> p t o", o=1).broadcast_to([P, QT, HD])
                    if job["kind"] == "nsa":
                        link(dve.tensor_scalar(den[:, n, :, :], den[:, n, :, :], 1e-30, None, ALU.max))
                        link(dve.reciprocal(rden[:, n, :, :], den[:, n, :, :]))
                        gg = gate_c[:, :, 3 * job["head"]:3 * job["head"] + 3].rearrange("p t s -> p s t")
                        link(dve.tensor_tensor(rden[:, n, :, :], rden[:, n, :, :], gg, ALU.mult))
                        part = prod[0][:, 0:QT * HD].rearrange("p (t d) -> p t d", t=QT)
                        link(dve.tensor_tensor(dst, cols(0), bc(0), ALU.mult))
                        for s in (1, 2):
                            link(dve.tensor_tensor(part, cols(s), bc(s), ALU.mult))
                            ins = dve.tensor_tensor(dst, dst, part, ALU.add)
                            if s == 1:
                                link(ins)
                    else:
                        if job["kind"] == "b":
                            c.wait(sink_exp)
                            link(dve.tensor_tensor(den[:, n, 0, :], den[:, n, 0, :], esink[:, n, :], ALU.add))
                        link(dve.reciprocal(rden[:, n, 0, :], den[:, n, 0, :]))
                        ins = dve.tensor_tensor(dst, cols(0), bc(0), ALU.mult)
                    ins.then_inc(o_read, 1)
                    c.tick("heads")

                def pair_out(k):
                    src = tmp[k % 2][:, :]
                    if group():
                        dve.wait_ge(blk_turned, c.n["blk_turned"])
                        if c.n.get("pairs", 0):
                            dve.wait_ge(ot_ready, c.n["pairs"])
                        dve.tensor_copy(src, bank[6][:, :]).then_inc(blk_dve, 1)
                        dve.wait_ge(blk_dve, c.n["blk"] // 2)
                    c.tick("pairs")
                    c.wait(ot_hi)
                    hi = outs[k][0].bitcast(F32)
                    dve.tensor_tensor(outs[k][1], in_order(outs[k], src), hi, ALU.subtract).then_inc(ot_ready, 1)

                masks(0)
                masks(1)
                copies(0)
                n_jobs = len(jobs)
                for j in range(n_jobs):
                    if j + 2 < n_jobs:
                        masks(j + 2)
                    if j + 1 < n_jobs:
                        copies(j + 1)
                    if jobs[j]["t"] == QT - 1:
                        norm(j)
                    if pair_done(j):
                        pair_out(j // 8 - 1)
                pair_out(n_jobs // 8 - 1)

            def copy_group(pt_, gi, grp, src, done):
                w0 = grp[0][3]
                first = 0 if w0 == P else P
                if len(grp) * P > first:
                    ins = dve.tensor_copy(pt_[:, gi * 512 + first:gi * 512 + len(grp) * P], src[:, first:len(grp) * P])
                if first:
                    ins = dve.tensor_copy(pt_[0:w0, 0:P], src[0:w0, 0:P])
                ins.then_inc(done, 1)

            def prepare(layer, k):
                if k == 3:
                    c.wait(z_done, 2)
                    c.wait(tab_in, 16)
                if k in (3, 4):
                    i, w = k - 3, (128, 64)[k - 3]
                    bg = V_BG + 2 * layer + i
                    c.wait(gk_act)
                    link(dve.tensor_scalar(tmp[i][0:w, :], bank[6 + i][0:w, :], vec[0:w, bg:bg + 1], 0.0, ALU.add, ALU.min))
                    link(dve.tensor_tensor(tmp[i][0:w, :], tmp[i][0:w, :], gt[0][0:w, i, :], ALU.subtract))
                    dve.tensor_tensor_scan(gt[0][0:w, i, :], tb1[0:w, T_RESET:T_RESET + S], tmp[i][0:w, :], 0.0,
                                           ALU.mult, ALU.add).then_inc(gk_done, 1)
                if k in (6, 7):
                    i, w, qc, kc = ((0, 128, GQ, GK), (1, 64, GQX, GKX))[k - 6]
                    c.wait(gla_exp, 2)
                    link(dve.scalar_tensor_tensor(proj[0:w, qc, :], proj[0:w, qc, :], 32.0 ** -0.5, gt[2][0:w, i, :], ALU.mult, ALU.mult))
                    link(dve.tensor_copy(prod[1][0:w, i * 8:i * 8 + 8], gt[2][0:w, i, 63::64]))
                    link(dve.tensor_tensor(gt[1][0:w, i, :], gt[1][0:w, i, :], proj[0:w, kc, :], ALU.mult))
                    b3 = gt[0][0:w, i, :].rearrange("p (n c) -> p n c", c=64)
                    link(dve.tensor_copy(prod[0][0:w, 0:8], gt[0][0:w, i, 63::64]))
                    last = prod[0][0:w, 0:8].rearrange("p (n o) -> p n o", o=1).broadcast_to([w, 8, 64])
                    dve.tensor_tensor(b3, last, b3, ALU.subtract).then_inc(gk_done, 1)
                if k in (8, 9):
                    i, w, kc = ((0, 128, GK), (1, 64, GKX))[k - 8]
                    c.wait(gla_exp)
                    ins = dve.tensor_tensor(proj[0:w, kc, :], proj[0:w, kc, :], gt[0][0:w, i, :], ALU.mult)
                    if i == 0:
                        link(ins)
                    else:
                        ins.then_inc(gla_kend, 1)
                if k == 12:
                    link(dve.memset(st_gla[:, 0, :, :], 0.0))
                    c.wait(ds_done)
                    for n in range(7):
                        for gi, w in enumerate((128, 64)):
                            ins = dve.scalar_tensor_tensor(
                                st_gla[0:w, n + 1, gi, :], st_gla[0:w, n, gi, :], prod[1][0:w, gi * 8 + n:gi * 8 + n + 1],
                                bank[(2, 3, 6, 7)[n % 2 * 2 + gi]][0:w, n // 2 * HD:n // 2 * HD + HD], ALU.mult, ALU.add)
                            if n < 6 or gi == 0:
                                link(ins)
                    ins.then_inc(st_done, 1)
                if 13 <= k < 17:
                    c.wait(am_done)
                    for hh in range(6):
                        ins = dve.scalar_tensor_tensor(
                            at_gla[:, k - 13, hh, :], bank[(2, 3, 6, 7)[hh % 4]][:, hh // 4 * P:hh // 4 * P + P], 3.0e38,
                            tb1[:, T_GLA:T_GLA + P], ALU.min, ALU.mult)
                    ins.then_inc(am_read, 1)
                if k >= 18:
                    cc = k - 18
                    c.wait(go_silu)
                    link(dve.tensor_tensor(prod[0][:, :], prod[0][:, :], proj[:, GO + cc, :], ALU.mult))
                    c.wait(rstd_ready)
                    ng = V_NG + 3 * layer + cc
                    link(dve.scalar_tensor_tensor(tmp[1][:, :], tmp[0][:, :], vec[:, ng:ng + 1], rs[:, :], ALU.mult, ALU.mult))
                    dve.tensor_tensor(proj[:, GO + cc, :], tmp[1][:, :], prod[0][:, :], ALU.mult).then_inc(go_out, 1)
                    c.wait(go_out)
                if 17 <= k < 20:
                    c.wait(go_done)
                    dve.tensor_copy(tmp[0][0:64, :], bank[2][0:64, :])
                    dve.tensor_copy(tmp[0][64:128, :], bank[3][64:128, :]).then_inc(go_copied, 1)
                if k in ROPED:
                    rope(proj[:, ROPED[k], :], tb1[:, T_COS:T_COS + S], tb1[:, T_SIN:T_SIN + S], (5,))
                if k in TURNED:
                    ch = TURNED[k]
                    three = lambda b: b[:, :].rearrange("p (t d) -> p t d", t=QT)
                    kt_ = gt[2][:, :, :].rearrange("p a s -> p (a s)")[:, 0:QT * 192].rearrange("p (t d) -> p t d", t=QT)
                    turned_into(*{
                        GK: (kt_[:, :, 0:128], three),
                        GKX: (kt_[:, :, 128:192], lambda b: b[:, 0:256].rearrange("p (t d) -> p t d", t=QT)),
                        VS: (vtok[:, :, 0, :], three), VW: (vtok[:, :, 1, :], three),
                        GQX: (gate_c[:, :, :], lambda b: three(b)[:, :, GATE_ROW:GATE_ROW + 18]),
                    }.get(ch, (proj[:, ch, :], lambda b: b[:, :])), (4,))

            def compress():
                for kind in range(2):
                    src = proj[:, (KC, VC)[kind], :]
                    win = bass.AP(tensor=src.tensor, offset=src.offset, ap=[list(src.ap[0]), [1, 32], [16, N_CMP]])
                    dve.tensor_copy(xp[kind][:, :, 0:N_CMP], win)
                    pos = sm[:, SM_POS + 32 * kind:SM_POS + 32 * kind + 32]
                    dve.tensor_copy(xp[kind][:, :, N_CMP:32].rearrange("p j o -> p (j o)"), pos).then_inc(cmp_in, 1)
                for m, ch in enumerate((GO, GO + 1, GO + 2, PU, PU + 1)):
                    c.wait(mx_hi)
                    lo_of(x[:, 3 + m, 1, :], proj[:, ch, :], x[:, 3 + m, 0, :], x_ready)
                z, t1 = tmp[0], tmp[1]
                for kind in range(2):
                    c.wait(cmp_mm)
                    for g in range(2):
                        r = slice(g * HD, g * HD + HD)
                        ps = bank[(2, 0)[kind] + g][r, 0:32]
                        link(dve.tensor_copy(cmpb[r, 0:1], ps[:, N_CMP:32]))
                        zz = z[r, 0:N_CMP]
                        link(dve.tensor_scalar(zz, ps[:, 0:N_CMP], cmpb[r, 0:1], None, ALU.add))
                        link(dve.tensor_tensor(t1[r, 0:N_CMP], zz, zz, ALU.mult))
                        link(dve.tensor_scalar(t1[r, 0:N_CMP], t1[r, 0:N_CMP], 0.044715, 1.0, ALU.mult, ALU.add))
                        dve.tensor_tensor(z[r, 64:64 + N_CMP], t1[r, 0:N_CMP], zz, ALU.mult).then_inc(cmp_bias, 1)
                        c.wait(gate_exp)
                        link(dve.tensor_scalar(t1[r, 0:N_CMP], hid[r, kind, 0:N_CMP], 1.0, None, ALU.add))
                        link(dve.reciprocal(t1[r, 64:64 + N_CMP], t1[r, 0:N_CMP]))
                        dve.tensor_tensor(hid[r, kind, 0:N_CMP], t1[r, 64:64 + N_CMP], zz, ALU.mult).then_inc(cmp_hid, 1)
                c.wait(cmp_out)
                for g in range(2):
                    r = slice(g * HD, g * HD + HD)
                    dve.tensor_copy(kc_c[r, 0:N_CMP], bank[6 + g][r, 0:N_CMP])
                    ins = dve.tensor_copy(vc_c[0:N_CMP, r], bank[4 + g][0:N_CMP, r])
                ins.then_inc(cmp_ready, 1)
                c.wait(gate_exp)
                link(dve.tensor_scalar(gate_c[:, :, :], gate_c[:, :, :], 1.0, None, ALU.add))
                link(dve.reciprocal(gate_c[:, :, :], gate_c[:, :, :]))

            c.wait(consts_in, 48)
            dve.tensor_scalar(nsink[:, :], vec[:, V_SINK:V_SINK + 16], -1.0, None, ALU.mult)
            for layer in range(DEPTH):
                for j in (1, 5):
                    g = V_RMS + 64 * layer + 8 * j
                    link(dve.tensor_scalar(vec[:, g:g + 8], vec[:, g:g + 8], 0.5, None, ALU.mult))
            split()
            for k in range(DC):
                c.wait(x_hi)
                lo_of(x[:, k, 1, :], h[:, k, :], x[:, k, 0, :], x_ready)

            for layer in range(DEPTH):
                for k in range(N_PROJ):
                    copy_tile(proj[:, ORDER[k], :])
                    prepare(layer, k)
                compress()
                attend(jobs_nsa(), sc1, pt1, otok1, [(x[:, k, 0, :], x[:, k, 1, :], False) for k in range(3)])
                with c.loop(2, hi_done=4, unit_done=4, **TILES4) as i:
                    for k in range(4):
                        units(1)
                        b = bank[c.n.get("tile", 0) % 2]
                        hm = h[:, i * 4 + k, :]
                        free(dve.scalar_tensor_tensor(hm, hm, ALPHA, b[:, :], ALU.mult, ALU.add))
                layer_norm(V_LN + 32 * layer, True)

                def up4(i):
                    for k in range(4):
                        units(1)
                        c.wait(relu_done)
                        b = bank[c.n.get("tile", 0) % 2]
                        free(dve.tensor_tensor(prod[k % 2][:, :], tmp[k % 2][:, :], b[:, :], ALU.mult))
                        c.wait(mid_hi)
                        lo_of(mid[:, i * 4 + k, 1, :], prod[k % 2][:, :], mid[:, i * 4 + k, 0, :], mid_ready)

                for half in range(2):
                    up4(0)
                    with c.loop(3, hi_done=4, unit_done=4, relu_done=4, mid_hi=4, **{"made mid_ready": 4}, **TILES4) as i:
                        up4(i + 1)
                    with c.loop(4, hi_done=4, unit_done=4, **TILES2) as i:
                        for k in range(2):
                            units(2)
                            b = bank[c.n.get("tile", 0) % 2]
                            hm = h[:, i * 2 + k, :]
                            free(dve.scalar_tensor_tensor(hm, hm, ALPHA if half == 0 else 1.0, b[:, :], ALU.mult, ALU.add))
                layer_norm(V_LN + 32 * layer + 16, layer == 0)

            def ffn2(embed=False):
                def two(i):
                    for k in range(2):
                        scale_tile(tmp[k][:, :])
                        scale_tile(prod[k][:, :])
                        b = 1 - c.n["tile"] % 2
                        dve.wait_ge(bank_free[b], c.at(f"used{b}"))
                        c.wait(gate_made)
                        dve.tensor_tensor(prod[k][:, :], tmp[k][:, :], prod[k][:, :], ALU.mult).then_inc(pair_made, 1)
                        c.wait(mid_hi)
                        lo_of(mid[:, i * 2 + k, 1, :], prod[k][:, :], mid[:, i * 2 + k, 0, :], mid_ready)

                two(0)
                with c.loop(FF2C // 2 - 1, hi_done=4, unit_done=4, mid_hi=2, gate_made=2, **{"made mid_ready": 2}, **TILES4) as i:
                    two(i + 1)
                if embed:
                    for k in range(2):
                        c.wait(p_hi)
                        lo_of(px[:, k, 1, :], pf[:, k, :], px[:, k, 0, :], p_ready)
                with c.loop(2, hi_done=12, unit_done=12, sq_done=4, **TILES4) as i:
                    for k in range(4):
                        copy_tile_sq(y[:, i * 4 + k, :], 3)

            for layer in range(DEPTH):
                g = V_RMS + 64 * layer
                if layer == 0:
                    for k in range(DC):
                        low_part(g, k)
                    c.wait(rstd_ready)
                ffn2()
                residual(g + 8, g + 16)
                if layer == 0:
                    for pair in range(4):
                        for k in range(9):
                            units(1)
                            b = bank[c.n["tile"] % 2]
                            view = [t[:, :].rearrange("p (j c r) -> p r c j", c=4, r=4) for t in (b, rs_in)]
                            free(dve.tensor_tensor(aq[:, k, :].rearrange("p (r c j) -> p r c j", r=4, c=4),
                                                   *view, ALU.mult))
                            if pair == 0 and k == 1:
                                c.wait(tab_in, 16)
                            if 1 <= k < 7:
                                rope(aq[:, k - 1, :], tba[:, A_COS:A_COS + S], tba[:, A_SIN:A_SIN + S])
                        for k in range(3):
                            turned_into(av[:, :, k, :], lambda b: b[:, :].rearrange("p (t d) -> p t d", t=QT))
                        attend(jobs_a(), sca, pta, otok, [outs_a(pair)])
                    for n in range(4):
                        units(1)
                        for j in range(2):
                            c.wait(sq_done)
                            dve.tensor_copy(y[:, 2 * n + j, :], bank[n % 2 * 2 + j][:, :]).then_inc(emb_read, 1)
                else:
                    for c4 in range(2):
                        for k in range(6):
                            scale_tile(bk[:, k, :])
                            if c4 == 0 and k == 1:
                                c.wait(tab_in, 16)
                            if k in (1, 3, 4, 5):
                                rope(bk[:, k - 1, :], tbb[:, B_COS:B_COS + S], tbb[:, B_SIN:B_SIN + S])
                        rope(bk[:, 5, :], tbb[:, B_COS:B_COS + S], tbb[:, B_SIN:B_SIN + S])
                        turned_into(bv[:, :, :], lambda b: b[:, :].rearrange("p (t d) -> p t d", t=QT))
                        attend(jobs_b(c4), scb, ptb, otokb, outs_b(c4))
                    with c.loop(2, hi_done=4, unit_done=4, sq_done=4, **TILES4) as i:
                        for k in range(4):
                            copy_tile_sq(y[:, i * 4 + k, :], 1)
                residual(g + 24, g + 32)
                ffn2(True)

                def emb_out(n):
                    for j in range(4):
                        dve.tensor_copy(emb[:, 4 * n + j, :], bank[4 + j][:, :]).then_inc(emb_read, 1)
                units(1)
                residual(g + 40, g + 48, lambda: emb_out(0), (0, 5))
                units(1)
                emb_out(1)
                for k in range(DC):
                    units(1, last=layer == DEPTH - 1 and k == DC - 1)
                    free(dve.tensor_tensor(tmp[k % 2][:, :], bank[c.n["tile"] % 2][:, :], rs_in[:, :], ALU.mult))
                    c.wait(gate_made)
                    dve.tensor_tensor(y[:, k, :], tmp[k % 2][:, :], emb[:, k, :], ALU.mult).then_inc(sig_done, 1)
                c.tick("sq_done", DC)
                residual(g + 56, g + 64 if layer < DEPTH - 1 else None)


def tables():
    f = np.float32
    pos = np.arange(S, dtype=f)
    inv = (f(500000.0) ** (-np.arange(8, dtype=f) * f(2.0) / f(16))).astype(f)
    ang = (pos[None, :] * inv[:, None]).astype(f)
    cos, sin = np.ones((P, S), f), np.zeros((P, S), f)
    rot = np.zeros((P, P), f)
    for r in (0, HD):
        for d in range(16):
            cos[r + d], sin[r + d] = np.cos(ang[d % 8]), np.sin(ang[d % 8])
        for d in range(8):
            rot[r + 8 + d, r + d], rot[r + d, r + 8 + d] = -1.0, 1.0
    p = np.arange(P)[:, None]

    def mask(width, first, ok):
        d = np.arange(width)[None, :] - first - p
        return np.where(ok(d), 0.0, BIG_NEG).astype(f)

    tok = np.arange(S)
    icnt = np.concatenate([np.repeat(np.stack([1.0 / np.minimum(tok + 1, w) for w in ws]), HD, 0)
                           for ws in ((2, 4), (8, 16))], 1).astype(f)
    reset = np.broadcast_to((tok % 64 != 0).astype(f), (P, S))
    t_, n_ = np.arange(QT)[None, :, None], np.arange(32)[None, None, :]
    cmp_ = np.where(16 * n_ + 31 <= t_ * P + p[:, :, None], 0.0, BIG_NEG).astype(f).reshape(P, QT * 32)
    i = np.arange(P)[None, :]
    gla = ((p <= i) & (p // 64 == i // 64)).astype(f)
    b64 = (p // HD == i // HD).astype(f) / HD
    t1 = np.concatenate([cos, sin, icnt, reset, mask(4 * P, 3 * P, lambda d: d <= 0), cmp_, gla, b64, rot], 1)
    order = tok.reshape(32, 4, 4).transpose(2, 1, 0).reshape(-1)
    d = order[None, :] - order[:, None]
    no = lambda ok: np.where(ok, 0.0, BIG_NEG).astype(f)
    near = no(abs(d) <= 64).reshape(QT, P, S).transpose(1, 0, 2).reshape(P, QT * S)
    own = d[:P, :P]
    ta = np.concatenate([cos[:, order], sin[:, order], rot, near, no((own % 4 == 0) & (abs(own) <= 256)),
                         no(own % 16 == 0)], 1)
    tb = np.concatenate([cos, sin, rot, mask(3 * P, P, lambda d: abs(d) <= 128)], 1)
    assert t1.shape[1] == T_N and ta.shape[1] == A_N and tb.shape[1] == B_N
    cs = np.stack([np.eye(P, dtype=f), np.full((P, P), 1.0 / D, f)])
    return [np.ascontiguousarray(a, dtype=f) for a in (t1, ta, tb, cs)]


def tiles(w):
    k, m = w.shape
    return w.reshape(k // P, P, m // P, P).transpose(2, 1, 0, 3).reshape(m // P, P, k)


def cut(t, n):
    return t.reshape(t.shape[0], P, n, UNIT).transpose(0, 2, 1, 3).reshape(-1, P, UNIT)


def weight_stream(a):
    units = []
    z = np.zeros
    for l in range(DEPTH):
        w = a["w_in"][l]
        cols = []
        for c in range(3):
            cols += [w[:, c * HD:c * HD + HD], w[:, (3 + c) * HD:(4 + c) * HD]]
        kv = [w[:, 384 + i * P:384 + i * P + P] for i in range(6)]
        cols += [kv[0], kv[1], kv[2], kv[4], kv[3], kv[5]]
        gate, gq, gk, gv, glr, go, pu = (w[:, i:j] for i, j in (
            (1152, 1170), (1170, 1362), (1362, 1554), (1554, 1938), (1938, 1954), (1954, 2338), (2338, 2594)))
        cols += [gv, gq, glr, z((D, 16), w.dtype), gate, z((D, 14), w.dtype), gk, z((D, 64), w.dtype), go, pu]
        units.append(tiles(np.concatenate(cols, 1))[list(ORDER)])
        wo = a["w_out"][l]
        rows = []
        for c in range(3):
            rows += [wo[c * HD:c * HD + HD], wo[(3 + c) * HD:(4 + c) * HD]]
        units.append(tiles(np.concatenate(rows + [wo[384:]], 0)))
        for half in range(2):
            units.append(tiles(a["w_up"][l][:, half * 2048:half * 2048 + 2048]))
            units.append(cut(tiles(a["w_down"][l][half * 2048:half * 2048 + 2048]), 2))
    for l in range(DEPTH):
        def ffn(i):
            wi = tiles(a["ffn_wi_2"][l, i])
            pairs = np.stack([wi[:FF2C], wi[FF2C:]], 1).reshape(-1, P, UNIT)
            wo = np.concatenate([a["ffn_wo_2"][l, i], z((2 * P, D), wi.dtype)], 0)
            return [pairs, cut(tiles(wo), 3)]
        units += ffn(0)
        if l == 0:
            w = a["a_wqkv_2"][0].reshape(D, 3, 3, 4, P)
            for pair in range(4):
                units.append(tiles(w[:, :, :, pair].reshape(D, 9 * P)))
            units.append(tiles(a["a_wo_2"][0]).reshape(4, 2, P, 512).transpose(0, 2, 1, 3).reshape(4, P, UNIT))
        else:
            w, wo = a["b_wqkv_2"][0], a["b_wo_2"][0]
            rows = []
            for c4 in range(2):
                cols = [w[:, 1024 + c4 * P:1024 + c4 * P + P], w[:, 1280 + c4 * P:1280 + c4 * P + P]]
                for c in range(4):
                    for hd in (8 * c4 + c, 8 * c4 + 4 + c):
                        cols.append(w[:, hd * HD:hd * HD + HD])
                        rows.append(wo[hd * HD:hd * HD + HD])
                units.append(tiles(np.concatenate(cols, 1)))
            units.append(tiles(np.concatenate(rows, 0)))
        units += ffn(1)
        units.append(tiles(a["ple_proj_2"][l]).reshape(2, 4, P, 256).transpose(0, 2, 1, 3).reshape(2, P, UNIT))
        units.append(tiles(a["ple_gate_2"][l]))
    return np.concatenate(units, 0)


def small_weights(a):
    out = []
    for l in range(DEPTH):
        blk = np.zeros((P, SM_W), a["cmp_w1"].dtype)
        for r in (0, HD):
            for kind in range(2):
                w1 = a["cmp_w1"][l, kind].reshape(32, HD, HD).transpose(1, 0, 2).reshape(HD, 2048)
                blk[r:r + HD, SM_W1 + kind * 2048:SM_W1 + kind * 2048 + 2048] = w1
                blk[r:r + HD, SM_POS + kind * 32:SM_POS + kind * 32 + 32] = a["cmp_pos"][l, kind].T
                blk[r:r + HD, SM_W2 + kind * HD:SM_W2 + kind * HD + HD] = a["cmp_w2"][l, kind]
        blk[GLR_ROW:GLR_ROW + 16, SM_G2:SM_G2 + 192] = a["gla_w_gate2"][l]
        for g in range(4):
            blk[g % 2 * HD:g % 2 * HD + HD, SM_PW + g // 2 * HD:SM_PW + g // 2 * HD + HD] = a["pool_w"][l, g]
        out.append(blk)
    return np.stack(out)


def vectors(a):
    v = np.zeros((P, V_N), a["ln1_g"].dtype)

    def put(col, x):
        n = -(-x.size // P)
        for i in range(n):
            part = x[i * P:(i + 1) * P]
            v[:part.size, col + i] = part

    for l in range(DEPTH):
        for j, name in enumerate(("ln1_g", "ln1_b", "ln2_g", "ln2_b")):
            put(V_LN + 32 * l + 8 * j, a[name][l])
        for j in range(8):
            put(V_RMS + 64 * l + 8 * j, a["norm_g_2"][l, j])
        put(V_BG + 2 * l, a["gla_b_gate"][l])
        put(V_NG + 3 * l, a["gla_norm_g"][l])
        put(V_PS + 2 * l, a["pool_scale"][l])
    v[:, V_SINK:V_SINK + 16] = a["b_sink_2"][0][None, :]
    return v


def kernel(**inputs):
    import concourse.bacc as _bacc
    from concourse.bass_utils import run_bass_kernel_spmd as _run

    a = {k: np.asarray(v) for k, v in inputs.items()}
    t1, ta, tb, cs = tables()
    arrays = {
        "stream": weight_stream(a),
        "x_t": np.ascontiguousarray(a["x"][0].T),
        "p_t": np.ascontiguousarray(a["p_2"][:, 0].transpose(0, 2, 1)),
        "small": small_weights(a),
        "vecs": vectors(a),
        "tab1": t1, "tab_a": ta, "tab_b": tb, "consts": cs,
    }
    nc = _bacc.Bacc("TRN2", target_bir_lowering=False, num_devices=1)
    args = [nc.dram_tensor(n, v.shape, F32, kind="ExternalInput").ap() for n, v in arrays.items()]
    out = nc.dram_tensor("out_t", (DC, P, S), F32, kind="ExternalOutput").ap()
    build(nc, *args, out)
    r = _run(nc, [arrays], core_ids=[0])
    return np.ascontiguousarray(r.results[0]["out_t"].reshape(D, S).T).reshape(1, S, D)
```

```python
from contextlib import ExitStack, contextmanager

import numpy as np
import concourse.bass as bass
from concourse import mybir

F32 = mybir.dt.float32
F32R = mybir.dt.float32r
ALU = mybir.AluOpType
ACT = mybir.ActivationFunctionType
AX = mybir.AxisListType

P = 128
S = 512
D = 1024
DC = D // P
QT = S // P
UNIT = 1024
DEPTH = 2
ALPHA = (2 * DEPTH) ** 0.25
LN_EPS, RMS_EPS = 1e-5, 1e-6
FF2C = 2816 // P
HD = 64
N_CMP = 31
BIG_NEG = -1.0e30
FLOOR = -1.0e20

Q0, KC, VC, KS, KW, VS, VW, GV, GQ, GQX, GK, GKX, GO, PU = 0, 3, 4, 5, 6, 7, 8, 9, 12, 13, 14, 15, 16, 19
N_PROJ = 21
GLR_ROW, GATE_ROW = 64, 96

SM_W1, SM_POS, SM_W2, SM_G2, SM_PW = 0, 4096, 4160, 4288, 4480
SM_W = 4608
V_LN = 0
V_RMS = 64
V_BG, V_NG, V_PS, V_SINK = 192, 196, 202, 206
V_N = 222
T_COS, T_SIN, T_ICNT, T_RESET, T_CAUS, T_CMP, T_GLA, T_B64, T_ROT = (
    0, 512, 1024, 2048, 2560, 3072, 3200, 3328, 3456)
T_N = 3584
A_COS, A_SIN, A_ROT, A_M0, A_M1 = 0, 512, 1024, 1152, 3200
A_N = 3456
B_COS, B_SIN, B_ROT, B_M = 0, 512, 1024, 1152
B_N = 1536


ORDER = (GQX, GK, GKX, GQ, KC, GV, GV + 1, GV + 2, KS, KW, VC, Q0, Q0 + 1, PU, PU + 1,
         GO, GO + 1, GO + 2, Q0 + 2, VS, VW)
ROPED = {5: KC, 9: KS, 10: KW, 12: Q0, 13: Q0 + 1, 20: Q0 + 2}
TURNED = {7: GV, 8: GV + 1, 9: GV + 2, 10: GK, 11: GKX, 18: GQX, 20: VS}

TILES4 = dict(tile=4, used0=2, used1=2)
TILES2 = dict(tile=2, used0=1, used1=1)


class Count:

    def __init__(self, eng):
        self.eng, self.n, self.loops = eng, {}, []

    def at(self, name, back=0, div=1, mult=1):
        v = (self.n.get(name, 0) // div - back) * mult
        for i, per in self.loops:
            k = per.get(name, 0) // div * mult
            if k:
                v = i * k + v
        return v

    def tick(self, name, k=1):
        self.n[name] = self.n.get(name, 0) + k

    def next_tile(self):
        b = self.n.get("tile", 0) % 2
        self.tick("tile")
        self.tick(f"used{b}")
        return b

    def skip_tiles(self, n):
        for _ in range(n):
            self.next_tile()

    def wait(self, sem, k=1):
        self.tick(sem.name, k)
        self.eng.wait_ge(sem, self.at(sem.name))

    @contextmanager
    def loop(self, rounds, **per):
        start = dict(self.n)
        with self.eng.Fori(0, rounds) as i:
            self.loops.append((i, per))
            yield i
            self.loops.pop()
        did = {k: v - start.get(k, 0) for k, v in self.n.items() if v != start.get(k, 0)}
        assert did == per, f"one round adds {did}"
        for k, v in per.items():
            self.n[k] += v * (rounds - 1)


def build(nc, stream, x_t, p_t, small, vecs, tab1, tab_a, tab_b, consts, out):
    n_units = stream.shape[0]
    with ExitStack() as ctx:
        place = [16512]

        def at(name, shape, dt=F32, offset=None):
            size = int(np.prod(shape[1:])) * 4
            if offset is None:
                offset = place[0]
                place[0] += (size + 31) // 32 * 32
            return nc.alloc_sbuf_tensor_at(name, shape, dt, offset=offset)

        def sem(name):
            s = ctx.enter_context(nc.semaphore(name))
            return s

        h = at("h", [P, DC, S])
        x_at = place[0]
        x = at("x", [P, DC, 2, S], F32R)
        y_at = place[0]
        y = at("y", [P, DC, S])
        px = at("px", [P, 2, 2, S], F32R, offset=x_at + 6 * 2 * S * 4)
        raw = [at(f"raw{i}", [P, UNIT]) for i in range(4)]
        wh = [at(f"wh{i}", [P, UNIT], F32R) for i in range(2)]
        wl = [at(f"wl{i}", [P, UNIT], F32R) for i in range(2)]
        pf = at("pf", [P, 2, S], offset=place[0])
        sq = [at(f"sq{i}", [P, S]) for i in range(2)]
        tmp = [at(f"tmp{i}", [P, S]) for i in range(2)]
        prod = [at(f"prod{i}", [P, S]) for i in range(2)]
        acc = at("acc", [P, S])
        rs = at("rs", [P, S])
        rs_in = at("rs_in", [P, S])
        ident = at("ident", [P, P])
        ones = at("ones", [P, P])
        vec = at("vec", [P, V_N])
        mix_at = place[0]
        mid = at("mid", [P, FF2C, 2, S], F32R)
        assert place[0] <= 229368, place[0]

        o = mix_at
        proj = at("proj", [P, N_PROJ, S], offset=o); o += N_PROJ * S * 4
        sm = at("sm", [P, SM_W], offset=o); o += SM_W * 4
        tb1 = at("tb1", [P, T_N], offset=o); o += T_N * 4
        xp = at("xp", [P, 32, 32], offset=o)
        vtok = at("vtok", [P, QT, 2, P], offset=o); o += QT * 2 * P * 4
        s1_at = o
        assert s1_at + 1056 * 4 <= mix_at + FF2C * 2 * S * 4, (s1_at - mix_at)
        gt = [at(f"gt{i}", [P, 2, S], offset=a_)
              for i, a_ in enumerate((y_at, s1_at, y_at + 4096))]
        at_gla = at("at_gla", [P, QT, 6, P], offset=y_at)
        st_gla = at("st_gla", [P, 8, 2, HD], offset=y_at + QT * 6 * P * 4)
        pt1 = [at(f"pt1_{i}", [P, 9 * P], offset=y_at + i * 9 * P * 4) for i in range(2)]
        sc1 = [at(f"sc1_{i}", [P, 1056], offset=a_)
               for i, a_ in enumerate((y_at + 18 * P * 4, s1_at, mix_at + GQ * S * 4))]
        win = at("win", [P, S], offset=s1_at + 1056 * 4 + 320)
        kc_c = at("kc_c", [P, 32], offset=s1_at + 1056 * 4 + 320 + QT * P * 4)
        vc_c = at("vc_c", [32, P], offset=s1_at + 1056 * 4 + 320 + QT * P * 4 + 128)
        hid = at("hid", [P, 2, 32], offset=s1_at + 1056 * 4 + 320 + QT * P * 4 + 640)
        gate_c = at("gate_c", [P, QT, 18], offset=s1_at + 1056 * 4)
        cmpb = at("cmpb", [P, 2], offset=s1_at + 1056 * 4 + 288)
        diag1 = [at(f"diag1_{i}", [P, 3, P], offset=a_)
                 for i, a_ in enumerate((s1_at + 1056 * 4 + 320, y_at + 18 * P * 4 + 1056 * 4))]
        assert s1_at + 1056 * 4 + 320 + QT * P * 4 + 896 <= mix_at + FF2C * 2 * S * 4
        o = mix_at
        aq = at("aq", [P, 9, S], offset=o); o += 9 * S * 4
        av = at("av", [P, QT, 3, P], offset=o); o += QT * 3 * P * 4
        tba = at("tba", [P, A_N], offset=o); o += A_N * 4
        sca = [at(f"sca{i}", [P, 6 * P], offset=o + i * 6 * P * 4) for i in range(3)]; o += 18 * P * 4
        pta = [at(f"pta{i}", [P, 6 * P], offset=o + i * 6 * P * 4) for i in range(2)]; o += 12 * P * 4
        diaga = [at(f"diaga{i}", [P, 3, P], offset=o + i * 3 * P * 4) for i in range(2)]; o += 6 * P * 4
        ao = at("ao", [P, 4, 2, S], F32R, offset=o); o += 4 * 2 * S * 4
        assert o <= mix_at + FF2C * 2 * S * 4
        o = mix_at
        bk = at("bk", [P, 6, S], offset=o); o += 6 * S * 4
        bv = at("bv", [P, QT, P], offset=o); o += QT * P * 4
        tbb = at("tbb", [P, B_N], offset=o); o += B_N * 4
        scb = [at(f"scb{i}", [P, 3 * P], offset=o + i * 3 * P * 4) for i in range(3)]; o += 9 * P * 4
        ptb = [at(f"ptb{i}", [P, 3 * P], offset=o + i * 3 * P * 4) for i in range(2)]; o += 6 * P * 4
        diagb = [at(f"diagb{i}", [P, 3, P], offset=o + i * 3 * P * 4) for i in range(2)]; o += 6 * P * 4
        bo = at("bo", [P, DC, 2, S], F32R, offset=o); o += DC * 2 * S * 4
        assert o <= mix_at + FF2C * 2 * S * 4
        emb = at("emb", [P, DC, S], offset=mix_at)
        mx = at("mx", [P, 2, QT, 4])
        negm = at("negm", [P, 2, 3, QT])
        den = at("den", [P, 2, 3, QT])
        rden = at("rden", [P, 2, 3, QT])
        esink = at("esink", [P, 2, QT])
        nsink = at("nsink", [P, 16])
        eps = at("eps", [P, 2])
        assert place[0] <= 229368, place[0]

        bank = [ctx.enter_context(nc.psum_tensor(f"bank{i}", [P, S], F32)) for i in range(8)]

        raw_in = [sem(f"raw_in{i}") for i in range(4)]
        hi_done = sem("hi_done")
        split_done = sem("split_done")
        unit_done = sem("unit_done")
        bank_free = [sem("bank_free0"), sem("bank_free1")]
        relu_done = sem("relu_done")
        mid_hi, mid_ready = sem("mid_hi"), sem("mid_ready")
        sq_done, acc_done = sem("sq_done"), sem("acc_done")
        z_added = sem("z_added")
        gate_made, pair_made = sem("gate_made"), sem("pair_made")
        stat_done = sem("stat_done")
        centred, sq_made, sq_used = sem("centred"), sem("sq_made"), sem("sq_used")
        rstd_ready, normed, affine = sem("rstd_ready"), sem("normed"), sem("affine")
        x_hi, x_ready = sem("x_hi"), sem("x_ready")
        part_made, h_ready = sem("part_made"), sem("h_ready")
        consts_in = sem("consts_in")
        h_in = [sem(f"h_in{i}") for i in range(4)]
        tab_in, sm_in, p_in = sem("tab_in"), sem("sm_in"), sem("p_in")
        dve_step, act_step, pool_step = sem("dve_step"), sem("act_step"), sem("pool_step")
        rot_done, rope_used, rope_done = sem("rot_done"), sem("rope_used"), sem("rope_done")
        turned, turn_read = sem("turned"), sem("turn_read")
        z_done, gk_act, gk_done = sem("z_done"), sem("gk_act"), sem("gk_done")
        gla_exp, gla_kend = sem("gla_exp"), sem("gla_kend")
        ds_done, st_done = sem("ds_done"), sem("st_done")
        am_done, am_read = sem("am_done"), sem("am_read")
        go_done, go_copied, go_sq, go_stat = sem("go_done"), sem("go_copied"), sem("go_sq"), sem("go_stat")
        go_silu, go_out = sem("go_silu"), sem("go_out")
        mx_hi = sem("mx_hi")
        pooled, pool_mm, pool_read = sem("pooled"), sem("pool_mm"), sem("pool_read")
        cmp_in = sem("cmp_in")
        cmp_mm, cmp_bias, cmp_hid, cmp_out, cmp_ready = (
            sem("cmp_mm"), sem("cmp_bias"), sem("cmp_hid"), sem("cmp_out"), sem("cmp_ready"))
        gate_exp = sem("gate_exp")
        scored, score_read = sem("scored"), sem("score_read")
        max_ready, exp_done = sem("max_ready"), sem("exp_done")
        blk_turned = sem("blk_turned")
        blk_read = [sem("blk_read0"), sem("blk_read1")]
        diag_ready, o_done = sem("diag_ready"), sem("o_done")
        ot_hi, ot_ready = sem("ot_hi"), sem("ot_ready")
        sink_exp = sem("sink_exp")
        p_hi, p_ready, emb_read = sem("p_hi"), sem("p_ready"), sem("emb_read")
        sig_done = sem("sig_done")
        out_done = sem("out_done")

        def gv_t(rows, t, head):
            return proj[rows, GV + head // 2, t * P + head % 2 * HD:t * P + head % 2 * HD + HD]

        def jobs_nsa():
            for c in range(3):
                for g in range(2):
                    r = slice(g * HD, g * HD + HD)
                    for t in range(QT):
                        n = (t + 1) * P
                        q = proj[r, Q0 + c, t * P:t * P + P]
                        caus = tb1[:, T_CAUS + (QT - 1 - t) * P:T_CAUS + QT * P]
                        yield dict(kind="nsa", t=t, g=g, head=g * 3 + c, segs=[
                            ([(q, kc_c[r, 0:N_CMP])], tb1[:, T_CMP + t * 32:T_CMP + t * 32 + N_CMP],
                             [vc_c[0:N_CMP, r]], 0),
                            ([(q, proj[r, KS, 0:n])], caus, [vtok[:, k, 0, r] for k in range(t + 1)], 1),
                            ([(q, proj[r, KW, 0:n])], caus, [vtok[:, k, 1, r] for k in range(t + 1)], 2)])

        def jobs_a():
            for g in range(2):
                r = slice(g * HD, g * HD + HD)
                for t in range(QT):
                    ts = slice(t * P, t * P + P)
                    yield dict(kind="a", t=t, g=g, head=g, segs=[
                        ([(aq[r, 0, ts], aq[r, 3, :])], tba[:, A_M0 + t * S:A_M0 + t * S + S],
                         [av[:, k, 0, r] for k in range(QT)], 0),
                        ([(aq[r, 1, ts], aq[r, 4, ts]), (aq[r, 2, ts], aq[r, 5, ts])], tba[:, A_M1:A_M1 + 2 * P],
                         [av[:, t, 1, r], av[:, t, 2, r]], 0)])

        def jobs_b(c4):
            for c in range(4):
                for g in range(2):
                    r = slice(g * HD, g * HD + HD)
                    for t in range(QT):
                        lo, hi = max(t - 1, 0), min(t + 2, QT)
                        yield dict(kind="b", t=t, g=g, head=8 * c4 + 4 * g + c, segs=[
                            ([(bk[r, 2 + c, t * P:t * P + P], bk[r, 0, lo * P:hi * P])],
                             tbb[:, B_M + (lo - t + 1) * P:B_M + (hi - t + 1) * P],
                             [bv[:, k, r] for k in range(lo, hi)], 0)])

        def width(seg):
            return sum(k.shape[-1] for _, k in seg[0])

        def spans(job):
            off, out_ = 0, []
            for seg in job["segs"]:
                w = width(seg)
                out_.append((off, w, [(off + j * P, min(P, w - j * P)) for j in range(len(seg[2]))]))
                off += max(w, 32)
            return out_

        def blocks(job):
            b = [(si, j, o_, w) for si, (_, _, tiles_) in enumerate(spans(job)) for j, (o_, w) in enumerate(tiles_)]
            return [b[i:i + 4] for i in range(0, len(b), 4)]

        def pair_done(j):
            return j and j % 8 == 0

        def outs_a(pair):
            view = [ao[:, pair, e, :].rearrange("p (j c r) -> p j c r", c=4, r=4) for e in range(2)]
            return (*view, True)

        def outs_b(c4):
            return [(bo[:, c4 * 4 + k, 0, :], bo[:, c4 * 4 + k, 1, :], False) for k in range(4)]

        def in_order(out_, src):
            return src.rearrange("p (r c j) -> p j c r", r=4, c=4) if out_[2] else src

        def o_bank(job, pair):
            return bank[((7, 0) if job["kind"] == "nsa" else (7, 4))[pair % 2]]

        block = ctx.enter_context(nc.Block())

        @block.sync
        def _(sp):
            c = Count(sp)

            def load(k, wait=True):
                if wait:
                    sp.wait_ge(split_done, c.at("unit", back=3))
                sp.dma_start(raw[k % 4][:, :], stream[c.at("unit"), :, :]).then_inc(raw_in[k % 4], 16)
                c.tick("unit")

            for k in range(4):
                if k == 1:
                    sp.wait_ge(h_in[2], 16)
                load(k, False)
            rounds = (n_units - 4) // 4
            with c.loop(rounds, unit=4):
                for k in range(4):
                    load(k)
            for k in range((n_units - 4) % 4):
                load(k)
            for k in range(DC):
                sp.wait_ge(h_ready, 7 * DC + k + 1)
                sp.dma_start(out[k], h[:, k, :]).then_inc(out_done, 16)
            sp.wait_ge(out_done, 16 * DC)

        @block.gpsimd
        def _(pool):
            c = Count(pool)
            pool.dma_start(ident[:, :], consts[0]).then_inc(consts_in, 16)
            pool.dma_start(ones[:, :], consts[1]).then_inc(consts_in, 16)
            pool.dma_start(vec[:, :], vecs).then_inc(consts_in, 16)
            pool.memset(eps[:, 0:1], LN_EPS).then_inc(pool_step, 1)
            pool.memset(eps[:, 1:2], RMS_EPS).then_inc(pool_step, 1)
            c.tick("pool_step", 2)

            def acc_read():
                k = c.n.get("stats", 0)
                if k:
                    pool.wait_ge(stat_done, k)
                c.tick("stats")

            def square_sums():
                acc_read()
                pool.memset(acc[:, :], 0.0).then_inc(acc_done, 1)
                c.wait(acc_done)
                for m in range(DC - 1):
                    c.wait(sq_done)
                    pool.tensor_tensor(acc[:, :], acc[:, :], sq[m % 2][:, :], ALU.add).then_inc(acc_done, 1)
                    c.wait(acc_done)
                c.tick("sq_done")

            def z_sums():
                acc_read()
                for m in range(DC - 1):
                    b = c.next_tile()
                    if m:
                        pool.wait_ge(bank_free[b], c.at(f"used{b}"))
                        if m == 1:
                            pool.wait_ge(bank_free[1 - b], c.at(f"used{1 - b}"))
                        pool.tensor_tensor(acc[:, :], h[:, 0, :] if m == 1 else acc[:, :], h[:, m, :],
                                           ALU.add).then_inc(z_added, 1)
                        c.wait(z_added)
                c.next_tile()

            def link(ins):
                ins.then_inc(pool_step, 1)
                c.wait(pool_step)

            def window_sums():
                a, b = acc[:, :], rs_in[:, :]
                for k in range(2):
                    t = c.next_tile()
                    pool.wait_ge(bank_free[t], c.at(f"used{t}"))
                    if k == 0:
                        c.wait(tab_in, 16)
                    src = proj[:, PU + k, :]
                    cur, nxt, w, res = src, a, 1, {}
                    for _ in range(2 + 2 * k):
                        pool.tensor_copy(nxt[:, 0:w], cur[:, 0:w])
                        link(pool.tensor_tensor(nxt[:, w:S], cur[:, w:S], cur[:, 0:S - w], ALU.add))
                        w *= 2
                        res[w] = nxt
                        cur, nxt = nxt, b if nxt is a else a
                    for e in range(2):
                        r = slice(e * HD, e * HD + HD)
                        ins = pool.tensor_tensor(win[r, :], res[(2, 4, 8, 16)[2 * k + e]][r, :],
                                                 tb1[r, T_ICNT + k * S:T_ICNT + k * S + S], ALU.mult)
                    link(ins)
                    pool.tensor_tensor(src, win[:, :], src, ALU.subtract).then_inc(pooled, 1)
                    c.wait(pooled)

            def add_parts():
                for m in range(DC):
                    c.wait(part_made)
                    pool.tensor_tensor(h[:, m, :], h[:, m, :], prod[m % 2][:, :], ALU.add).then_inc(h_ready, 1)

            def after(units_):
                pool.wait_ge(unit_done, units_)

            ffn, ple = 2 * FF2C + 3 * DC, 2 + DC
            u = 0
            for layer in range(DEPTH):
                if layer:
                    after(u)
                else:
                    pool.wait_ge(raw_in[1], 16)
                pool.dma_start(sm[:, :], small[layer]).then_inc(sm_in, 16)
                pool.dma_start(tb1[:, :], tab1).then_inc(tab_in, 16)
                u += N_PROJ + DC + 8 * DC
                c.skip_tiles(ORDER.index(PU))
                window_sums()
                c.skip_tiles(N_PROJ - ORDER.index(PU) - 2)
                z_sums()
                c.skip_tiles(16 + DC + 16)
                z_sums()
            for layer in range(DEPTH):
                square_sums()
                add_parts()
                u += ffn
                after(u)
                if layer == 0:
                    pool.dma_start(tba[:, :], tab_a).then_inc(tab_in, 16)
                else:
                    pool.dma_start(tbb[:, :], tab_b).then_inc(tab_in, 16)
                square_sums()
                add_parts()
                u += (40, 20)[layer]
                pool.wait_ge(sq_used, DC * (2 * DEPTH + 4 * layer + 3))
                pool.dma_start(pf[:, :, :], p_t[layer].rearrange("(c p) t -> p c t", p=P)).then_inc(p_in, 16)
                square_sums()
                add_parts()
                u += ffn + ple
                square_sums()
                add_parts()
            assert u == n_units, (u, n_units)

        @block.tensor
        def _(pe):
            c = Count(pe)

            def unit(bk_, cols, src, chunks, start, stop, last=True, ready=None, also=None):
                u = c.n.get("unit", 0) % 2
                for j, (col, kc) in enumerate(zip(cols, chunks)):
                    if ready is not None:
                        c.wait(ready)
                    if also is not None and j:
                        also(j - 1)
                    hi = wh[u][:, col:col + P]
                    lo = wl[u][:, col:col + P]
                    pe.matmul(bk_[:, :], hi, src[:, kc, 0, :], start=start and j == 0, stop=False)
                    pe.matmul(bk_[:, :], hi, src[:, kc, 1, :], start=False, stop=False)
                    mm = pe.matmul(bk_[:, :], lo, src[:, kc, 0, :], start=False, stop=stop and j == len(cols) - 1)
                if last:
                    mm.then_inc(unit_done, 1)
                    c.tick("unit")
                if also is not None:
                    also(len(cols) - 1)

            def tile(src, spread=(range(8),), ready=None, also=None):
                t = c.next_tile()
                if c.n[f"used{t}"] > 1:
                    pe.wait_ge(bank_free[t], c.at(f"used{t}", back=1))
                for n, chunks in enumerate(spread):
                    pe.wait_ge(split_done, c.at("unit") + 1)
                    unit(bank[t], [kc % 8 * P for kc in chunks], src, chunks, n == 0, n == len(spread) - 1,
                         ready=ready, also=also)

            def tiles_of(n, per, src, spread=(range(8),), ready=None, also=None):
                for k in range(per):
                    tile(src, spread, *((ready, also) if k == 0 else ()))
                with c.loop(n // per - 1, unit=per * len(spread), **(TILES4 if per == 4 else TILES2)):
                    for k in range(per):
                        tile(src, spread)

            def read_all():
                for t in range(2):
                    pe.wait_ge(bank_free[t], c.at(f"used{t}"))
                if c.n.get("pairs", 0):
                    pe.wait_ge(ot_ready, c.n["pairs"])

            def stat(added, n, last, made=None):
                c.wait(added, n)
                pe.matmul(bank[2][:, :], ones[:, :], acc[:, :], start=True, stop=False)
                if made is None:
                    read_all()
                else:
                    c.wait(made, DC)
                pe.matmul(bank[2][:, :], ones[:, :], last, start=False, stop=True).then_inc(stat_done, 1)

            def stat_z():
                stat(z_added, DC - 2, h[:, DC - 1, :])

            def stat_sq():
                stat(acc_done, DC, sq[1][:, :], sq_done)

            def square_sum(k):
                c.wait(sq_made)
                pe.matmul(bank[3][:, :], ones[:, :], sq[k % 2][:, :], start=k == 0,
                          stop=k == DC - 1).then_inc(sq_used, 1)

            def stat_chunks():
                for k in range(DC):
                    square_sum(k)

            def rope(ap, rot, waited=False, banks=(2, 3)):
                if not waited:
                    b = c.n["tile"] % 2
                    pe.wait_ge(bank_free[b], c.at(f"used{b}"))
                n = len(banks)
                if c.n.get("rope", 0) >= n:
                    pe.wait_ge(rope_used, c.at("rope", back=n - 1))
                pe.matmul(bank[banks[c.n.get("rope", 0) % n]][:, :], rot, ap, start=True, stop=True).then_inc(rot_done, 1)
                c.tick("rope")

            def turn(groups, banks=(4, 5)):
                for g in groups:
                    k, n = c.n.get("turn", 0), len(banks)
                    if k >= n:
                        pe.wait_ge(turn_read, c.at("turn", back=n - 1))
                    for i, (dst, src) in enumerate(g):
                        mm = pe.transpose(dst(bank[banks[k % n]]), src, ident[:src.shape[0], :src.shape[0]])
                    mm.then_inc(turned, 1)
                    c.tick("turn")

            def turn_chunk(ap, back, banks=(4, 5)):
                b = (c.n["tile"] - 1 - back) % 2
                pe.wait_ge(bank_free[b], c.at(f"used{b}"))
                turn([[(lambda b, i=i: b[:, i * P:i * P + P], ap[:, i * P:i * P + P]) for i in range(QT)]], banks)

            def attend(jobs, sc, pt, diag, last_turns=None):
                jobs = list(jobs)

                def scores(j):
                    for si, seg in enumerate(jobs[j]["segs"]):
                        n = c.n.get("scored", 0)
                        key = f"bank_seg{si}"
                        if c.n.get(key, 0):
                            pe.wait_ge(score_read, c.n[key])
                        at_ = 0
                        for q, k in seg[0]:
                            w = k.shape[-1]
                            mm = pe.matmul(bank[2 + si][:, at_:at_ + w], q, k, start=True, stop=True, skip_group_check=True)
                            at_ += w
                        mm.then_inc(scored, 1)
                        c.tick("scored")
                        c.n[key] = n + 1

                def bank_of_group():
                    b = c.n.get("blk", 0) % 2
                    if c.n.get(f"blk{b}", 0):
                        pe.wait_ge(blk_read[b], c.n[f"blk{b}"])
                    c.tick("blk")
                    c.tick(f"blk{b}")
                    return bank[5 + b]

                def turns(j):
                    job = jobs[j]
                    c.wait(diag_ready)
                    for grp in blocks(job):
                        dst = bank_of_group()
                        for i, (si, t_, off, w) in enumerate(grp):
                            mm = pe.matmul(dst[0:w, i * P:i * P + P], sc[j % 3][:, off:off + w],
                                           diag[j % 2][:, job["segs"][si][3], :], start=True, stop=True)
                        mm.then_inc(blk_turned, 1)
                    return c.n.get("blk0", 0), c.n.get("blk1", 0)

                def values(j, copied):
                    job = jobs[j]
                    pe.wait_ge(blk_read[0], copied[0])
                    if copied[1]:
                        pe.wait_ge(blk_read[1], copied[1])
                    pair = c.n.get("o", 0) // 8
                    if c.n.get("o", 0) % 8 == 0 and pair >= 2:
                        pe.wait_ge(ot_ready, pair - 1)
                    r = slice(job["g"] * HD, job["g"] * HD + HD)
                    dst = o_bank(job, pair)[r, job["t"] * P:job["t"] * P + P]
                    flat = [x_ for g in blocks(job) for x_ in g]
                    for p_, (si, t_, off, w) in enumerate(flat):
                        mm = pe.matmul(dst, job["segs"][si][2][t_], pt[j % 2][0:w, p_ * P:p_ * P + P],
                                       start=p_ == 0, stop=p_ == len(flat) - 1, skip_group_check=True)
                    mm.then_inc(o_done, 1)
                    c.tick("o")

                scores(0)
                scores(1)
                if last_turns is not None:
                    last_turns()
                    pe.wait_ge(turn_read, c.n["turn"])
                copied = {0: turns(0)}
                n_jobs = len(jobs)
                for j in range(n_jobs):
                    if j + 2 < n_jobs:
                        scores(j + 2)
                    values(j, copied[j])
                    if j + 1 < n_jobs:
                        copied[j + 1] = turns(j + 1)
                c.tick("pairs", n_jobs // 8)

            def ds():
                for n in range(8):
                    t, half = n // 2, n % 2
                    r = slice(half * 64, half * 64 + 64)
                    for hh in range(6):
                        gi, q = hh // 4, hh % 4
                        mm = pe.matmul(bank[(2, 3, 6, 7)[half * 2 + gi]][q * 32:q * 32 + 32, n // 2 * HD:n // 2 * HD + HD],
                                       gt[2][r, :, :].rearrange("p a s -> p (a s)")[:, t * 192 + hh * 32:t * 192 + hh * 32 + 32],
                                       gv_t(r, t, hh), start=True, stop=True, skip_group_check=True)
                mm.then_inc(ds_done, 1)

            def inside(t):
                ts = slice(t * P, t * P + P)
                for hh in range(6):
                    r = slice(hh % 4 * 32, hh % 4 * 32 + 32)
                    mm = pe.matmul(bank[(2, 3, 6, 7)[hh % 4]][:, hh // 4 * P:hh // 4 * P + P],
                                   gt[1][r, hh // 4, ts], proj[r, (GQ, GQX)[hh // 4], ts],
                                   start=True, stop=True, skip_group_check=True)
                mm.then_inc(am_done, 1)

            def gla_out(cc):
                for e in range(2):
                    hh = 2 * cc + e
                    r = slice(hh % 4 * 32, hh % 4 * 32 + 32)
                    for t in range(QT):
                        dst = bank[2 + e][e * HD:e * HD + HD, :]
                        pe.matmul(dst[:, t * P:t * P + P], gv_t(slice(0, P), t, hh), at_gla[:, t, hh, :],
                                  start=True, stop=False, skip_group_check=True)
                        for n in (2 * t, 2 * t + 1):
                            mm = pe.matmul(dst[:, n * 64:n * 64 + 64], st_gla[r, n, hh // 4, :],
                                           proj[r, (GQ, GQX)[hh // 4], n * 64:n * 64 + 64],
                                           start=False, stop=n % 2 == 1, skip_group_check=True)
                mm.then_inc(go_done, 1)

            def prepare(k):
                b = c.n["tile"] % 2
                pe.wait_ge(bank_free[b], c.at(f"used{b}"))
                if k == 2:
                    c.wait(sm_in, 16)
                    for i, (a, b) in enumerate(((0, 128), (128, 192))):
                        pe.matmul(bank[6 + i][0:b - a, :], sm[GLR_ROW:GLR_ROW + 16, SM_G2 + a:SM_G2 + b],
                                  proj[GLR_ROW:GLR_ROW + 16, GQX, :], start=True, stop=True).then_inc(z_done, 1)
                if k == 12:
                    pe.wait_ge(turn_read, c.n["turn"])
                    ds()
                if k == 13:
                    c.wait(st_done)
                if k == 17:
                    c.wait(am_read)
                if 13 <= k < 17:
                    if k > 13:
                        c.wait(am_read)
                    inside(k - 13)
                if 18 <= k:
                    c.wait(go_sq)
                    pe.matmul(bank[6][:, :], tb1[:, T_B64:T_B64 + P], sq[0][:, :], start=True, stop=True).then_inc(go_stat, 1)
                if 17 <= k < 20:
                    if k > 17:
                        c.wait(go_copied)
                    gla_out(k - 17)
                if k in (14, 16):
                    kind = (k - 14) // 2
                    if kind == 0:
                        pe.wait_ge(rope_used, c.n["rope"])
                    c.wait(cmp_in)
                    for j in range(32):
                        for g in range(2):
                            r = slice(g * HD, g * HD + HD)
                            mm = pe.matmul(bank[5][r, kind * 32:kind * 32 + 32],
                                           sm[r, SM_W1 + kind * 2048 + j * HD:SM_W1 + kind * 2048 + j * HD + HD],
                                           xp[r, j, :], start=j == 0, stop=j == 31, skip_group_check=True)
                    mm.then_inc(cmp_mm, 1)
                if k == 19:
                    c.wait(cmp_hid)
                    for g in range(2):
                        r = slice(g * HD, g * HD + HD)
                        pe.matmul(bank[7][r, 0:N_CMP], sm[r, SM_W2:SM_W2 + HD], hid[r, 0, 0:N_CMP], start=True, stop=True, skip_group_check=True)
                        mm = pe.matmul(bank[(7, 5)[g]][0:N_CMP, P:P + HD], hid[r, 1, 0:N_CMP], sm[r, SM_W2 + HD:SM_W2 + 2 * HD], start=True, stop=True, skip_group_check=True)
                    mm.then_inc(cmp_out, 1)
                if k == 20:
                    c.wait(cmp_ready)
                if k in ROPED:
                    if k == 5:
                        c.wait(tab_in, 16)
                    rope(proj[:, ROPED[k], :], tb1[:, T_ROT:T_ROT + P], True, (5,))
                if k in TURNED:
                    ch = TURNED[k]
                    if ch == GK:
                        c.wait(gla_kend)
                    w = 64 if ch == GKX else P
                    turn([[(lambda b, i=i: b[:, i * w:i * w + w], proj[0:w, ch, i * P:i * P + P]) for i in range(QT)]], (4,))

            def pool_mix():
                for k in range(2):
                    c.wait(pooled)
                    for e in range(2):
                        r = slice(e * HD, e * HD + HD)
                        mm = pe.matmul(bank[6 + k][r, :], sm[r, SM_PW + k * HD:SM_PW + k * HD + HD], proj[r, PU + k, :],
                                       start=True, stop=True)
                    mm.then_inc(pool_mm, 1)

            for layer in range(DEPTH):
                tile(x, ready=x_ready)
                if layer == 0:
                    c.wait(consts_in, 48)
                for k in range(1, N_PROJ):
                    tile(x)
                    prepare(k)
                c.wait(go_copied)
                c.wait(rope_done, 6)
                pe.wait_ge(turn_read, c.n["turn"])

                def last_turns():
                    turn_chunk(proj[:, VW, :], 0, (5,))
                    read_all()
                    c.wait(go_out, 3)
                    pool_mix()
                    c.wait(pool_read, 2)
                attend(jobs_nsa(), sc1, pt1, diag1, last_turns)
                c.wait(x_ready, 5)
                read_all()
                with c.loop(2, unit=4, **TILES4):
                    for k in range(4):
                        tile(x)
                stat_z()
                stat_chunks()
                for half in range(2):
                    tiles_of(16, 4, x, ready=None if half else x_ready)
                    tiles_of(8, 2, mid, (range(0, 8), range(8, 16)), ready=mid_ready)
                stat_z()
                stat_chunks()

            def ffn2():
                tiles_of(2 * FF2C, 4, x, ready=x_ready, also=square_sum)
                tiles_of(8, 2, mid, (range(0, 8), range(8, 16), range(16, FF2C)), ready=mid_ready)

            for layer in range(DEPTH):
                ffn2()
                stat_sq()
                first = dict(ready=x_ready, also=square_sum)
                if layer == 0:
                    for pair in range(4):
                        for k in range(9):
                            tile(x, **(first if pair == k == 0 else {}))
                            if pair == 0 and k == 1:
                                c.wait(tab_in, 16)
                            if 1 <= k < 7:
                                rope(aq[:, k - 1, :], tba[:, A_ROT:A_ROT + P])
                            if k >= 7:
                                pe.wait_ge(ot_ready, c.n.get("pairs", 0))
                                turn_chunk(aq[:, k - 1, :], 1)
                        c.wait(rope_done, 6)
                        attend(jobs_a(), sca, pta, diaga, lambda: turn_chunk(aq[:, 8, :], 0))
                    read_all()
                    for n in range(4):
                        pe.wait_ge(split_done, c.at("unit") + 1)
                        if n >= 2:
                            c.wait(emb_read, 2)
                        for j in range(2):
                            unit(bank[n % 2 * 2 + j], [j * 512 + q * P for q in range(4)], ao, range(4), True, True, last=j == 1)
                    c.wait(emb_read, 4)
                else:
                    for c4 in range(2):
                        for k in range(6):
                            tile(x, **(first if c4 == k == 0 else {}))
                            if c4 == 0 and k == 1:
                                c.wait(tab_in, 16)
                            if k in (1, 3, 4, 5):
                                rope(bk[:, k - 1, :], tbb[:, B_ROT:B_ROT + P])
                            if k == 2:
                                pe.wait_ge(ot_ready, c.n.get("pairs", 0))
                                turn_chunk(bk[:, 1, :], 1)
                        read_all()
                        rope(bk[:, 5, :], tbb[:, B_ROT:B_ROT + P], True)
                        c.wait(rope_done, 4)
                        c.tick("rope_done")
                        pe.wait_ge(rope_used, c.n["rope"])
                        attend(jobs_b(c4), scb, ptb, diagb, lambda: pe.wait_ge(rope_done, c.n["rope_done"]))
                    read_all()
                    with c.loop(2, unit=4, **TILES4):
                        for k in range(4):
                            tile(bo)
                stat_sq()
                ffn2()
                read_all()
                c.wait(p_ready, 2)
                for n in range(2):
                    pe.wait_ge(split_done, c.at("unit") + 1)
                    if n == 1:
                        c.wait(emb_read, 4)
                    for j in range(4):
                        unit(bank[4 + j], [j * 256, j * 256 + P], px, range(2), True, True, last=j == 3)
                    if n == 0:
                        stat_sq()
                tiles_of(8, 2, x, ready=x_ready, also=square_sum)
                c.wait(emb_read, 4)
                stat_sq()

        @block.scalar
        def _(act):
            c = Count(act)

            def split(last=False):
                if last:
                    return
                n = c.n.get("split", 0)
                act.wait_ge(raw_in[n % 4], c.at("split", back=-1, div=4, mult=16))
                if n >= 2:
                    act.wait_ge(unit_done, c.at("split", back=1))
                act.activation(wh[n % 2][:, :], raw[n % 4][:, :], ACT.Copy).then_inc(hi_done, 1)
                c.tick("split")

            def units(n, last=False):
                for k in range(n):
                    if c.n.get("early", 0):
                        c.n["early"] -= 1
                    else:
                        split(last and k == n - 1)
                c.wait(unit_done, n)

            def split_early():
                split()
                c.tick("early")

            def link(ins):
                ins.then_inc(act_step, 1)
                c.wait(act_step)

            def rstd(src, e, dst=rs):
                link(act.activation(dst[:, :], src, ACT.Ln, bias=eps[:, e:e + 1]))
                act.activation(dst[:, :], dst[:, :], ACT.Exp, scale=-0.5).then_inc(rstd_ready, 1)

            def square(k):
                n = c.n.get("sqm", 0)
                if n >= 2:
                    act.wait_ge(sq_used, n - 1)
                act.activation(sq[k % 2][:, :], h[:, k, :], ACT.Square).then_inc(sq_made, 1)
                c.tick("sqm")

            def layer_norm(g, b, to_x, after=None):
                c.tick("stat_done")
                for k in range(DC):
                    c.wait(centred)
                    square(k)
                c.wait(sq_used, DC)
                rstd(bank[3][:, :], 0)
                for k in range(DC):
                    c.wait(normed)
                    bias = vec[:, b + k:b + k + 1]
                    if to_x:
                        act.activation(x[:, k, 0, :], prod[k % 2][:, :], ACT.Identity, bias=bias)
                        c.tick("affine")
                    act.activation(h[:, k, :], prod[k % 2][:, :], ACT.Identity, bias=bias).then_inc(affine, 1)
                    if to_x and k == 3:
                        split_early()
                    if after is not None:
                        after(k)

            def pre_chunk(g, k, ready, early=(4,)):
                c.wait(ready)
                act.activation(x[:, k, 0, :], h[:, k, :], ACT.Copy, scale=vec[:, g + k:g + k + 1]).then_inc(x_hi, 1)
                square(k)
                if k in early:
                    split_early()

            def rms_pre(g, ready, early=(4,)):
                for k in range(DC):
                    pre_chunk(g, k, ready, early)
                c.wait(sq_used, DC)
                rstd(bank[3][:, :], 1, rs_in)

            def rms_post():
                c.wait(stat_done)
                rstd(bank[2][:, :], 1)

            def tile_square(n, last=False):
                units(n, last)
                square_of(bank[c.next_tile()][:, :])

            def square_of(src):
                k = c.n.get("sqs", 0)
                act.wait_ge(acc_done, c.at("acc") + 1)
                act.activation(sq[k % 2][:, :], src, ACT.Square).then_inc(sq_done, 1)
                c.tick("sqs")
                c.tick("acc")

            def attend(jobs, sc, pt, outs, last_turns=None, later=None):
                jobs = list(jobs)

                def exps(j):
                    job = jobs[j]
                    n, t = c.n.get("job", 0) // 4 % 2, job["t"]
                    parts = {}
                    for seg, (off, w, _) in zip(job["segs"], spans(job)):
                        parts.setdefault(seg[3], []).append((off, off + w))
                    c.wait(max_ready)
                    for s_, p_ in sorted(parts.items()):
                        sl = sc[j % 3][:, p_[0][0]:p_[-1][1]]
                        act.activation(sl, sl, ACT.Exp, bias=negm[:, n, s_, t:t + 1], scale=0.125,
                                       accum_out=den[:, n, s_, t:t + 1]).then_inc(exp_done, 1)
                    if job["kind"] == "b":
                        act.activation(esink[:, n, t:t + 1], negm[:, n, 0, t:t + 1], ACT.Exp,
                                       bias=vec[:, V_SINK + job["head"]:V_SINK + job["head"] + 1]).then_inc(sink_exp, 1)
                    c.tick("job")

                def group():
                    c.tick("blk_turned")
                    c.tick("blk")
                    b = (c.n["blk"] - 1) % 2
                    return b if b == 0 or jobs[0]["kind"] != "nsa" else None

                def copies(j):
                    for gi, grp in enumerate(blocks(jobs[j])):
                        b = group()
                        if b is not None:
                            act.wait_ge(blk_turned, c.n["blk_turned"])
                            if c.n.get("o", 0) >= 2:
                                act.wait_ge(o_done, c.n["o"] - 1)
                            copy_group(pt[j % 2], gi, grp, bank[5 + b], blk_read[b])
                    c.tick("o")

                def pair_out(k):
                    c.wait(o_done, 8)
                    src = o_bank(jobs[0], c.n.get("pairs", 0))[:, :]
                    c.tick("pairs")
                    act.activation(outs[k][0], in_order(outs[k], src), ACT.Copy).then_inc(ot_hi, 1)

                exps(0)
                exps(1)
                if last_turns is not None:
                    last_turns()
                copies(0)
                n_jobs = len(jobs)
                for j in range(n_jobs):
                    if j + 2 < n_jobs:
                        exps(j + 2)
                    if j + 1 < n_jobs:
                        copies(j + 1)
                    if later is not None and j == 2:
                        later()
                    if pair_done(j):
                        pair_out(j // 8 - 1)
                pair_out(n_jobs // 8 - 1)

            def log_exp():
                act.preload_act_table_set("natural_log_exp_and_others")

            def copy_group(pt_, gi, grp, src, done):
                w0 = grp[0][3]
                first = 0 if w0 == P else P
                if len(grp) * P > first:
                    ins = act.activation(pt_[:, gi * 512 + first:gi * 512 + len(grp) * P], src[:, first:len(grp) * P], ACT.Copy)
                if first:
                    ins = act.activation(pt_[0:w0, 0:P], src[0:w0, 0:P], ACT.Copy)
                ins.then_inc(done, 1)

            for k in range(4):
                act.dma_start(h[:, 2 * k:2 * k + 2, :],
                              x_t[2 * k * P:2 * k * P + 2 * P].rearrange("(c p) t -> p c t", p=P)).then_inc(h_in[k], 16)
            log_exp()
            split()
            act.wait_ge(pool_step, 2)
            for k in range(DC):
                if k % 2 == 0:
                    act.wait_ge(h_in[k // 2], 16)
                act.activation(x[:, k, 0, :], h[:, k, :], ACT.Copy).then_inc(x_hi, 1)
            act.wait_ge(consts_in, 48)

            for layer in range(DEPTH):
                def prepare(k):
                    if k in (3, 4):
                        i, w = k - 3, (128, 64)[k - 3]
                        c.wait(z_done)
                        bg = V_BG + 2 * layer + i
                        link(act.activation(gt[0][0:w, i, :], bank[6 + i][0:w, :], ACT.Abs, bias=vec[0:w, bg:bg + 1]))
                        link(act.activation(gt[0][0:w, i, :], gt[0][0:w, i, :], ACT.Exp, scale=-1.0))
                        act.activation(gt[0][0:w, i, :], gt[0][0:w, i, :], ACT.Ln, bias=1.0).then_inc(gk_act, 1)
                    if k in (5, 6):
                        i, w = k - 5, (128, 64)[k - 5]
                        c.wait(gk_done)
                        act.activation(gt[2][0:w, i, :], gt[0][0:w, i, :], ACT.Exp, scale=1.0 / 16).then_inc(gla_exp, 1)
                        act.activation(gt[1][0:w, i, :], gt[0][0:w, i, :], ACT.Exp, scale=-1.0 / 16).then_inc(gla_exp, 1)
                    if k in (7, 8):
                        i, w = k - 7, (128, 64)[k - 7]
                        c.wait(gk_done)
                        act.activation(gt[0][0:w, i, :], gt[0][0:w, i, :], ACT.Exp, scale=1.0 / 16).then_inc(gla_exp, 1)
                    if k == 17:
                        c.wait(cmp_bias)
                        act.activation(hid[:, :, 0:N_CMP], sq[1][:, 64:128].rearrange("p (a n) -> p a n", a=2)[:, :, 0:N_CMP],
                                       ACT.Exp, scale=-2.0 * 0.7978845608028654).then_inc(gate_exp, 1)
                    if k >= 18:
                        c.wait(go_stat)
                        rstd(bank[6][:, :], 1)
                    if 17 <= k < 20:
                        if k > 17:
                            c.wait(go_out)
                        link(act.activation(prod[0][:, :], proj[:, GO + k - 17, :], ACT.Exp, scale=-1.0))
                        link(act.activation(prod[0][:, :], prod[0][:, :], ACT.Ln, bias=1.0))
                        act.activation(prod[0][:, :], prod[0][:, :], ACT.Exp, scale=-1.0).then_inc(go_silu, 1)
                        c.wait(go_copied)
                        act.activation(sq[0][:, :], tmp[0][:, :], ACT.Square).then_inc(go_sq, 1)
                    if k == 20:
                        c.wait(cmp_ready)
                        act.activation(gate_c[:, :, :], gate_c[:, :, :], ACT.Exp, scale=-1.0).then_inc(gate_exp, 1)

                def scale_pooled():
                    for k in range(2):
                        c.wait(pool_mm)
                        ps = V_PS + 2 * layer + k
                        act.activation(proj[:, PU + k, :], bank[6 + k][:, :], ACT.Copy, scale=vec[:, ps:ps + 1]).then_inc(pool_read, 1)

                def mixed_hi():
                    c.wait(pool_read, 2)
                    for m, ch in enumerate((GO, GO + 1, GO + 2, PU, PU + 1)):
                        act.activation(x[:, 3 + m, 0, :], proj[:, ch, :], ACT.Copy).then_inc(mx_hi, 1)

                for k in range(N_PROJ):
                    units(1)
                    c.next_tile()
                    prepare(k)
                c.wait(go_out)
                attend(jobs_nsa(), sc1, pt1, [(x[:, k, 0, :], x[:, k, 1, :], False) for k in range(3)],
                       scale_pooled, mixed_hi)
                with c.loop(2, split=4, unit_done=4, **TILES4):
                    for k in range(4):
                        units(1)
                        c.next_tile()
                layer_norm(V_LN + 32 * layer, V_LN + 32 * layer + 8, True)
                def up4(i):
                    for k in range(4):
                        units(1)
                        b = c.next_tile()
                        act.activation(tmp[k % 2][:, :], bank[b][:, :], ACT.Relu).then_inc(relu_done, 1)
                        act.wait_ge(bank_free[b], c.at(f"used{b}"))
                        act.activation(mid[:, i * 4 + k, 0, :], prod[k % 2][:, :], ACT.Copy).then_inc(mid_hi, 1)

                for half in range(2):
                    up4(0)
                    with c.loop(3, split=4, unit_done=4, **TILES4) as i:
                        up4(i + 1)
                    with c.loop(4, split=4, unit_done=4, **TILES2):
                        for k in range(2):
                            units(2)
                            c.next_tile()
                layer_norm(V_LN + 32 * layer + 16, V_LN + 32 * layer + 24, layer == 0,
                           None if layer == 0 else lambda k: pre_chunk(V_RMS, k, affine))

            def ffn2(embed=False):
                def two(i):
                    for k in range(2):
                        units(1)
                        b = c.next_tile()
                        act.wait_ge(bank_free[b], c.at(f"used{b}"))
                        act.activation(tmp[k][:, :], tmp[k][:, :], ACT.Silu).then_inc(gate_made, 1)
                        units(1)
                        c.next_tile()
                        c.wait(pair_made)
                        act.activation(mid[:, i * 2 + k, 0, :], prod[k][:, :], ACT.Copy).then_inc(mid_hi, 1)

                two(0)
                with c.loop(FF2C // 2 - 1, split=4, unit_done=4, pair_made=2, **TILES4) as i:
                    two(i + 1)
                log_exp()
                if embed:
                    c.wait(p_in, 16)
                    for k in range(2):
                        act.activation(px[:, k, 0, :], pf[:, k, :], ACT.Copy).then_inc(p_hi, 1)
                    c.wait(p_ready, 2)
                with c.loop(2, split=12, unit_done=12, sqs=4, acc=4, **TILES4):
                    for k in range(4):
                        tile_square(3)

            for layer in range(DEPTH):
                g = V_RMS + 64 * layer
                if layer == 0:
                    c.wait(sq_used, DC)
                    rstd(bank[3][:, :], 1, rs_in)
                ffn2()
                rms_post()
                rms_pre(g + 16, h_ready)
                if layer == 0:
                    for pair in range(4):
                        for k in range(9):
                            units(1)
                            c.next_tile()
                        attend(jobs_a(), sca, pta, [outs_a(pair)])
                    for n in range(4):
                        units(1)
                        for j in range(2):
                            square_of(bank[n % 2 * 2 + j][:, :])
                else:
                    for c4 in range(2):
                        for k in range(6):
                            units(1)
                            c.next_tile()
                        attend(jobs_b(c4), scb, ptb, outs_b(c4))
                    with c.loop(2, split=4, unit_done=4, sqs=4, acc=4, **TILES4):
                        for k in range(4):
                            tile_square(1)
                rms_post()
                rms_pre(g + 32, h_ready)
                ffn2(True)
                units(1)
                rms_post()
                rms_pre(g + 48, h_ready, (0, 5))
                units(1)
                for k in range(DC):
                    units(1, last=layer == DEPTH - 1 and k == DC - 1)
                    b = c.next_tile()
                    act.wait_ge(bank_free[b], c.at(f"used{b}"))
                    act.activation(tmp[k % 2][:, :], tmp[k % 2][:, :], ACT.Sigmoid).then_inc(gate_made, 1)
                    if k == DC - 1:
                        log_exp()
                    c.wait(sig_done)
                    square_of(y[:, k, :])
                rms_post()
                if layer < DEPTH - 1:
                    rms_pre(g + 64, h_ready)

        @block.vector
        def _(dve):
            c = Count(dve)

            def split(last=False):
                if last:
                    return
                n = c.n.get("hi_done", 0)
                c.wait(hi_done)
                dve.tensor_tensor(wl[n % 2][:, :], raw[n % 4][:, :], wh[n % 2][:, :].bitcast(F32),
                                  ALU.subtract).then_inc(split_done, 1)

            def units(n, last=False):
                for k in range(n):
                    if c.n.get("early", 0):
                        c.n["early"] -= 1
                    else:
                        split(last and k == n - 1)
                c.wait(unit_done, n)

            def split_early():
                split()
                c.tick("early")

            def link(ins):
                ins.then_inc(dve_step, 1)
                c.wait(dve_step)

            def free(ins):
                ins.then_inc(bank_free[c.next_tile()], 1)

            def lo_of(dst, src, hi, done):
                dve.tensor_tensor(dst, src, hi.bitcast(F32), ALU.subtract).then_inc(done, 1)
                c.tick(f"made {done.name}")

            def layer_norm(g, to_x, after=None):
                c.wait(stat_done)
                for k in range(DC):
                    dve.tensor_tensor(h[:, k, :], h[:, k, :], bank[2][:, :], ALU.subtract).then_inc(centred, 1)
                c.wait(centred, DC)
                c.wait(rstd_ready)

                def scaled(k):
                    if k >= 2:
                        c.wait(affine)
                    dve.scalar_tensor_tensor(prod[k % 2][:, :], h[:, k, :], vec[:, g + k:g + k + 1], rs[:, :],
                                             ALU.mult, ALU.mult).then_inc(normed, 1)
                scaled(0)
                scaled(1)
                for k in range(DC):
                    if k + 2 < DC:
                        scaled(k + 2)
                    else:
                        c.wait(affine)
                    if to_x:
                        lo_of(x[:, k, 1, :], h[:, k, :], x[:, k, 0, :], x_ready)
                        if k == 3:
                            split_early()
                    elif after is not None:
                        after(k)

            def low_part(g, k, early=(4,)):
                c.wait(x_hi)
                dve.scalar_tensor_tensor(x[:, k, 1, :], h[:, k, :], vec[:, g + k:g + k + 1],
                                         x[:, k, 0, :].bitcast(F32), ALU.mult, ALU.subtract).then_inc(x_ready, 1)
                if k in early:
                    split_early()

            def residual(g, pre=None, meanwhile=None, early=(4,)):
                c.wait(rstd_ready)

                def part(k):
                    if k >= 2:
                        c.wait(h_ready)
                    dve.scalar_tensor_tensor(prod[k % 2][:, :], y[:, k, :], vec[:, g + k:g + k + 1], rs[:, :],
                                             ALU.mult, ALU.mult).then_inc(part_made, 1)
                part(0)
                part(1)
                if meanwhile is not None:
                    meanwhile()
                for k in range(DC):
                    if k + 2 < DC:
                        part(k + 2)
                    else:
                        c.wait(h_ready)
                    if pre is not None:
                        low_part(pre, k, early)
                if pre is not None:
                    c.wait(rstd_ready)

            def copy_tile(dst, n=1, last=False):
                units(n, last)
                free(dve.tensor_copy(dst, bank[c.n.get("tile", 0) % 2][:, :]))

            def scale_tile(dst):
                units(1)
                free(dve.tensor_tensor(dst, bank[c.n.get("tile", 0) % 2][:, :], rs_in[:, :], ALU.mult))

            def copy_tile_sq(dst, n):
                units(n)
                c.wait(sq_done)
                free(dve.tensor_copy(dst, bank[c.n.get("tile", 0) % 2][:, :]))

            def rope(ap, cos, sin, banks=(2, 3)):
                c.wait(rot_done)
                k = c.n.get("rope", 0)
                dve.tensor_tensor(tmp[k % 2][:, :], bank[banks[k % len(banks)]][:, :], sin, ALU.mult).then_inc(rope_used, 1)
                link(dve.tensor_tensor(ap, ap, cos, ALU.mult))
                dve.wait_ge(rope_used, k + 1)
                dve.tensor_tensor(ap, ap, tmp[k % 2][:, :], ALU.add).then_inc(rope_done, 1)
                c.tick("rope")

            def turned_into(dst, src, banks=(4, 5)):
                c.wait(turned)
                k = c.n.get("turn", 0)
                dve.tensor_copy(dst, src(bank[banks[k % len(banks)]])).then_inc(turn_read, 1)
                c.tick("turn")

            def attend(jobs, sc, pt, diag, outs, last_turns=None, later=None):
                jobs = list(jobs)

                def masks(j):
                    job = jobs[j]
                    n, t = c.n.get("job", 0) // 4 % 2, job["t"]
                    nsa = job["kind"] == "nsa"
                    for si, (seg, (off, w, _)) in enumerate(zip(job["segs"], spans(job))):
                        c.wait(scored)
                        dve.tensor_tensor_reduce(
                            out=sc[j % 3][:, off:off + w], in0=bank[2 + si][:, 0:w], in1=seg[1], scale=1.0,
                            scalar=-3.0e38, op0=ALU.add, op1=ALU.max,
                            accum_out=mx[:, n, t, si:si + 1]).then_inc(score_read, 1)
                        c.wait(score_read)
                    if nsa:
                        dve.tensor_scalar(negm[:, n, :, t], mx[:, n, t, 0:3], FLOOR, -0.125, ALU.max, ALU.mult).then_inc(max_ready, 1)
                    elif job["kind"] == "a":
                        dve.tensor_scalar(negm[:, n, 0, t:t + 1], mx[:, n, t, 0:1], mx[:, n, t, 1:2], -0.125,
                                          ALU.max, ALU.mult).then_inc(max_ready, 1)
                    else:
                        hd_ = job["head"]
                        dve.tensor_scalar(negm[:, n, 0, t:t + 1], mx[:, n, t, 0:1], -0.125, nsink[:, hd_:hd_ + 1],
                                          ALU.mult, ALU.min).then_inc(max_ready, 1)
                    c.tick("job")

                def group():
                    c.tick("blk_turned")
                    c.tick("blk")
                    return c.n["blk"] % 2 == 0 and jobs[0]["kind"] == "nsa"

                def copies(j):
                    for gi, grp in enumerate(blocks(jobs[j])):
                        if group():
                            dve.wait_ge(blk_turned, c.n["blk_turned"])
                            if c.n.get("copied", 0) >= 2:
                                dve.wait_ge(o_done, c.n["copied"] - 1)
                            copy_group(pt[j % 2], gi, grp, bank[6], blk_read[1])
                    c.tick("copied")
                    turned_by[j] = c.n["blk_turned"]

                def scales(j):
                    job = jobs[j]
                    n, t = c.n.get("scales", 0) // 4 % 2, job["t"]
                    c.wait(exp_done, 3 if job["kind"] == "nsa" else 1)
                    if j >= 2:
                        dve.wait_ge(blk_turned, turned_by[j - 2])
                    w = 3 if job["kind"] == "nsa" else 1
                    d, rd = den[:, n, 0:w, t], rden[:, n, 0:w, t]
                    if job["kind"] == "nsa":
                        link(dve.tensor_scalar(d, d, 1e-30, None, ALU.max))
                    if job["kind"] == "b":
                        c.wait(sink_exp)
                        link(dve.tensor_tensor(den[:, n, 0, t:t + 1], den[:, n, 0, t:t + 1], esink[:, n, t:t + 1], ALU.add))
                    link(dve.reciprocal(rd, d))
                    if job["kind"] == "nsa":
                        link(dve.tensor_tensor(rd, rd, gate_c[:, t, 3 * job["head"]:3 * job["head"] + 3], ALU.mult))
                        ins = dve.tensor_tensor(
                            diag[j % 2][:, :, :], ident[:, :].rearrange("p (o q) -> p o q", o=1).broadcast_to([P, 3, P]),
                            rden[:, n, :, t:t + 1].broadcast_to([P, 3, P]), ALU.mult)
                    else:
                        ins = dve.tensor_scalar(diag[j % 2][:, 0, :], ident[:, :], rden[:, n, 0, t:t + 1], None, ALU.mult)
                    ins.then_inc(diag_ready, 1)
                    c.tick("scales")

                def pair_out(k):
                    src = o_bank(jobs[0], c.n.get("pairs", 0))[:, :]
                    c.tick("pairs")
                    c.wait(ot_hi)
                    hi = outs[k][0].bitcast(F32)
                    dve.tensor_tensor(outs[k][1], in_order(outs[k], src), hi, ALU.subtract).then_inc(ot_ready, 1)

                turned_by = {}
                masks(0)
                masks(1)
                if last_turns is not None:
                    last_turns()
                scales(0)
                copies(0)
                n_jobs = len(jobs)
                for j in range(n_jobs):
                    if j + 1 < n_jobs:
                        scales(j + 1)
                    if j + 2 < n_jobs:
                        masks(j + 2)
                    if j + 1 < n_jobs:
                        copies(j + 1)
                    if later is not None and j == 2:
                        later()
                    if pair_done(j):
                        pair_out(j // 8 - 1)
                pair_out(n_jobs // 8 - 1)

            def copy_group(pt_, gi, grp, src, done):
                w0 = grp[0][3]
                first = 0 if w0 == P else P
                if len(grp) * P > first:
                    ins = dve.tensor_copy(pt_[:, gi * 512 + first:gi * 512 + len(grp) * P], src[:, first:len(grp) * P])
                if first:
                    ins = dve.tensor_copy(pt_[0:w0, 0:P], src[0:w0, 0:P])
                ins.then_inc(done, 1)

            def prepare(layer, k):
                if k == 3:
                    c.wait(z_done, 2)
                    c.wait(tab_in, 16)
                if k in (3, 4):
                    i, w = k - 3, (128, 64)[k - 3]
                    bg = V_BG + 2 * layer + i
                    c.wait(gk_act)
                    link(dve.tensor_scalar(tmp[i][0:w, :], bank[6 + i][0:w, :], vec[0:w, bg:bg + 1], 0.0, ALU.add, ALU.min))
                    link(dve.tensor_tensor(tmp[i][0:w, :], tmp[i][0:w, :], gt[0][0:w, i, :], ALU.subtract))
                    dve.tensor_tensor_scan(gt[0][0:w, i, :], tb1[0:w, T_RESET:T_RESET + S], tmp[i][0:w, :], 0.0,
                                           ALU.mult, ALU.add).then_inc(gk_done, 1)
                if k in (6, 7):
                    i, w, qc, kc = ((0, 128, GQ, GK), (1, 64, GQX, GKX))[k - 6]
                    c.wait(gla_exp, 2)
                    link(dve.scalar_tensor_tensor(proj[0:w, qc, :], proj[0:w, qc, :], 32.0 ** -0.5, gt[2][0:w, i, :], ALU.mult, ALU.mult))
                    link(dve.tensor_copy(prod[1][0:w, i * 8:i * 8 + 8], gt[2][0:w, i, 63::64]))
                    link(dve.tensor_tensor(gt[1][0:w, i, :], gt[1][0:w, i, :], proj[0:w, kc, :], ALU.mult))
                    b3 = gt[0][0:w, i, :].rearrange("p (n c) -> p n c", c=64)
                    link(dve.tensor_copy(prod[0][0:w, 0:8], gt[0][0:w, i, 63::64]))
                    last = prod[0][0:w, 0:8].rearrange("p (n o) -> p n o", o=1).broadcast_to([w, 8, 64])
                    dve.tensor_tensor(b3, last, b3, ALU.subtract).then_inc(gk_done, 1)
                if k in (8, 9):
                    i, w, kc = ((0, 128, GK), (1, 64, GKX))[k - 8]
                    c.wait(gla_exp)
                    ins = dve.tensor_tensor(proj[0:w, kc, :], proj[0:w, kc, :], gt[0][0:w, i, :], ALU.mult)
                    if i == 0:
                        link(ins)
                    else:
                        ins.then_inc(gla_kend, 1)
                if k == 12:
                    link(dve.memset(st_gla[:, 0, :, :], 0.0))
                    c.wait(ds_done)
                    for n in range(7):
                        for gi, w in enumerate((128, 64)):
                            ins = dve.scalar_tensor_tensor(
                                st_gla[0:w, n + 1, gi, :], st_gla[0:w, n, gi, :], prod[1][0:w, gi * 8 + n:gi * 8 + n + 1],
                                bank[(2, 3, 6, 7)[n % 2 * 2 + gi]][0:w, n // 2 * HD:n // 2 * HD + HD], ALU.mult, ALU.add)
                            if n < 6 or gi == 0:
                                link(ins)
                    ins.then_inc(st_done, 1)
                if 13 <= k < 17:
                    c.wait(am_done)
                    for hh in range(6):
                        ins = dve.scalar_tensor_tensor(
                            at_gla[:, k - 13, hh, :], bank[(2, 3, 6, 7)[hh % 4]][:, hh // 4 * P:hh // 4 * P + P], 3.0e38,
                            tb1[:, T_GLA:T_GLA + P], ALU.min, ALU.mult)
                    ins.then_inc(am_read, 1)
                z, u, t = (sq[1][:, i * 64:i * 64 + 64].rearrange("p (a n) -> p a n", a=2) for i in range(3))
                if k in (13, 15):
                    kind = (k - 13) // 2
                    if kind:
                        c.wait(cmp_mm)
                    src = proj[:, (KC, VC)[kind], :]
                    dve.tensor_copy(xp[:, :, 0:N_CMP], bass.AP(tensor=src.tensor, offset=src.offset,
                                                               ap=[list(src.ap[0]), [1, 32], [16, N_CMP]]))
                    pos = sm[:, SM_POS + 32 * kind:SM_POS + 32 * kind + 32]
                    dve.tensor_copy(xp[:, :, N_CMP:32].rearrange("p j o -> p (j o)"), pos).then_inc(cmp_in, 1)
                if k == 17:
                    c.wait(cmp_mm)
                    link(dve.tensor_copy(cmpb[:, :], bank[5][:, N_CMP:64:32]))
                    for kind in range(2):
                        ins = dve.tensor_scalar(z[:, kind, 0:N_CMP], bank[5][:, kind * 32:kind * 32 + N_CMP],
                                                cmpb[:, kind:kind + 1], None, ALU.add)
                    link(ins)
                    link(dve.tensor_tensor(t[:, :, 0:N_CMP], z[:, :, 0:N_CMP], z[:, :, 0:N_CMP], ALU.mult))
                    link(dve.tensor_scalar(t[:, :, 0:N_CMP], t[:, :, 0:N_CMP], 0.044715, 1.0, ALU.mult, ALU.add))
                    dve.tensor_tensor(u[:, :, 0:N_CMP], t[:, :, 0:N_CMP], z[:, :, 0:N_CMP], ALU.mult).then_inc(cmp_bias, 1)
                if k == 18:
                    c.wait(gate_exp)
                    link(dve.tensor_scalar(t[:, :, 0:N_CMP], hid[:, :, 0:N_CMP], 1.0, None, ALU.add))
                    link(dve.reciprocal(t[:, :, 0:N_CMP], t[:, :, 0:N_CMP]))
                    dve.tensor_tensor(hid[:, :, 0:N_CMP], t[:, :, 0:N_CMP], z[:, :, 0:N_CMP], ALU.mult).then_inc(cmp_hid, 1)
                if k >= 18:
                    cc = k - 18
                    c.wait(go_silu)
                    link(dve.tensor_tensor(prod[0][:, :], prod[0][:, :], proj[:, GO + cc, :], ALU.mult))
                    c.wait(rstd_ready)
                    ng = V_NG + 3 * layer + cc
                    link(dve.scalar_tensor_tensor(tmp[1][:, :], tmp[0][:, :], vec[:, ng:ng + 1], rs[:, :], ALU.mult, ALU.mult))
                    dve.tensor_tensor(proj[:, GO + cc, :], tmp[1][:, :], prod[0][:, :], ALU.mult).then_inc(go_out, 1)
                    c.wait(go_out)
                if 17 <= k < 20:
                    c.wait(go_done)
                    dve.tensor_copy(tmp[0][0:64, :], bank[2][0:64, :])
                    dve.tensor_copy(tmp[0][64:128, :], bank[3][64:128, :]).then_inc(go_copied, 1)
                if k in ROPED:
                    rope(proj[:, ROPED[k], :], tb1[:, T_COS:T_COS + S], tb1[:, T_SIN:T_SIN + S], (5,))
                if k in TURNED:
                    turned_chunk(TURNED[k])
                if k == 19:
                    c.wait(cmp_out)
                    dve.tensor_copy(kc_c[:, 0:N_CMP], bank[7][:, 0:N_CMP])
                    for g in range(2):
                        ins = dve.tensor_copy(vc_c[0:N_CMP, g * HD:g * HD + HD], bank[(7, 5)[g]][0:N_CMP, P:P + HD])
                    ins.then_inc(cmp_ready, 1)

            def turned_chunk(ch, banks=(4,)):
                three = lambda b: b[:, :].rearrange("p (t d) -> p t d", t=QT)
                kt_ = gt[2][:, :, :].rearrange("p a s -> p (a s)")[:, 0:QT * 192].rearrange("p (t d) -> p t d", t=QT)
                turned_into(*{
                    GK: (kt_[:, :, 0:128], three),
                    GKX: (kt_[:, :, 128:192], lambda b: b[:, 0:256].rearrange("p (t d) -> p t d", t=QT)),
                    VS: (vtok[:, :, 0, :], three), VW: (vtok[:, :, 1, :], three),
                    GQX: (gate_c[:, :, :], lambda b: three(b)[:, :, GATE_ROW:GATE_ROW + 18]),
                }.get(ch, (proj[:, ch, :], lambda b: b[:, :])), banks)

            split()
            for k in range(DC):
                c.wait(x_hi)
                lo_of(x[:, k, 1, :], h[:, k, :], x[:, k, 0, :], x_ready)
            c.wait(consts_in, 48)
            dve.tensor_scalar(nsink[:, :], vec[:, V_SINK:V_SINK + 16], -1.0, None, ALU.mult)
            for layer in range(DEPTH):
                for j in (1, 5):
                    g = V_RMS + 64 * layer + 8 * j
                    link(dve.tensor_scalar(vec[:, g:g + 8], vec[:, g:g + 8], 0.5, None, ALU.mult))

            for layer in range(DEPTH):
                for k in range(N_PROJ):
                    copy_tile(proj[:, ORDER[k], :])
                    prepare(layer, k)

                def mixed_lo():
                    for m, ch in enumerate((GO, GO + 1, GO + 2, PU, PU + 1)):
                        c.wait(mx_hi)
                        lo_of(x[:, 3 + m, 1, :], proj[:, ch, :], x[:, 3 + m, 0, :], x_ready)

                def last_turns():
                    turned_chunk(VW, (5,))
                    c.wait(pooled, 2)
                    c.wait(gate_exp)
                    link(dve.tensor_scalar(gate_c[:, :, :], gate_c[:, :, :], 1.0, None, ALU.add))
                    link(dve.reciprocal(gate_c[:, :, :], gate_c[:, :, :]))

                attend(jobs_nsa(), sc1, pt1, diag1, [(x[:, k, 0, :], x[:, k, 1, :], False) for k in range(3)],
                       last_turns, mixed_lo)
                with c.loop(2, hi_done=4, unit_done=4, **TILES4) as i:
                    for k in range(4):
                        units(1)
                        b = bank[c.n.get("tile", 0) % 2]
                        hm = h[:, i * 4 + k, :]
                        free(dve.scalar_tensor_tensor(hm, hm, ALPHA, b[:, :], ALU.mult, ALU.add))
                layer_norm(V_LN + 32 * layer, True)

                def up4(i):
                    for k in range(4):
                        units(1)
                        c.wait(relu_done)
                        b = bank[c.n.get("tile", 0) % 2]
                        free(dve.tensor_tensor(prod[k % 2][:, :], tmp[k % 2][:, :], b[:, :], ALU.mult))
                        c.wait(mid_hi)
                        lo_of(mid[:, i * 4 + k, 1, :], prod[k % 2][:, :], mid[:, i * 4 + k, 0, :], mid_ready)

                for half in range(2):
                    up4(0)
                    with c.loop(3, hi_done=4, unit_done=4, relu_done=4, mid_hi=4, **{"made mid_ready": 4}, **TILES4) as i:
                        up4(i + 1)
                    with c.loop(4, hi_done=4, unit_done=4, **TILES2) as i:
                        for k in range(2):
                            units(2)
                            b = bank[c.n.get("tile", 0) % 2]
                            hm = h[:, i * 2 + k, :]
                            free(dve.scalar_tensor_tensor(hm, hm, ALPHA if half == 0 else 1.0, b[:, :], ALU.mult, ALU.add))
                layer_norm(V_LN + 32 * layer + 16, layer == 0, lambda k: low_part(V_RMS, k))

            def ffn2(embed=False):
                def two(i):
                    for k in range(2):
                        scale_tile(tmp[k][:, :])
                        scale_tile(prod[k][:, :])
                        b = 1 - c.n["tile"] % 2
                        dve.wait_ge(bank_free[b], c.at(f"used{b}"))
                        c.wait(gate_made)
                        dve.tensor_tensor(prod[k][:, :], tmp[k][:, :], prod[k][:, :], ALU.mult).then_inc(pair_made, 1)
                        c.wait(mid_hi)
                        lo_of(mid[:, i * 2 + k, 1, :], prod[k][:, :], mid[:, i * 2 + k, 0, :], mid_ready)

                two(0)
                with c.loop(FF2C // 2 - 1, hi_done=4, unit_done=4, mid_hi=2, gate_made=2, **{"made mid_ready": 2}, **TILES4) as i:
                    two(i + 1)
                if embed:
                    for k in range(2):
                        c.wait(p_hi)
                        lo_of(px[:, k, 1, :], pf[:, k, :], px[:, k, 0, :], p_ready)
                with c.loop(2, hi_done=12, unit_done=12, sq_done=4, **TILES4) as i:
                    for k in range(4):
                        copy_tile_sq(y[:, i * 4 + k, :], 3)

            for layer in range(DEPTH):
                g = V_RMS + 64 * layer
                if layer == 0:
                    c.wait(rstd_ready)
                ffn2()
                residual(g + 8, g + 16)
                if layer == 0:
                    for pair in range(4):
                        for k in range(9):
                            units(1)
                            b = bank[c.n["tile"] % 2]
                            view = [t[:, :].rearrange("p (j c r) -> p r c j", c=4, r=4) for t in (b, rs_in)]
                            free(dve.tensor_tensor(aq[:, k, :].rearrange("p (r c j) -> p r c j", r=4, c=4),
                                                   *view, ALU.mult))
                            if pair == 0 and k == 1:
                                c.wait(tab_in, 16)
                            if 1 <= k < 7:
                                rope(aq[:, k - 1, :], tba[:, A_COS:A_COS + S], tba[:, A_SIN:A_SIN + S])
                            if k >= 7:
                                turned_into(av[:, :, k - 7, :], lambda b: b[:, :].rearrange("p (t d) -> p t d", t=QT))
                        attend(jobs_a(), sca, pta, diaga, [outs_a(pair)],
                               lambda: turned_into(av[:, :, 2, :], lambda b: b[:, :].rearrange("p (t d) -> p t d", t=QT)))
                    for n in range(4):
                        units(1)
                        for j in range(2):
                            c.wait(sq_done)
                            dve.tensor_copy(y[:, 2 * n + j, :], bank[n % 2 * 2 + j][:, :]).then_inc(emb_read, 1)
                else:
                    for c4 in range(2):
                        for k in range(6):
                            scale_tile(bk[:, k, :])
                            if c4 == 0 and k == 1:
                                c.wait(tab_in, 16)
                            if k in (1, 3, 4, 5):
                                rope(bk[:, k - 1, :], tbb[:, B_COS:B_COS + S], tbb[:, B_SIN:B_SIN + S])
                            if k == 2:
                                turned_into(bv[:, :, :], lambda b: b[:, :].rearrange("p (t d) -> p t d", t=QT))
                        rope(bk[:, 5, :], tbb[:, B_COS:B_COS + S], tbb[:, B_SIN:B_SIN + S])
                        attend(jobs_b(c4), scb, ptb, diagb, outs_b(c4))
                    with c.loop(2, hi_done=4, unit_done=4, sq_done=4, **TILES4) as i:
                        for k in range(4):
                            copy_tile_sq(y[:, i * 4 + k, :], 1)
                residual(g + 24, g + 32)
                ffn2(True)

                def emb_out(n):
                    for j in range(4):
                        dve.tensor_copy(emb[:, 4 * n + j, :], bank[4 + j][:, :]).then_inc(emb_read, 1)
                units(1)
                residual(g + 40, g + 48, lambda: emb_out(0), (0, 5))
                units(1)
                emb_out(1)
                for k in range(DC):
                    units(1, last=layer == DEPTH - 1 and k == DC - 1)
                    free(dve.tensor_tensor(tmp[k % 2][:, :], bank[c.n["tile"] % 2][:, :], rs_in[:, :], ALU.mult))
                    c.wait(gate_made)
                    dve.tensor_tensor(y[:, k, :], tmp[k % 2][:, :], emb[:, k, :], ALU.mult).then_inc(sig_done, 1)
                c.tick("sq_done", DC)
                residual(g + 56, g + 64 if layer < DEPTH - 1 else None)


def tables():
    f = np.float32
    pos = np.arange(S, dtype=f)
    inv = (f(500000.0) ** (-np.arange(8, dtype=f) * f(2.0) / f(16))).astype(f)
    ang = (pos[None, :] * inv[:, None]).astype(f)
    cos, sin = np.ones((P, S), f), np.zeros((P, S), f)
    rot = np.zeros((P, P), f)
    for r in (0, HD):
        for d in range(16):
            cos[r + d], sin[r + d] = np.cos(ang[d % 8]), np.sin(ang[d % 8])
        for d in range(8):
            rot[r + 8 + d, r + d], rot[r + d, r + 8 + d] = -1.0, 1.0
    p = np.arange(P)[:, None]

    def mask(width, first, ok):
        d = np.arange(width)[None, :] - first - p
        return np.where(ok(d), 0.0, BIG_NEG).astype(f)

    tok = np.arange(S)
    icnt = np.concatenate([np.repeat(np.stack([1.0 / np.minimum(tok + 1, w) for w in ws]), HD, 0)
                           for ws in ((2, 4), (8, 16))], 1).astype(f)
    reset = np.broadcast_to((tok % 64 != 0).astype(f), (P, S))
    t_, n_ = np.arange(QT)[None, :, None], np.arange(32)[None, None, :]
    cmp_ = np.where(16 * n_ + 31 <= t_ * P + p[:, :, None], 0.0, BIG_NEG).astype(f).reshape(P, QT * 32)
    i = np.arange(P)[None, :]
    gla = ((p <= i) & (p // 64 == i // 64)).astype(f)
    b64 = (p // HD == i // HD).astype(f) / HD
    t1 = np.concatenate([cos, sin, icnt, reset, mask(4 * P, 3 * P, lambda d: d <= 0), cmp_, gla, b64, rot], 1)
    order = tok.reshape(32, 4, 4).transpose(2, 1, 0).reshape(-1)
    d = order[None, :] - order[:, None]
    no = lambda ok: np.where(ok, 0.0, BIG_NEG).astype(f)
    near = no(abs(d) <= 64).reshape(QT, P, S).transpose(1, 0, 2).reshape(P, QT * S)
    own = d[:P, :P]
    ta = np.concatenate([cos[:, order], sin[:, order], rot, near, no((own % 4 == 0) & (abs(own) <= 256)),
                         no(own % 16 == 0)], 1)
    tb = np.concatenate([cos, sin, rot, mask(3 * P, P, lambda d: abs(d) <= 128)], 1)
    assert t1.shape[1] == T_N and ta.shape[1] == A_N and tb.shape[1] == B_N
    cs = np.stack([np.eye(P, dtype=f), np.full((P, P), 1.0 / D, f)])
    return [np.ascontiguousarray(a, dtype=f) for a in (t1, ta, tb, cs)]


def tiles(w):
    k, m = w.shape
    return w.reshape(k // P, P, m // P, P).transpose(2, 1, 0, 3).reshape(m // P, P, k)


def cut(t, n):
    return t.reshape(t.shape[0], P, n, UNIT).transpose(0, 2, 1, 3).reshape(-1, P, UNIT)


def weight_stream(a):
    units = []
    z = np.zeros
    for l in range(DEPTH):
        w = a["w_in"][l]
        cols = []
        for c in range(3):
            cols += [w[:, c * HD:c * HD + HD], w[:, (3 + c) * HD:(4 + c) * HD]]
        kv = [w[:, 384 + i * P:384 + i * P + P] for i in range(6)]
        cols += [kv[0], kv[1], kv[2], kv[4], kv[3], kv[5]]
        gate, gq, gk, gv, glr, go, pu = (w[:, i:j] for i, j in (
            (1152, 1170), (1170, 1362), (1362, 1554), (1554, 1938), (1938, 1954), (1954, 2338), (2338, 2594)))
        cols += [gv, gq, glr, z((D, 16), w.dtype), gate, z((D, 14), w.dtype), gk, z((D, 64), w.dtype), go, pu]
        units.append(tiles(np.concatenate(cols, 1))[list(ORDER)])
        wo = a["w_out"][l]
        rows = []
        for c in range(3):
            rows += [wo[c * HD:c * HD + HD], wo[(3 + c) * HD:(4 + c) * HD]]
        units.append(tiles(np.concatenate(rows + [wo[384:]], 0)))
        for half in range(2):
            units.append(tiles(a["w_up"][l][:, half * 2048:half * 2048 + 2048]))
            units.append(cut(tiles(a["w_down"][l][half * 2048:half * 2048 + 2048]), 2))
    for l in range(DEPTH):
        def ffn(i):
            wi = tiles(a["ffn_wi_2"][l, i])
            pairs = np.stack([wi[:FF2C], wi[FF2C:]], 1).reshape(-1, P, UNIT)
            wo = np.concatenate([a["ffn_wo_2"][l, i], z((2 * P, D), wi.dtype)], 0)
            return [pairs, cut(tiles(wo), 3)]
        units += ffn(0)
        if l == 0:
            w = a["a_wqkv_2"][0].reshape(D, 3, 3, 4, P)
            for pair in range(4):
                units.append(tiles(w[:, :, :, pair].reshape(D, 9 * P)))
            units.append(tiles(a["a_wo_2"][0]).reshape(4, 2, P, 512).transpose(0, 2, 1, 3).reshape(4, P, UNIT))
        else:
            w, wo = a["b_wqkv_2"][0], a["b_wo_2"][0]
            rows = []
            for c4 in range(2):
                cols = [w[:, 1024 + c4 * P:1024 + c4 * P + P], w[:, 1280 + c4 * P:1280 + c4 * P + P]]
                for c in range(4):
                    for hd in (8 * c4 + c, 8 * c4 + 4 + c):
                        cols.append(w[:, hd * HD:hd * HD + HD])
                        rows.append(wo[hd * HD:hd * HD + HD])
                units.append(tiles(np.concatenate(cols, 1)))
            units.append(tiles(np.concatenate(rows, 0)))
        units += ffn(1)
        units.append(tiles(a["ple_proj_2"][l]).reshape(2, 4, P, 256).transpose(0, 2, 1, 3).reshape(2, P, UNIT))
        units.append(tiles(a["ple_gate_2"][l]))
    return np.concatenate(units, 0)


def small_weights(a):
    out = []
    for l in range(DEPTH):
        blk = np.zeros((P, SM_W), a["cmp_w1"].dtype)
        for r in (0, HD):
            for kind in range(2):
                w1 = a["cmp_w1"][l, kind].reshape(32, HD, HD).transpose(1, 0, 2).reshape(HD, 2048)
                blk[r:r + HD, SM_W1 + kind * 2048:SM_W1 + kind * 2048 + 2048] = w1
                blk[r:r + HD, SM_POS + kind * 32:SM_POS + kind * 32 + 32] = a["cmp_pos"][l, kind].T
                blk[r:r + HD, SM_W2 + kind * HD:SM_W2 + kind * HD + HD] = a["cmp_w2"][l, kind]
        blk[GLR_ROW:GLR_ROW + 16, SM_G2:SM_G2 + 192] = a["gla_w_gate2"][l]
        for g in range(4):
            blk[g % 2 * HD:g % 2 * HD + HD, SM_PW + g // 2 * HD:SM_PW + g // 2 * HD + HD] = a["pool_w"][l, g]
        out.append(blk)
    return np.stack(out)


def vectors(a):
    v = np.zeros((P, V_N), a["ln1_g"].dtype)

    def put(col, x):
        n = -(-x.size // P)
        for i in range(n):
            part = x[i * P:(i + 1) * P]
            v[:part.size, col + i] = part

    for l in range(DEPTH):
        for j, name in enumerate(("ln1_g", "ln1_b", "ln2_g", "ln2_b")):
            put(V_LN + 32 * l + 8 * j, a[name][l])
        for j in range(8):
            put(V_RMS + 64 * l + 8 * j, a["norm_g_2"][l, j])
        put(V_BG + 2 * l, a["gla_b_gate"][l])
        put(V_NG + 3 * l, a["gla_norm_g"][l])
        put(V_PS + 2 * l, a["pool_scale"][l])
    v[:, V_SINK:V_SINK + 16] = a["b_sink_2"][0][None, :]
    return v


def kernel(**inputs):
    import concourse.bacc as _bacc
    from concourse.bass_utils import run_bass_kernel_spmd as _run

    a = {k: np.asarray(v) for k, v in inputs.items()}
    t1, ta, tb, cs = tables()
    arrays = {
        "stream": weight_stream(a),
        "x_t": np.ascontiguousarray(a["x"][0].T),
        "p_t": np.ascontiguousarray(a["p_2"][:, 0].transpose(0, 2, 1)),
        "small": small_weights(a),
        "vecs": vectors(a),
        "tab1": t1, "tab_a": ta, "tab_b": tb, "consts": cs,
    }
    nc = _bacc.Bacc("TRN2", target_bir_lowering=False, num_devices=1)
    args = [nc.dram_tensor(n, v.shape, F32, kind="ExternalInput").ap() for n, v in arrays.items()]
    out = nc.dram_tensor("out_t", (DC, P, S), F32, kind="ExternalOutput").ap()
    build(nc, *args, out)
    r = _run(nc, [arrays], core_ids=[0])
    return np.ascontiguousarray(r.results[0]["out_t"].reshape(D, S).T).reshape(1, S, D)
```
